# Optimizing a Trainium2 kernel written in Bass

```python
import math
import jax, jax.numpy as jnp
from jax import lax
import numpy as np

D_MODEL = 1024
BATCH = 1
SEQ = 1024
DEPTH = 1

CHUNK = 64
Q_BLOCK = 128
D_MIX = D_MODEL
LRU_WIDTH = D_MIX // 2
LRU_BLOCKS = 8
LRU_BLOCK_W = LRU_WIDTH // LRU_BLOCKS
CONV_W = 4
LRU_C = 8.0
ATT_WIDTH = D_MIX - LRU_WIDTH
N_HEADS = 4
HEAD_DIM = ATT_WIDTH // (2 * N_HEADS)
V_DIM = 2 * HEAD_DIM
IN_COLS = 2 * LRU_WIDTH + 3 * ATT_WIDTH
N_GROUPS = 4
EXPERTS_PER_GROUP = 4
N_EXPERTS = N_GROUPS * EXPERTS_PER_GROUP
TOP_K_IN_GROUP = 2
D_EXPERT = D_MODEL // 2
EPS = 1e-6
NEG_BIG = -1e30

kernel_name = "hybrid_rglru_diffattn_hiermoe"

def rms_norm(x, g):
    xf = x.astype(jnp.float32)
    y = xf * lax.rsqrt(jnp.mean(xf * xf, axis=-1, keepdims=True) + EPS)
    return (y * g.astype(jnp.float32)).astype(x.dtype)

def alibi_slopes(n_heads):
    return jnp.exp2(-8.0 * jnp.arange(1, n_heads + 1, dtype=jnp.float32) / n_heads)

def causal_depthwise_conv(x, w, b):
    S = x.shape[1]
    xp = jnp.pad(x, ((0, 0), (CONV_W - 1, 0), (0, 0)))
    y = b
    for j in range(CONV_W):
        y = y + xp[:, j:j + S] * w[j]
    return y

def rg_lru(xc, w_a, b_a, w_x, b_x, lam):
    B, S, _ = xc.shape
    f32 = jnp.float32
    xf = xc.astype(f32)
    xb = xf.reshape(B, S, LRU_BLOCKS, LRU_BLOCK_W)
    r = jax.nn.sigmoid(jnp.einsum('bsnc,ncd->bsnd', xb, w_a.astype(f32)).reshape(B, S, LRU_WIDTH) + b_a.astype(f32))
    i = jax.nn.sigmoid(jnp.einsum('bsnc,ncd->bsnd', xb, w_x.astype(f32)).reshape(B, S, LRU_WIDTH) + b_x.astype(f32))
    log_a = -LRU_C * r * jax.nn.softplus(-lam.astype(f32))
    a = jnp.exp(log_a)
    u = jnp.sqrt(-jnp.expm1(2.0 * log_a)) * (i * xf)

    def combine(left, right):
        a1, b1 = left
        a2, b2 = right
        return a1 * a2, a2 * b1 + b2

    _, h = lax.associative_scan(combine, (a, u), axis=1)
    return h.astype(xc.dtype)

def diff_attention(q, k, v, lam, slopes):
    S = q.shape[1]
    f32 = jnp.float32
    scale = HEAD_DIM ** -0.5
    outs = []
    for blk in range(S // Q_BLOCK):
        q0 = blk * Q_BLOCK
        q1 = q0 + Q_BLOCK
        qb = q[:, q0:q1].astype(f32)
        kb = k[:, :q1].astype(f32)
        vb = v[:, :q1].astype(f32)
        s = jnp.einsum('bqhcd,bkhcd->bhcqk', qb, kb) * scale
        tq = jnp.arange(q0, q1)
        tk = jnp.arange(q1)
        dist = jnp.abs(tq[:, None] - tk[None, :]).astype(f32)
        allowed = (tk[None, :] // CHUNK) <= (tq[:, None] // CHUNK)
        bias = jnp.where(allowed[None], -slopes[:, None, None] * dist[None], NEG_BIG)
        p = jax.nn.softmax(s + bias[None, :, None], axis=-1)
        w = p[:, :, 0] - lam * p[:, :, 1]
        outs.append(jnp.einsum('bhqk,bkhe->bqhe', w, vb))
    return jnp.concatenate(outs, axis=1)

def hier_moe(xt, w_rg, b_rg, w_re, b_re, w_g, w_u, w_d):
    f32 = jnp.float32
    xf = xt.astype(f32)
    p_group = jax.nn.softmax(xf @ w_rg.astype(f32) + b_rg.astype(f32), axis=-1)
    g_gate, g_idx = lax.top_k(p_group, 1)
    e_logits = jnp.einsum('td,gde->tge', xf, w_re.astype(f32)) + b_re.astype(f32)
    sel = jnp.take_along_axis(e_logits, g_idx[:, :, None], axis=1)[:, 0]
    p_exp = jax.nn.softmax(sel, axis=-1)
    e_w, e_idx = lax.top_k(p_exp, TOP_K_IN_GROUP)
    e_w = e_w / jnp.sum(e_w, axis=-1, keepdims=True)
    gates = g_gate * e_w
    expert_id = g_idx * EXPERTS_PER_GROUP + e_idx
    dense_gates = jnp.einsum('tk,tke->te', gates, jax.nn.one_hot(expert_id, N_EXPERTS, dtype=f32))
    y = jnp.zeros_like(xf)
    for e in range(N_EXPERTS):
        hid = jax.nn.silu(xt @ w_g[e]) * (xt @ w_u[e])
        y = y + dense_gates[:, e:e + 1] * (hid @ w_d[e]).astype(f32)
    return y.astype(xt.dtype)

def setup_inputs(seed: int = 0) -> dict:
    key = jax.random.key(seed)
    ks = jax.random.split(key, 32)
    f32 = jnp.float32
    L = DEPTH

    def nrm(k, shape, std):
        return std * jax.random.normal(k, shape, f32)

    u = jax.random.uniform(ks[9], (L, LRU_WIDTH), f32, 0.9, 0.999)
    sig = u ** (1.0 / LRU_C)
    lru_lambda = jnp.log(sig) - jnp.log1p(-sig)
    return {
        'x': nrm(ks[0], (BATCH, SEQ, D_MODEL), 1.0),
        'norm1_g': 1.0 + nrm(ks[1], (L, D_MODEL), 0.02),
        'w_in': nrm(ks[2], (L, D_MODEL, IN_COLS), D_MODEL ** -0.5),
        'conv_w': nrm(ks[3], (L, CONV_W, LRU_WIDTH), CONV_W ** -0.5),
        'conv_b': nrm(ks[4], (L, LRU_WIDTH), 0.01),
        'w_gate_a': nrm(ks[5], (L, LRU_BLOCKS, LRU_BLOCK_W, LRU_BLOCK_W), LRU_BLOCK_W ** -0.5),
        'b_gate_a': nrm(ks[6], (L, LRU_WIDTH), 0.01),
        'w_gate_x': nrm(ks[7], (L, LRU_BLOCKS, LRU_BLOCK_W, LRU_BLOCK_W), LRU_BLOCK_W ** -0.5),
        'b_gate_x': nrm(ks[8], (L, LRU_WIDTH), 0.01),
        'lru_lambda': lru_lambda,
        'lru_out_g': 1.0 + nrm(ks[10], (L, LRU_WIDTH), 0.02),
        'q_norm_g': 1.0 + nrm(ks[11], (L, HEAD_DIM), 0.02),
        'k_norm_g': 1.0 + nrm(ks[12], (L, HEAD_DIM), 0.02),
        'lambda_q1': nrm(ks[13], (L, HEAD_DIM), 0.1),
        'lambda_k1': nrm(ks[14], (L, HEAD_DIM), 0.1),
        'lambda_q2': nrm(ks[15], (L, HEAD_DIM), 0.1),
        'lambda_k2': nrm(ks[16], (L, HEAD_DIM), 0.1),
        'sub_norm_g': 1.0 + nrm(ks[17], (L, V_DIM), 0.02),
        'w_out': nrm(ks[18], (L, D_MIX, D_MODEL), D_MIX ** -0.5),
        'norm2_g': 1.0 + nrm(ks[19], (L, D_MODEL), 0.02),
        'w_router_group': nrm(ks[20], (L, D_MODEL, N_GROUPS), D_MODEL ** -0.5),
        'b_router_group': nrm(ks[21], (L, N_GROUPS), 0.01),
        'w_router_expert': nrm(ks[22], (L, N_GROUPS, D_MODEL, EXPERTS_PER_GROUP), D_MODEL ** -0.5),
        'b_router_expert': nrm(ks[23], (L, N_GROUPS, EXPERTS_PER_GROUP), 0.01),
        'w_expert_gate': nrm(ks[24], (L, N_EXPERTS, D_MODEL, D_EXPERT), D_MODEL ** -0.5),
        'w_expert_up': nrm(ks[25], (L, N_EXPERTS, D_MODEL, D_EXPERT), D_MODEL ** -0.5),
        'w_expert_down': nrm(ks[26], (L, N_EXPERTS, D_EXPERT, D_MODEL), D_EXPERT ** -0.5),
    }

def reference(x, norm1_g, w_in, conv_w, conv_b, w_gate_a, b_gate_a, w_gate_x, b_gate_x,
              lru_lambda, lru_out_g, q_norm_g, k_norm_g, lambda_q1, lambda_k1, lambda_q2,
              lambda_k2, sub_norm_g, w_out, norm2_g, w_router_group, b_router_group,
              w_router_expert, b_router_expert, w_expert_gate, w_expert_up, w_expert_down):
    B, S, D = x.shape
    f32 = jnp.float32
    slopes = alibi_slopes(N_HEADS)
    splits = [LRU_WIDTH, 2 * LRU_WIDTH, 2 * LRU_WIDTH + ATT_WIDTH, 2 * LRU_WIDTH + 2 * ATT_WIDTH]
    h = x
    for l in range(DEPTH):
        lambda_init = 0.8 - 0.6 * math.exp(-0.3 * l)
        hn = rms_norm(h, norm1_g[l])
        proj = hn @ w_in[l]
        x_lru, g_lru, q, k, v = jnp.split(proj, splits, axis=-1)
        xc = causal_depthwise_conv(x_lru, conv_w[l], conv_b[l])
        y_lru = rg_lru(xc, w_gate_a[l], b_gate_a[l], w_gate_x[l], b_gate_x[l], lru_lambda[l]) * jax.nn.gelu(g_lru)
        y_lru = rms_norm(y_lru, lru_out_g[l])
        q = rms_norm(q.reshape(B, S, N_HEADS, 2, HEAD_DIM), q_norm_g[l])
        k = rms_norm(k.reshape(B, S, N_HEADS, 2, HEAD_DIM), k_norm_g[l])
        v = v.reshape(B, S, N_HEADS, V_DIM)
        lam = (jnp.exp(jnp.sum(lambda_q1[l].astype(f32) * lambda_k1[l].astype(f32)))
               - jnp.exp(jnp.sum(lambda_q2[l].astype(f32) * lambda_k2[l].astype(f32)))
               + lambda_init)
        o = diff_attention(q, k, v, lam, slopes)
        o = rms_norm(o, sub_norm_g[l]) * (1.0 - lambda_init)
        y_att = o.reshape(B, S, ATT_WIDTH).astype(h.dtype)
        h = h + jnp.concatenate([y_lru.astype(h.dtype), y_att], axis=-1) @ w_out[l]
        hn2 = rms_norm(h, norm2_g[l]).reshape(B * S, D)
        h = h + hier_moe(hn2, w_router_group[l], b_router_group[l], w_router_expert[l],
                         b_router_expert[l], w_expert_gate[l], w_expert_up[l],
                         w_expert_down[l]).reshape(B, S, D)
    return h


_drawn_inputs = setup_inputs


def setup_inputs(seed=0):
    import zlib

    import numpy as np

    out = dict(_drawn_inputs(seed))
    spreads = {}
    factors = {'b_gate_a': 8.0,
     'b_gate_x': 8.0,
     'q_norm_g': 3.499,
     'k_norm_g': 3.623,
     'sub_norm_g': 3.729,
     'norm2_g': 2.805,
     'b_router_group': 23.797,
     'b_router_expert': 8.0}
    for name, (base, spread) in spreads.items():
        noise = np.random.default_rng([zlib.crc32(name.encode()), seed]).standard_normal(out[name].shape)
        drawn = base * np.exp(spread * noise) if base else spread * noise
        out[name] = __import__('jax').numpy.asarray(drawn.astype(out[name].dtype))
    for name, factor in factors.items():
        out[name] = (out[name] * factor).astype(out[name].dtype)
    return out
```

```python
import math
from contextlib import ExitStack

import concourse.bass as bass
from concourse import mybir

F32 = mybir.dt.float32
U32 = mybir.dt.uint32
I32 = mybir.dt.int32
ALU = mybir.AluOpType
ACT = mybir.ActivationFunctionType
AX = mybir.AxisListType

P = 128
EPS = 1e-6
NEG_BIG = -1e30
LAMBDA_INIT = 0.8 - 0.6 * math.exp(-0.3 * 0)
LRU_C = 8.0
CHUNK = 64


def build_block(nc, x, norm1_g, w_in, conv_w, conv_b, w_gate_a, b_gate_a, w_gate_x, b_gate_x,
                lru_lambda, lru_out_g, q_norm_g, k_norm_g, lambda_q1, lambda_k1, lambda_q2, lambda_k2,
                sub_norm_g, w_out, norm2_g, w_router_group, b_router_group, w_router_expert,
                b_router_expert, w_expert_gate, w_expert_up, w_expert_down, out, hn2_dram):
    T, D = x.shape[1], x.shape[2]
    NB = T // P
    KD = D // P
    NG, EPG = b_router_expert.shape[1], b_router_expert.shape[2]
    NE = NG * EPG
    DE = w_expert_gate.shape[3]
    KE = DE // P
    HALF = 512
    NM = 4
    HD = q_norm_g.shape[1]
    NR = NG + NG * EPG
    MAX_TILES = NE + (2 * T - NE) // P
    LIST = MAX_TILES + 1
    RING = 8
    assert D == 1024 and T == 1024 and NM * P == 512 and DE == HALF and LIST <= 32

    BASE = 16512
    used = {}

    def at(name, word, shape, dt=F32):
        n = 1
        for s in shape[1:]:
            n *= s
        used[name] = (word, word + n)
        assert BASE + 4 * (word + n) <= nc.sbuf_usable_end, name
        return nc.alloc_sbuf_tensor_at(name, shape, dt, offset=BASE + 4 * word)

    A0 = 0
    A1 = A0 + 2 * KD * T
    A2 = A1 + 4112 + 8192
    A3 = A2 + 5 * 4096
    A4 = A3 + 2048
    hnT = at("hnT", A0, [P, KD, T])
    ring = at("ring", A0 + 8192, [P, RING, KD, P])
    XW = 3 + T
    xlp = at("xlp", A1, [P, NM, XW])
    a2 = at("a2", A1, [P, NM, T])
    v = at("v", A1, [P, NB, 512])
    q = at("q", A1 + 4112, [P, NM, T])
    k = at("k", A1 + 4112 + 4096, [P, NM, T])
    xc = at("xc", A2, [P, NM, T])
    gg = at("gg", A2 + 4096, [P, NM, T])
    r = at("r", A2 + 8192, [P, NM, T])
    ig = at("ig", A2 + 12288, [P, NM, T])
    th = at("th", A2 + 16384, [P, NM, T])
    xs = at("xs", A2 + 16384, [P, 2, D])
    g1b = at("g1b", A2 + 18432, [P, D])
    sq = at("sq", A3, [P, 2, HALF])
    rt = at("rt", A3 + 1024, [P, 2, HALF])
    junk = at("junk", A3, [P, D])
    qz = at("qz", A0, [P, 2, 2, T])
    pr = at("pr", A0 + 4096, [P, 3, 2, T])
    wT = at("wT", A0 + 10240, [P, 2, T])
    nd = at("nd", A0 + 12288, [P, T])
    osb = at("osb", A0 + 13312, [P, 2, NB, P])
    ndt = at("ndt", A0 + 13312, [P, T])
    osq = at("osq", A0 + 15360, [P, NB, P])
    yatt = at("yatt", A2, [P, NM, T])
    wout = at("wout", A2 + 8192, [P, KD, D])
    xr = at("xr", A2 + 16384, [P, 2, D])
    g2b = at("g2b", A2 + 18432, [P, D])
    h = at("h", A0, [P, 2, D])
    hn2 = at("hn2", A0 + 2048, [P, 2, D])
    hn2T = at("hn2T", A0 + 4096, [P, 2, KD, P])
    rc = [A0 + 12800]

    def route(name, shape, dt=F32):
        n = 1
        for s in shape[1:]:
            n *= s
        t = at(name, rc[0], shape, dt)
        rc[0] += (n + 7) // 8 * 8
        assert rc[0] <= A1
        return t

    upper = route("upper", [P, P])
    iota_row = route("iota_row", [P, P])
    tok1 = route("tok1", [P, NB])
    pad1 = route("pad1", [P, 32])
    ohg, gexp = route("ohg", [P, NB, NG]), route("gexp", [P, NB, NG])
    sel, stmp = route("sel", [P, NB, EPG]), route("stmp", [P, NB, EPG])
    oh1, oh2 = route("oh1", [P, NB, EPG]), route("oh2", [P, NB, EPG])
    gtop, etop1, etop2, free = (route(f"top{j}", [P, NB]) for j in range(4))
    edif, esum, gsum = (route(f"e{j}", [P, NB]) for j in range(3))
    mm = route("mm", [P, 2, NB, NE])
    msum, mcum = route("msum", [P, NB, NE]), route("mcum", [P, NB, NE])
    mtot = route("mtot", [P, NE])
    gates = route("gates", [P, 2, NB])
    cnt, ntile, texcl = route("cnt", [P, NE]), route("ntile", [P, NE]), route("texcl", [P, NE])
    tincl = route("tincl", [P, NE + 1])
    slotm, stmp2 = route("slotm", [P, NB, NE]), route("stmp2", [P, NB, NE])
    slot, srow, scol = (route(f"slot{j}", [P, 2, NB]) for j in range(3))
    slot_i, srow_i, scol_i = (route(f"sloti{j}", [P, 2, NB], I32) for j in range(3))
    lrow = route("lrow", [P, 2, P])
    lval = route("lval", [P, 2, 2, 32])
    tcmp = route("tcmp", [P, 32, NE])
    texp = route("texp", [P, 32])
    lemp = route("lemp", [P, 32])
    wg = at("wg", A1, [P, KD, DE])
    wu = at("wu", A1 + 4096, [P, KD, DE])
    wd = at("wd", A1 + 8192, [P, KE, D])
    xg = at("xg", A0 + 8192, [P, D])
    xT = at("xT", A0 + 9216, [P, KD, P])
    sil = at("sil", A0 + 10240, [P, DE])
    hid = at("hid", A0 + 10752, [P, DE])
    hT = at("hT", A0 + 11264, [P, KE, P])
    ysb = at("ysb", A0 + 11776, [P, D])
    c = [A4]

    def const(name, shape, dt=F32):
        n = 1
        for s in shape[1:]:
            n *= s
        t = at(name, c[0], shape, dt)
        c[0] += (n + 7) // 8 * 8
        return t

    ident = const("ident", [P, P])
    ones_blk = const("ones_blk", [P, P])
    ones = const("ones", [P, P])
    bd = at("bd", A1 + 4112 + 4096, [P, 2, NM, P])
    vrow = at("vrow", A3, [P, P])
    NV = 39
    vc = const("vc", [P, 40])
    CW, CB, BA, BX, LAM, LG, QG, KG, SG = 0, 16, 20, 24, 28, 32, 36, 37, 38
    wr = at("wr", A2 + 19456, [P, KD, NR])
    br = const("br", [P, NR])
    eps = const("eps", [P, 1])
    ss = const("ss", [P, NB])
    rs = const("rs", [P, NB])
    sp = const("sp", [P, 8, NM])
    qgh = const("qgh", [P, NM])
    lamv = at("lamv", A3 + 128, [P, 4, HD])
    lams = const("lams", [P, 8])
    mx = const("mx", [P, NB * NM, 2])
    nb = const("nb", [P, NB * NM, 2])
    sm = const("sm", [P, NB * NM, 2])
    ri = const("ri", [P, NB * NM, 2])
    ra = const("ra", [P, NB * NM])
    oss = const("oss", [P, 2, NB])
    phalf = const("phalf", [P, NB])
    lg = const("lg", [P, NB, NR])
    ltok = const("ltok", [P, 32])
    lgate = const("lgate", [P, 32])
    tiles_i = const("tiles_i", [P, NE + 1], I32)
    texp_i = const("texp_i", [P, 32], I32)
    idx_g = const("idx_g", [P, 2], U32)
    idx_s = const("idx_s", [P, 2], U32)
    gcol = const("gcol", [P, 2])

    ps = nc.alloc_psum_tensor("ps", [P, 8, HALF], F32)
    xT_ps = ps[:, 2:4, :].rearrange("p a n -> p (a n)")
    y_ps = ps[:, 4:6, :].rearrange("p a n -> p (a n)")

    with ExitStack() as ctx:
        def sem(name):
            return ctx.enter_context(nc.semaphore(name))

        consts_built = sem("consts_built")
        vec_landed = sem("vec_landed")
        bd_landed = sem("bd_landed")
        bcast_landed = sem("bcast_landed")
        br_landed = sem("br_landed")
        g1_landed = sem("g1_landed")
        x_landed = [sem(f"x_landed{i}") for i in range(2)]
        w_landed = [sem(f"w_landed{i}") for i in range(RING)]
        x_rms = sem("x_rms")
        hn_ready = sem("hn_ready")
        hn_transposed = sem("hn_transposed")
        hnT_act = sem("hnT_act")
        hnT_dve = sem("hnT_dve")
        act_seq = sem("act_seq")
        dve_seq = sem("dve_seq")
        pool_seq = sem("pool_seq")
        vec_transposed = sem("vec_transposed")
        vec_ready = sem("vec_ready")
        lam_y = sem("lam_y")
        sp_ready = sem("sp_ready")
        lam_dots = sem("lam_dots")
        lam_exp = sem("lam_exp")
        group_done = sem("group_done")
        lru_evac = sem("lru_evac")
        conv_done = sem("conv_done")
        gate_mm = sem("gate_mm")
        gate_sig = sem("gate_sig")
        lru_exp = sem("lru_exp")
        om_ready = sem("om_ready")
        om_sqrt = sem("om_sqrt")
        y_lru = sem("y_lru")
        y_sq = sem("y_sq")
        y_norm_mm = sem("y_norm_mm")
        y_rms = sem("y_rms")
        lru_ready = sem("lru_ready")
        qk_sq = sem("qk_sq")
        qk_mm = sem("qk_mm")
        qk_rms = sem("qk_rms")
        qk_done = sem("qk_done")
        v_evac = sem("v_evac")
        qz_ready = sem("qz_ready")
        nd_ready = sem("nd_ready")
        s_done = sem("s_done")
        s_biased = sem("s_biased")
        s_nmax = sem("s_nmax")
        p_ready = sem("p_ready")
        w_ready = sem("w_ready")
        t_done = sem("t_done")
        t_evac = sem("t_evac")
        pv_done = sem("pv_done")
        o_evac = sem("o_evac")
        o_ms = sem("o_ms")
        o_pow = sem("o_pow")
        o_normed = sem("o_normed")
        wout_landed = sem("wout_landed")
        xr_landed = [sem(f"xr_landed{i}") for i in range(2)]
        op_done = sem("op_done")
        h_ready = sem("h_ready")
        h_rms = sem("h_rms")
        hn2_ready = sem("hn2_ready")
        h_stored = [sem(f"h_stored{i}") for i in range(2)]
        hn2_stored = [sem(f"hn2_stored{i}") for i in range(2)]
        pad_ready = sem("pad_ready")
        pad_stored = sem("pad_stored")
        xt2_done = sem("xt2_done")
        xt2_evac = sem("xt2_evac")
        r_done = sem("r_done")
        logits_ready = sem("logits_ready")
        route_const = sem("route_const")
        route_max = sem("route_max")
        route_exp = sem("route_exp")
        mask_ready = sem("mask_ready")
        prefix_done = sem("prefix_done")
        list_operands = sem("list_operands")
        list_mm = sem("list_mm")
        lists_ready = sem("lists_ready")
        we_landed = [sem(f"we_landed{i}") for i in range(6)]
        gather_index = sem("gather_index")
        gathered = sem("gathered")
        scatter_index = sem("scatter_index")
        scattered = sem("scattered")
        gate_done = sem("gate_done")
        up_done = sem("up_done")
        sil_ready = sem("sil_ready")
        hid_ready = sem("hid_ready")
        mxt_done = sem("mxt_done")
        mxt_evac = sem("mxt_evac")
        ht_done = sem("ht_done")
        ht_evac = sem("ht_evac")
        y_done = sem("y_done")
        gcol_ready = sem("gcol_ready")
        y_ready = sem("y_ready")

        NI = NM * NB
        slope = [2.0 ** (-8.0 * (hh + 1) / NM) for hh in range(NM)]

        tslots = []
        for t in range(NI):
            tslots.append(("w", t))
            if t % NB == 4 and t >= NB:
                tslots.append(("y", t // NB - 1))
        tslots.append(("y", NM - 1))
        tpos = {s: n for n, s in enumerate(tslots)}

        def unit_columns(u):
            order = [0, 1, 2, 3, 4]
            return (order[u // NM] * NM + u % NM) * P

        def weights_of(e):
            kh, fh = KD // 2, KE // 2
            for w, t in ((w_expert_gate, wg), (w_expert_up, wu)):
                for s in range(2):
                    yield t[:, s * kh:(s + 1) * kh, :], \
                        w[0, e, s * kh * P:(s + 1) * kh * P, :].rearrange("(k p) n -> p k n", p=P)
            for s in range(2):
                yield wd[:, s * fh:(s + 1) * fh, :], \
                    w_expert_down[0, e, s * fh * P:(s + 1) * fh * P, :].rearrange("(k p) n -> p k n", p=P)

        def weights_of_dynamic(e):
            kh, fh = KD // 2, KE // 2
            for w, t in ((w_expert_gate, wg), (w_expert_up, wu)):
                for s in range(2):
                    yield t[:, s * kh:(s + 1) * kh, :], \
                        w[0, bass.ds(e, 1), s * kh * P:(s + 1) * kh * P, :].rearrange(
                            "o (k p) n -> p (o k) n", p=P)
            for s in range(2):
                yield wd[:, s * fh:(s + 1) * fh, :], \
                    w_expert_down[0, bass.ds(e, 1), s * fh * P:(s + 1) * fh * P, :].rearrange(
                        "o (k p) n -> p (o k) n", p=P)

        block = ctx.enter_context(nc.Block())

        @block.sync
        def _(sp_):
            def load_unit(u):
                if u >= RING:
                    sp_.wait_ge(group_done, 2 * (u - RING) + 2)
                sp_.dma_start(ring[:, u % RING, :, :],
                              w_in[0, :, unit_columns(u):unit_columns(u) + P]
                              .rearrange("(k p) n -> p k n", p=P)).then_inc(w_landed[u % RING], 16)

            for b in range(NB):
                if b >= 2:
                    sp_.wait_ge(hn_transposed, b - 1)
                sp_.dma_start(xs[:, b % 2, :], x[0, b * P:(b + 1) * P, :]).then_inc(x_landed[b % 2], 16)
                if b >= 2:
                    load_unit(b - 2)
            for u in range(NB - 2, 5 * NM):
                load_unit(u)
            sp_.wait_ge(lru_ready, NM)
            sp_.wait_ge(y_norm_mm, 2)
            sp_.dma_start(wout[:, :, :], w_out[0].rearrange("(k p) n -> p k n", p=P)).then_inc(wout_landed, 16)
            sp_.dma_start(wr[:, :, 0:NG], w_router_group[0].rearrange("(k p) n -> p k n", p=P)).then_inc(wout_landed, 16)
            for gq in range(NG):
                sp_.dma_start(wr[:, :, NG + gq * EPG:NG + (gq + 1) * EPG],
                              w_router_expert[0, gq].rearrange("(k p) n -> p k n", p=P)).then_inc(wout_landed, 16)
            sp_.dma_start(g2b[:, :], norm2_g.to_broadcast([P, D])).then_inc(wout_landed, 16)
            for b in range(2):
                sp_.dma_start(xr[:, b, :], x[0, b * P:(b + 1) * P, :]).then_inc(xr_landed[b], 16)
            sp_.wait_ge(pv_done, NI)
            for n, (dst, src) in enumerate(weights_of(0)):
                sp_.dma_start(dst, src).then_inc(we_landed[n], 16)
            sp_.wait_ge(pad_ready, 1)
            sp_.dma_start(hn2_dram[T:T + P, :], ysb[:, :]).then_inc(pad_stored, 16)
            for b in range(NB):
                sp_.wait_ge(h_ready, b + 1)
                sp_.dma_start(out[b * P:(b + 1) * P, :], h[:, b % 2, :]).then_inc(h_stored[b % 2], 16)
                if b + 2 < NB:
                    sp_.dma_start(xr[:, b % 2, :], x[0, (b + 2) * P:(b + 3) * P, :]).then_inc(xr_landed[b % 2], 16)
                sp_.wait_ge(hn2_ready, b + 1)
                sp_.dma_start(hn2_dram[b * P:(b + 1) * P, :], hn2[:, b % 2, :]).then_inc(hn2_stored[b % 2], 16)
            sp_.wait_ge(lists_ready, 1)
            with sp_.Fori(1, NE) as e:
                tiles_before = sp_.value_load(tiles_i[0:1, bass.ds(e - 1, 1)], min_val=1, max_val=MAX_TILES)
                for n, (dst, src) in enumerate(weights_of_dynamic(e)):
                    sp_.wait_ge((gate_done, up_done, y_done)[n // 2], tiles_before)
                    sp_.dma_start(dst, src).then_inc(we_landed[n], 16)
            for n in range(6):
                sp_.wait_ge(we_landed[n], 16 * NE)

        @block.gpsimd
        def _(pool):
            n = [0]

            def step(ins):
                n[0] += 1
                ins.then_inc(pool_seq, 1)
                pool.wait_ge(pool_seq, n[0])

            step(nc.gpsimd.memset(ident[:], 0.0))
            step(nc.gpsimd.memset(eps[:], EPS))
            step(nc.gpsimd.affine_select(out=ident[:], in_=ident[:], compare_op=ALU.not_equal, fill=1.0,
                                         base=0, pattern=[[-1, P]], channel_multiplier=1))
            step(nc.gpsimd.memset(ones[:], 1.0))
            step(nc.gpsimd.memset(ones_blk[:], 0.0))
            step(nc.gpsimd.memset(ones_blk[0:64, 0:64], 1.0))
            step(nc.gpsimd.memset(ones_blk[64:128, 64:128], 1.0))
            step(nc.gpsimd.memset(phalf[:], -0.5))
            nc.gpsimd.memset(bd[:], 0.0).then_inc(consts_built, 1)
            pool.wait_ge(group_done, 5 * NB)
            step(nc.gpsimd.iota(ndt[:], pattern=[[-1, T]], base=T - P, channel_multiplier=1,
                                allow_small_or_imprecise_dtypes=True))
            step(nc.gpsimd.tensor_scalar(nd[:], ndt[:], -1.0, None, ALU.mult))
            nc.gpsimd.memset(qz[:], 0.0).then_inc(nd_ready, 1)
            pool.wait_ge(nd_ready, 1)
            for hh in range(NM):
                if hh >= 2:
                    pool.wait_ge(s_done, 2 * NB * (hh - 1))
                pool.wait_ge(qk_done, 2 * hh + 2)
                for cc in range(2):
                    sl = slice(64 * cc, 64 * cc + 64)
                    nc.gpsimd.tensor_copy(qz[sl, hh % 2, cc, :], q[sl, hh, :]).then_inc(qz_ready, 1)
                    pool.wait_ge(qz_ready, 2 * hh + cc + 1)
                if hh >= 1:
                    pool.wait_ge(o_ms, hh)
                    nc.gpsimd.tensor_tensor(oss[:, (hh - 1) % 2, :], oss[:, (hh - 1) % 2, :], phalf[:], ALU.pow).then_inc(o_pow, 1)
                    pool.wait_ge(o_pow, hh)
            pool.wait_ge(o_ms, NM)
            nc.gpsimd.tensor_tensor(oss[:, (NM - 1) % 2, :], oss[:, (NM - 1) % 2, :], phalf[:], ALU.pow).then_inc(o_pow, 1)
            pool.wait_ge(o_pow, NM)
            nc.gpsimd.memset(ysb[:], 0.0).then_inc(pad_ready, 1)
            pool.wait_ge(pad_ready, 1)
            pool.dma_start(out[T:T + P, :], ysb[:, :]).then_inc(scattered, 16)
            pool.wait_ge(t_done, len(tslots))
            step(nc.gpsimd.memset(upper[:], 1.0))
            step(nc.gpsimd.affine_select(out=upper[:], in_=upper[:], compare_op=ALU.is_gt, fill=0.0,
                                         base=0, pattern=[[1, P]], channel_multiplier=-1))
            step(nc.gpsimd.iota(iota_row[:], pattern=[[1, P]], base=0, channel_multiplier=0,
                                allow_small_or_imprecise_dtypes=True))
            step(nc.gpsimd.iota(tok1[:], pattern=[[P, NB]], base=1, channel_multiplier=1,
                                allow_small_or_imprecise_dtypes=True))
            nc.gpsimd.iota(pad1[:], pattern=[[0, 32]], base=T, channel_multiplier=1,
                           allow_small_or_imprecise_dtypes=True).then_inc(route_const, 1)
            for b in range(2):
                pool.wait_ge(hn2_stored[b], 16 * NB // 2)
                pool.wait_ge(h_stored[b], 16 * NB // 2)
            pool.wait_ge(pad_stored, 16)
            pool.wait_ge(scattered, 16)
            pool.wait_ge(lists_ready, 1)
            nt = pool.value_load(tiles_i[0:1, NE:NE + 1], min_val=NE, max_val=MAX_TILES)

            def gather():
                nc.gpsimd.indirect_dma_start(
                    out=xg[:], out_offset=None, in_=hn2_dram,
                    in_offset=bass.IndirectOffsetOnAxis(ap=idx_g[:, 0:1], axis=0)).then_inc(gathered, 16)

            step(nc.gpsimd.tensor_copy(idx_g[:, 0:1], ltok[:, 0:1]))
            gather()
            with pool.Fori(0, nt) as g:
                pool.wait_ge(mxt_done, g + 1)
                nc.gpsimd.tensor_copy(idx_g[:, 0:1], ltok[:, bass.ds(g + 1, 1)]).then_inc(gather_index, 1)
                pool.wait_ge(lists_ready, 1)
                pool.wait_ge(gather_index, g + 1)
                gather()
                pool.wait_ge(scattered, g * 16 + 16)
                nc.gpsimd.tensor_copy(idx_s[:, 0:1], ltok[:, bass.ds(g, 1)]).then_inc(scatter_index, 1)
                pool.wait_ge(lists_ready, 1)
                pool.wait_ge(scatter_index, g + 1)
                pool.wait_ge(y_ready, g + 1)
                nc.gpsimd.indirect_dma_start(
                    out=out, out_offset=bass.IndirectOffsetOnAxis(ap=idx_s[:, 0:1], axis=0),
                    in_=ysb[:], in_offset=None, compute_op=ALU.add).then_inc(scattered, 16)
            pool.wait_ge(scattered, nt * 16 + 16)
            pool.wait_ge(gathered, nt * 16 + 16)

        @block.scalar
        def _(act):
            n = [0]

            def step(ins):
                n[0] += 1
                ins.then_inc(act_seq, 1)
                act.wait_ge(act_seq, n[0])

            A = nc.scalar.activation
            vrows = [(conv_w[0].rearrange("j (m c) -> (j m) c", c=P), CW, 4 * NM)]
            for ap, row in ((conv_b, CB), (b_gate_a, BA), (b_gate_x, BX), (lru_lambda, LAM), (lru_out_g, LG)):
                vrows.append((ap[0].rearrange("(m c) -> m c", c=P), row, NM))
            vrows.append((sub_norm_g, SG, 1))
            nvec = 0
            for src, row, cnt in vrows:
                act.dma_start(vrow[row:row + cnt, :], src).then_inc(vec_landed, 16)
                nvec += 16
            for src, row in ((q_norm_g, QG), (k_norm_g, KG)):
                for s in range(2):
                    act.dma_start(vrow[row:row + 1, s * HD:(s + 1) * HD], src).then_inc(vec_landed, 16)
                    nvec += 16
            for j, src in enumerate((lambda_q1, lambda_k1, lambda_q2, lambda_k2)):
                act.dma_start(lamv[:, j, :], src.to_broadcast([P, HD])).then_inc(bcast_landed, 16)
            act.dma_start(g1b[:, :], norm1_g.to_broadcast([P, D])).then_inc(g1_landed, 16)
            act.wait_ge(consts_built, 1)
            for gi, src in enumerate((w_gate_a, w_gate_x)):
                for s in range(2):
                    act.dma_start(bd[64 * s:64 * s + 64, gi, :, 64 * s:64 * s + 64],
                                  src[0].rearrange("(m two) c d -> two c m d", two=2)[s]).then_inc(bd_landed, 16)
            act.dma_start(br[:, 0:NG], b_router_group.to_broadcast([P, NG])).then_inc(br_landed, 16)
            act.dma_start(br[:, NG:NR], b_router_expert.rearrange("a g e -> a (g e)").to_broadcast([P, NE])).then_inc(br_landed, 16)

            act.wait_ge(vec_ready, 1)
            step(A(sp[:, 0, :], vc[:, LAM:LAM + NM], ACT.Abs))
            A(sp[:, 1, :], sp[:, 0, :], ACT.Exp, scale=-1.0).then_inc(lam_y, 1)
            act.wait_ge(lam_dots, 2)
            A(lams[:, 2:4], lams[:, 0:2], ACT.Exp).then_inc(lam_exp, 1)
            for b in range(NB + 1):
                if b < NB:
                    act.wait_ge(x_landed[b % 2], 16 * (b // 2 + 1))
                    if b == 0:
                        act.wait_ge(sp_ready, 1)
                    step(A(junk[:], xs[:, b % 2, :], ACT.Square, accum_out=ss[:, b:b + 1]))
                    A(ss[:, b:b + 1], ss[:, b:b + 1], ACT.Sqrt, scale=1.0 / D, bias=eps[:, 0:1]).then_inc(x_rms, 1)
                if b >= 1:
                    bb = b - 1
                    act.wait_ge(hn_transposed, bb + 1)
                    A(hnT[:, 0:4, bb * P:(bb + 1) * P], ps[:, 2 * (bb % 2), :].rearrange("p (k n) -> p k n", n=P),
                      ACT.Copy).then_inc(hnT_act, 1)
                    act.wait_ge(hnT_act, bb + 1)
            for g in range(4 * NM):
                m, s = g // 2 % NM, g % 2
                act.wait_ge(group_done, g + 1)
                if g < 2 * NM:
                    A(xlp[:, m, 3 + s * HALF:3 + (s + 1) * HALF], ps[:, g % 4, :], ACT.Copy).then_inc(lru_evac, 1)
                else:
                    A(gg[:, m, s * HALF:(s + 1) * HALF], ps[:, g % 4, :], ACT.Gelu_apprx_tanh).then_inc(lru_evac, 1)
            for j in range(4 * NM):
                m, gi, s = j // 4, j // 2 % 2, j % 2
                act.wait_ge(gate_mm, j + 1)
                dst = (r, ig)[gi]
                A(dst[:, m, s * HALF:(s + 1) * HALF], ps[:, 6 + j % 2, :], ACT.Sigmoid,
                  bias=vc[:, (BA, BX)[gi] + m:(BA, BX)[gi] + m + 1]).then_inc(gate_sig, 1)
            act.wait_ge(conv_done, NM)
            act.wait_ge(gate_sig, 4 * NM)
            for m in range(NM):
                A(a2[:, m, :], r[:, m, :], ACT.Exp, scale=sp[:, 5, m:m + 1]).then_inc(lru_exp, 1)
                A(th[:, m, :], r[:, m, :], ACT.Tanh, scale=sp[:, 6, m:m + 1]).then_inc(lru_exp, 1)
                act.wait_ge(lru_exp, 3 * m + 2)
                A(r[:, m, :], r[:, m, :], ACT.Exp, scale=sp[:, 4, m:m + 1]).then_inc(lru_exp, 1)
            for m in range(NM):
                act.wait_ge(om_ready, m + 1)
                A(th[:, m, :], th[:, m, :], ACT.Sqrt).then_inc(om_sqrt, 1)
            for j in range(4 * NM + 1):
                g = 4 * NM + j
                if j < 4 * NM:
                    act.wait_ge(group_done, g + 1)
                    if j >= 2:
                        act.wait_ge(qk_mm, j - 1)
                    A(sq[:, j % 2, :], ps[:, g % 4, :], ACT.Square).then_inc(qk_sq, 1)
                if j >= 1:
                    jj = j - 1
                    act.wait_ge(qk_mm, jj + 1)
                    if jj >= 2:
                        act.wait_ge(qk_done, jj - 1)
                    A(rt[:, jj % 2, :], ps[:, 4 + jj % 2, :], ACT.Sqrt, scale=1.0 / HD, bias=eps[:, 0:1]).then_inc(qk_rms, 1)
            for m in range(NM):
                act.wait_ge(y_lru, m + 1)
                A(th[:, m, :], gg[:, m, :], ACT.Square).then_inc(y_sq, 1)
            for s in range(2):
                act.wait_ge(y_norm_mm, s + 1)
                A(ig[:, 0, s * HALF:(s + 1) * HALF], ps[:, 6 + s, :], ACT.Sqrt, scale=1.0 / (NM * P), bias=eps[:, 0:1]).then_inc(y_rms, 1)
            for b in range(NB):
                act.wait_ge(group_done, 8 * NM + b + 1)
                if b == 0:
                    act.wait_ge(om_ready, NM)
                A(v[:, b, :], ps[:, b % 4, :], ACT.Copy).then_inc(v_evac, 1)
            for t in range(NI + 3):
                if t < NI:
                    hh, i = t // NB, t % NB
                    w = P * (i + 1)
                    act.wait_ge(s_nmax, t + 1)
                    for cc in range(2):
                        A(pr[:, t % 3, cc, 0:w], pr[:, t % 3, cc, 0:w], ACT.Exp, scale=slope[hh],
                          bias=nb[:, t, cc:cc + 1], accum_out=sm[:, t, cc:cc + 1]).then_inc(p_ready, 1)
                for kind, tt in ((kd, tt) for kd, tt in tslots
                                 if (kd == "w" and tt == t - 2) or (kd == "y" and tt < NM - 1 and t - 2 == NB * (tt + 1) + 4)
                                 or (kd == "y" and tt == NM - 1 and t == NI + 2)):
                    ti = tpos[(kind, tt)]
                    act.wait_ge(t_done, ti + 1)
                    src = ps[:, 4:6, :].rearrange("p a n -> p (a n)")
                    if kind == "w":
                        w = P * (tt % NB + 1)
                        if tt >= 2:
                            act.wait_ge(pv_done, tt - 1)
                        A(wT[:, tt % 2, 0:w], src[:, 0:w], ACT.Copy).then_inc(t_evac, 1)
                    else:
                        A(yatt[:, tt, :], src, ACT.Copy, scale=lams[:, 6:7]).then_inc(t_evac, 1)
            for b in range(NB + 1):
                if b < NB:
                    act.wait_ge(h_ready, b + 1)
                    step(A(junk[:], h[:, b % 2, :], ACT.Square, accum_out=ss[:, b:b + 1]))
                    A(ss[:, b:b + 1], ss[:, b:b + 1], ACT.Sqrt, scale=1.0 / D, bias=eps[:, 0:1]).then_inc(h_rms, 1)
                if b >= 1:
                    bb = b - 1
                    act.wait_ge(xt2_done, bb + 1)
                    if bb >= 2:
                        act.wait_ge(r_done, bb - 1)
                    A(hn2T[:, bb % 2, :, :], ps[:, 4:6, :].rearrange("p a (k n) -> p (a k) n", n=P), ACT.Copy).then_inc(xt2_evac, 1)
            act.wait_ge(route_max, 1)
            step(A(gexp[:], gexp[:], ACT.Exp))
            A(edif[:], edif[:], ACT.Exp).then_inc(route_exp, 1)
            act.wait_ge(lists_ready, 1)
            nt = act.value_load(tiles_i[0:1, NE:NE + 1], min_val=NE, max_val=MAX_TILES)
            act.wait_ge(mxt_done, 1)
            A(xT[:, :, :].rearrange("p k n -> p (k n)"), xT_ps, ACT.Copy).then_inc(mxt_evac, 1)
            with act.Fori(0, nt) as g:
                act.wait_ge(gate_done, g + 1)
                A(sil[:], ps[:, 0, :], ACT.Silu).then_inc(sil_ready, 1)
                act.wait_ge(mxt_done, g + 2)
                A(xT[:, :, :].rearrange("p k n -> p (k n)"), xT_ps, ACT.Copy).then_inc(mxt_evac, 1)
                act.wait_ge(ht_done, g + 1)
                A(hT[:, :, :].rearrange("p k n -> p (k n)"), ps[:, 6, :], ACT.Copy).then_inc(ht_evac, 1)

        @block.vector
        def _(dve):
            n = [0]
            V = nc.vector

            def step(ins):
                n[0] += 1
                ins.then_inc(dve_seq, 1)
                dve.wait_ge(dve_seq, n[0])

            step(V.memset(xlp[:, :, 0:3], 0.0))
            dve.wait_ge(vec_transposed, 1)
            step(V.tensor_copy(vc[:, 0:NV], ps[:, 7, 0:NV]))
            for hh in range(NM):
                step(V.tensor_scalar(qgh[:, hh:hh + 1], vc[:, QG:QG + 1], HD ** -0.5 / slope[hh], None, ALU.mult))
            V.tensor_scalar(lams[:, 6:7], vc[:, SG:SG + 1], 1.0 - LAMBDA_INIT, None, ALU.mult).then_inc(vec_ready, 1)
            dve.wait_ge(vec_ready, 1)
            dve.wait_ge(bcast_landed, 64)
            for j in range(2):
                V.tensor_tensor_reduce(out=lamv[:, 2 * j, :], in0=lamv[:, 2 * j, :], in1=lamv[:, 2 * j + 1, :], scale=1.0,
                                       scalar=0.0, op0=ALU.mult, op1=ALU.add, accum_out=lams[:, j:j + 1]).then_inc(lam_dots, 1)
            dve.wait_ge(lam_y, 1)
            y_, z_, z2, acc = sp[:, 1, :], sp[:, 2, :], sp[:, 3, :], sp[:, 7, :]
            step(V.tensor_scalar(z2, y_, 2.0, None, ALU.add))
            step(V.reciprocal(z2, z2))
            step(V.tensor_tensor(z_, y_, z2, ALU.mult))
            step(V.tensor_tensor(z2, z_, z_, ALU.mult))
            step(V.tensor_scalar(acc, z2, 1.0 / 17, 1.0 / 15, ALU.mult, ALU.add))
            for d in (13, 11, 9, 7, 5, 3, 1):
                step(V.tensor_tensor(acc, acc, z2, ALU.mult))
                step(V.tensor_scalar(acc, acc, 1.0 / d, None, ALU.add))
            step(V.tensor_tensor(acc, acc, z_, ALU.mult))
            step(V.tensor_scalar(z_, vc[:, LAM:LAM + NM], -1.0, 0.0, ALU.mult, ALU.max))
            step(V.scalar_tensor_tensor(out=acc, in0=acc, scalar=2.0, in1=z_, op0=ALU.mult, op1=ALU.add))
            step(V.tensor_scalar(sp[:, 4, :], acc, -LRU_C, None, ALU.mult))
            step(V.tensor_scalar(sp[:, 5, :], acc, -2.0 * LRU_C, None, ALU.mult))
            step(V.tensor_scalar(sp[:, 6, :], acc, LRU_C, None, ALU.mult))
            dve.wait_ge(lam_exp, 1)
            step(V.tensor_tensor(lams[:, 4:5], lams[:, 3:4], lams[:, 2:3], ALU.subtract))
            V.tensor_scalar(lams[:, 5:6], lams[:, 4:5], -LAMBDA_INIT, None, ALU.add).then_inc(sp_ready, 1)
            neg_lam = lams[:, 5:6]
            dve.wait_ge(g1_landed, 16)
            for b in range(NB + 1):
                if b < NB:
                    dve.wait_ge(x_rms, b + 1)
                    step(V.reciprocal(rs[:, b:b + 1], ss[:, b:b + 1]))
                    V.scalar_tensor_tensor(out=xs[:, b % 2, :], in0=xs[:, b % 2, :], scalar=rs[:, b:b + 1],
                                           in1=g1b[:], op0=ALU.mult, op1=ALU.mult).then_inc(hn_ready, 1)
                if b >= 1:
                    bb = b - 1
                    dve.wait_ge(hn_transposed, bb + 1)
                    V.tensor_copy(hnT[:, 4:8, bb * P:(bb + 1) * P],
                                  ps[:, 2 * (bb % 2) + 1, :].rearrange("p (k n) -> p k n", n=P)).then_inc(hnT_dve, 1)
            for m in range(NM):
                dve.wait_ge(lru_evac, 2 * m + 2)
                step(V.tensor_scalar(xc[:, m, :], xlp[:, m, 0:T], vc[:, CW + m:CW + m + 1],
                                     vc[:, CB + m:CB + m + 1], ALU.mult, ALU.add))
                for j in (1, 2, 3):
                    ins = V.scalar_tensor_tensor(out=xc[:, m, :], in0=xlp[:, m, j:j + T],
                                                 scalar=vc[:, CW + NM * j + m:CW + NM * j + m + 1],
                                                 in1=xc[:, m, :], op0=ALU.mult, op1=ALU.add)
                    if j < 3:
                        step(ins)
                ins.then_inc(conv_done, 1)
            dve.wait_ge(conv_done, NM)
            for m in range(NM):
                dve.wait_ge(lru_exp, 3 * m + 2)
                V.scalar_tensor_tensor(out=th[:, m, :], in0=a2[:, m, :], scalar=1.0, in1=th[:, m, :],
                                       op0=ALU.add, op1=ALU.mult).then_inc(om_ready, 1)
                dve.wait_ge(gate_sig, 4 * m + 4)
                step(V.tensor_tensor(ig[:, m, :], ig[:, m, :], xc[:, m, :], ALU.mult))
            for m in range(NM):
                dve.wait_ge(om_sqrt, m + 1)
                dve.wait_ge(lru_exp, 3 * m + 3)
                step(V.tensor_tensor(ig[:, m, :], ig[:, m, :], th[:, m, :], ALU.mult))
                step(V.tensor_tensor_scan(xc[:, m, :], r[:, m, :], ig[:, m, :], 0.0, ALU.mult, ALU.add))
                V.tensor_tensor(gg[:, m, :], gg[:, m, :], xc[:, m, :], ALU.mult).then_inc(y_lru, 1)
            for j in range(4 * NM):
                m, s, isk = j // 2 % NM, j % 2, j >= 2 * NM
                dve.wait_ge(qk_rms, j + 1)
                step(V.reciprocal(rt[:, j % 2, :], rt[:, j % 2, :]))
                gain = vc[:, KG:KG + 1] if isk else qgh[:, m:m + 1]
                V.scalar_tensor_tensor(out=(k if isk else q)[:, m, s * HALF:(s + 1) * HALF], in0=ps[:, (4 * NM + j) % 4, :],
                                       scalar=gain, in1=rt[:, j % 2, :], op0=ALU.mult, op1=ALU.mult).then_inc(qk_done, 1)
            dve.wait_ge(y_rms, 2)
            step(V.reciprocal(ig[:, 0, :], ig[:, 0, :]))
            dve.wait_ge(y_sq, NM)
            for m in range(NM):
                V.scalar_tensor_tensor(out=gg[:, m, :], in0=gg[:, m, :], scalar=vc[:, LG + m:LG + m + 1],
                                       in1=ig[:, 0, :], op0=ALU.mult, op1=ALU.mult).then_inc(lru_ready, 1)
            dve.wait_ge(nd_ready, 1)
            step(V.tensor_tensor(nd[:], nd[:], ndt[:], ALU.min))
            step(V.memset(nd[0:CHUNK, T - CHUNK:T], NEG_BIG))
            for t in range(NI + 6):
                if t < NI:
                    hh, i = t // NB, t % NB
                    w = P * (i + 1)
                    for cc in range(2):
                        dve.wait_ge(s_done, 2 * t + cc + 1)
                        if t >= 3:
                            dve.wait_ge(t_done, tpos[("w", t - 3)] + 1)
                        src = ps[:, 2 * cc:2 * cc + 2, :].rearrange("p a n -> p (a n)")
                        V.tensor_tensor_reduce(out=pr[:, t % 3, cc, 0:w], in0=src[:, 0:w], in1=nd[:, T - w:T], scale=1.0,
                                               scalar=-3e38, op0=ALU.add, op1=ALU.max,
                                               accum_out=mx[:, t, cc:cc + 1]).then_inc(s_biased, 1)
                    dve.wait_ge(s_biased, 2 * t + 2)
                    V.tensor_scalar(nb[:, t, :], mx[:, t, :], -slope[hh], None, ALU.mult).then_inc(s_nmax, 1)
                u = t - 4
                if 0 <= u < NI:
                    dve.wait_ge(pv_done, u + 1)
                    hh, i = u // NB, u % NB
                    if hh >= 2 and i == 0:
                        dve.wait_ge(t_done, tpos[("y", hh - 2)] + 1)
                    V.tensor_scalar(osb[:, hh % 2, i, :], ps[:, 6 + u % 2, 0:P], ri[:, u, 0:1], None, ALU.mult).then_inc(o_evac, 1)
                    if i == NB - 1:
                        dve.wait_ge(o_evac, u + 1)
                        step(V.tensor_tensor(osq[:], osb[:, hh % 2, :, :], osb[:, hh % 2, :, :], ALU.mult))
                        step(V.tensor_reduce(out=oss[:, hh % 2, :], in_=osq[:], axis=AX.X, op=ALU.add))
                        V.tensor_scalar(oss[:, hh % 2, :], oss[:, hh % 2, :], 1.0 / P, EPS, ALU.mult, ALU.add).then_inc(o_ms, 1)
                u = t - 1
                if 0 <= u < NI:
                    w = P * (u % NB + 1)
                    dve.wait_ge(p_ready, 2 * u + 2)
                    step(V.reciprocal(ri[:, u, :], sm[:, u, :]))
                    step(V.tensor_scalar(ra[:, u:u + 1], ri[:, u, 1:2], neg_lam, sm[:, u, 0:1], ALU.mult, ALU.mult))
                    V.scalar_tensor_tensor(out=pr[:, u % 3, 1, 0:w], in0=pr[:, u % 3, 1, 0:w], scalar=ra[:, u:u + 1],
                                           in1=pr[:, u % 3, 0, 0:w], op0=ALU.mult, op1=ALU.add).then_inc(w_ready, 1)
                u = t - 5
                if 0 <= u < NI and u % NB == NB - 1:
                    hh = u // NB
                    dve.wait_ge(o_pow, hh + 1)
                    V.tensor_tensor(osb[:, hh % 2, :, :], osb[:, hh % 2, :, :],
                                    oss[:, hh % 2, :].unsqueeze(2).to_broadcast([P, NB, P]), ALU.mult).then_inc(o_normed, 1)
            for b in range(NB + 2):
                if b < NB:
                    dve.wait_ge(op_done, b + 1)
                    dve.wait_ge(xr_landed[b % 2], 16 * (b // 2 + 1))
                    if b >= 2:
                        dve.wait_ge(h_stored[b % 2], 16 * (b // 2))
                        dve.wait_ge(hn2_stored[b % 2], 16 * (b // 2))
                        dve.wait_ge(xt2_done, b - 1)
                    src = ps[:, 2 * (b % 2):2 * (b % 2) + 2, :].rearrange("p a n -> p (a n)")
                    V.tensor_tensor(h[:, b % 2, :], src, xr[:, b % 2, :], ALU.add).then_inc(h_ready, 1)
                    dve.wait_ge(h_rms, b + 1)
                    if b == 0:
                        dve.wait_ge(wout_landed, 16 * 7)
                        dve.wait_ge(br_landed, 32)
                    step(V.reciprocal(rs[:, b:b + 1], ss[:, b:b + 1]))
                    V.scalar_tensor_tensor(out=hn2[:, b % 2, :], in0=h[:, b % 2, :], scalar=rs[:, b:b + 1],
                                           in1=g2b[:], op0=ALU.mult, op1=ALU.mult).then_inc(hn2_ready, 1)
                if b >= 2:
                    bb = b - 2
                    dve.wait_ge(r_done, bb + 1)
                    V.tensor_tensor(lg[:, bb, :], ps[:, 6 + bb % 2, 0:NR], br[:], ALU.add).then_inc(logits_ready, 1)
            dve.wait_ge(logits_ready, NB)
            dve.wait_ge(route_const, 1)

            def first_max(onehot, values, top, free, cnt):
                step(V.tensor_reduce(out=top, in_=values, axis=AX.X, op=ALU.max))
                step(V.tensor_tensor(onehot, values, top.unsqueeze(2).to_broadcast([P, NB, cnt]), ALU.is_equal))
                step(V.tensor_scalar(free, onehot[:, :, 0], -1.0, 1.0, ALU.mult, ALU.add))
                for j in range(1, cnt):
                    step(V.tensor_tensor(onehot[:, :, j], onehot[:, :, j], free, ALU.mult))
                    if j < cnt - 1:
                        step(V.tensor_tensor(free, free, onehot[:, :, j], ALU.subtract))

            lgg = lg[:, :, 0:NG]
            first_max(ohg[:], lgg, gtop[:], free[:], NG)
            step(V.tensor_tensor(gexp[:], lgg, gtop[:].unsqueeze(2).to_broadcast([P, NB, NG]), ALU.subtract))
            for gq in range(NG):
                le = lg[:, :, NG + gq * EPG:NG + (gq + 1) * EPG]
                oh = ohg[:, :, gq].unsqueeze(2).to_broadcast([P, NB, EPG])
                if gq == 0:
                    step(V.tensor_tensor(sel[:], le, oh, ALU.mult))
                else:
                    step(V.tensor_tensor(stmp[:], le, oh, ALU.mult))
                    step(V.tensor_tensor(sel[:], sel[:], stmp[:], ALU.add))
            first_max(oh1[:], sel[:], etop1[:], free[:], EPG)
            step(V.tensor_scalar(stmp[:], oh1[:], -3e38, None, ALU.mult))
            step(V.tensor_tensor(stmp[:], stmp[:], sel[:], ALU.add))
            first_max(oh2[:], stmp[:], etop2[:], free[:], EPG)
            V.tensor_tensor(edif[:], etop2[:], etop1[:], ALU.subtract).then_inc(route_max, 1)
            for j, oh in enumerate((oh1, oh2)):
                for gq in range(NG):
                    step(V.tensor_tensor(mm[:, j, :, gq * EPG:(gq + 1) * EPG], oh[:],
                                         ohg[:, :, gq].unsqueeze(2).to_broadcast([P, NB, EPG]), ALU.mult))
            step(V.tensor_tensor(msum[:], mm[:, 0, :, :], mm[:, 1, :, :], ALU.add))
            step(V.memset(mcum[:, 0, :], 0.0))
            for b in range(1, NB):
                step(V.tensor_tensor(mcum[:, b, :], mcum[:, b - 1, :], msum[:, b - 1, :], ALU.add))
            V.tensor_tensor(mtot[:], mcum[:, NB - 1, :], msum[:, NB - 1, :], ALU.add).then_inc(mask_ready, 1)
            dve.wait_ge(route_exp, 1)
            step(V.tensor_reduce(out=gsum[:], in_=gexp[:], axis=AX.X, op=ALU.add))
            step(V.tensor_scalar(esum[:], edif[:], 1.0, None, ALU.add))
            step(V.tensor_tensor(gsum[:], gsum[:], esum[:], ALU.mult))
            step(V.reciprocal(gates[:, 0, :], gsum[:]))
            step(V.tensor_tensor(gates[:, 1, :], gates[:, 0, :], edif[:], ALU.mult))
            dve.wait_ge(prefix_done, 2)
            step(V.tensor_copy(cnt[:], ps[:, 1, 0:NE]))
            step(V.memset(ntile[:], 1.0))
            for j in range(1, NB):
                step(V.scalar_tensor_tensor(out=ntile[:], in0=cnt[:], scalar=float(P * j), in1=ntile[:],
                                            op0=ALU.is_gt, op1=ALU.add))
            step(V.tensor_tensor_scan(tincl[:, 0:NE], ones[:, 0:NE], ntile[:], 0.0, ALU.mult, ALU.add))
            step(V.tensor_copy(tincl[:, NE:NE + 1], tincl[:, NE - 1:NE]))
            step(V.tensor_copy(tiles_i[:], tincl[:]))
            step(V.tensor_tensor(texcl[:], tincl[:, 0:NE], ntile[:], ALU.subtract))
            step(V.scalar_tensor_tensor(out=slotm[:], in0=texcl[:].unsqueeze(1).to_broadcast([P, NB, NE]), scalar=float(P),
                                        in1=ps[:, 0, 0:NB * NE].rearrange("p (b e) -> p b e", e=NE), op0=ALU.mult, op1=ALU.add))
            for j in range(2):
                step(V.tensor_tensor(stmp2[:], slotm[:], mm[:, j, :, :], ALU.mult))
                step(V.tensor_reduce(out=slot[:, j, :], in_=stmp2[:], axis=AX.X, op=ALU.add))
            step(V.tensor_copy(slot_i[:], slot[:]))
            step(V.tensor_scalar(srow_i[:], slot_i[:], P - 1, None, ALU.bitwise_and))
            step(V.tensor_scalar(scol_i[:], slot_i[:], 7, None, ALU.logical_shift_right))
            step(V.tensor_copy(srow[:], srow_i[:]))
            step(V.tensor_copy(scol[:], scol_i[:]))
            for j in range(2 * NB):
                jj, b = j % 2, j // 2
                if j >= 2:
                    dve.wait_ge(list_mm, j - 1)
                step(V.tensor_scalar(lrow[:, jj, :], iota_row[:], srow[:, jj, b:b + 1], None, ALU.is_equal))
                step(V.tensor_scalar(lval[:, jj, 0, :], iota_row[:, 0:32], scol[:, jj, b:b + 1], tok1[:, b:b + 1],
                                     ALU.is_equal, ALU.mult))
                V.tensor_scalar(lval[:, jj, 1, :], iota_row[:, 0:32], scol[:, jj, b:b + 1], gates[:, jj, b:b + 1],
                                ALU.is_equal, ALU.mult).then_inc(list_operands, 1)
            step(V.tensor_tensor(tcmp[:], iota_row[:, 0:32].unsqueeze(2).to_broadcast([P, 32, NE]),
                                 tincl[:, 0:NE].unsqueeze(1).to_broadcast([P, 32, NE]), ALU.is_ge))
            step(V.tensor_reduce(out=texp[:], in_=tcmp[:], axis=AX.X, op=ALU.add))
            step(V.tensor_copy(texp_i[:], texp[:]))
            dve.wait_ge(list_mm, 2 * NB)
            step(V.tensor_copy(ltok[:], ps[:, 2, 0:32]))
            step(V.tensor_copy(lgate[:], ps[:, 2, 32:64]))
            step(V.tensor_scalar(lemp[:], ltok[:], 0.0, 1.0, ALU.is_equal, ALU.mult))
            step(V.scalar_tensor_tensor(out=ltok[:], in0=ltok[:], scalar=-1.0, in1=lemp[:], op0=ALU.add, op1=ALU.add))
            step(V.tensor_tensor(lemp[:], lemp[:], pad1[:], ALU.mult))
            V.tensor_tensor(ltok[:], ltok[:], lemp[:], ALU.add).then_inc(lists_ready, 1)
            dve.wait_ge(lists_ready, 1)
            nt = dve.value_load(tiles_i[0:1, NE:NE + 1], min_val=NE, max_val=MAX_TILES)
            dve.wait_ge(pad_stored, 16)
            dve.wait_ge(scattered, 16)
            with dve.Fori(0, nt) as g:
                V.tensor_copy(gcol[:, 0:1], lgate[:, bass.ds(g, 1)]).then_inc(gcol_ready, 1)
                dve.wait_ge(sil_ready, g + 1)
                dve.wait_ge(up_done, g + 1)
                V.tensor_tensor(hid[:], ps[:, 1, :], sil[:], ALU.mult).then_inc(hid_ready, 1)
                dve.wait_ge(gcol_ready, g + 1)
                dve.wait_ge(y_done, g + 1)
                dve.wait_ge(scattered, g * 16 + 16)
                V.tensor_scalar(ysb[:], y_ps, gcol[:, 0:1], None, ALU.mult).then_inc(y_ready, 1)
                dve.wait_ge(y_ready, g + 1)

        @block.tensor
        def _(pe):
            mm_, tr = nc.tensor.matmul, nc.tensor.transpose

            pe.wait_ge(consts_built, 1)
            pe.wait_ge(vec_landed, 16 * 11)
            tr(ps[:, 7, 0:NV], vrow[0:NV, :], ident[0:NV, 0:NV]).then_inc(vec_transposed, 1)
            for b in range(NB):
                pe.wait_ge(hn_ready, b + 1)
                if b >= 2:
                    pe.wait_ge(hnT_act, b - 1)
                    pe.wait_ge(hnT_dve, b - 1)
                for kk in range(KD):
                    last = tr(ps[:, 2 * (b % 2) + kk // 4, kk % 4 * P:(kk % 4 + 1) * P],
                              xs[:, b % 2, kk * P:(kk + 1) * P], ident[:])
                last.then_inc(hn_transposed, 1)
            pe.wait_ge(hnT_act, NB)
            pe.wait_ge(hnT_dve, NB)

            def bank_free(g):
                if g < 4 * NM:
                    pe.wait_ge(lru_evac, g + 1)
                elif g < 8 * NM:
                    pe.wait_ge(qk_done, g - 4 * NM + 1)
                else:
                    pe.wait_ge(v_evac, g - 8 * NM + 1)

            def qk_norm(j):
                pe.wait_ge(qk_sq, j + 1)
                if j >= 2:
                    pe.wait_ge(qk_rms, j - 1)
                mm_(ps[:, 4 + j % 2, :], ones_blk[:], sq[:, j % 2, :], start=True, stop=True).then_inc(qk_mm, 1)

            for u in range(4 * NM):
                pe.wait_ge(w_landed[u % RING], 16 * (u // RING + 1))
                for s in range(2):
                    g = 2 * u + s
                    if g >= 4:
                        bank_free(g - 4)
                    for kk in range(KD):
                        last = mm_(ps[:, g % 4, :], ring[:, u % RING, kk, :], hnT[:, kk, s * HALF:(s + 1) * HALF],
                                   start=(kk == 0), stop=(kk == KD - 1))
                    last.then_inc(group_done, 1)
                    if g >= 4 * NM + 1:
                        qk_norm(g - 4 * NM - 1)
                if u == 2 * NM - 1:
                    pe.wait_ge(bd_landed, 64)
                    for j in range(4 * NM):
                        m, gi, s = j // 4, j // 2 % 2, j % 2
                        pe.wait_ge(conv_done, m + 1)
                        if j >= 2:
                            pe.wait_ge(gate_sig, j - 1)
                        mm_(ps[:, 6 + j % 2, :], bd[:, gi, m, :], xc[:, m, s * HALF:(s + 1) * HALF],
                            start=True, stop=True).then_inc(gate_mm, 1)
            for u in range(4 * NM, 5 * NM):
                pe.wait_ge(w_landed[u % RING], 16 * (u // RING + 1))
            s0 = 4 * NM % RING
            for b in range(NB):
                g = 8 * NM + b
                bank_free(g - 4)
                for kk in range(KD):
                    last = mm_(ps[:, g % 4, :].rearrange("p (u n) -> p u n", n=P), hnT[:, kk, b * P:(b + 1) * P],
                               ring[:, s0:s0 + NM, kk, :], start=(kk == 0), stop=(kk == KD - 1))
                last.then_inc(group_done, 1)
                if b == 0:
                    qk_norm(4 * NM - 1)
                if b == 1:
                    pe.wait_ge(gate_sig, 4 * NM)
                    for s in range(2):
                        for m in range(NM):
                            pe.wait_ge(y_sq, m + 1)
                            last = mm_(ps[:, 6 + s, :], ones[:], th[:, m, s * HALF:(s + 1) * HALF],
                                       start=(m == 0), stop=(m == NM - 1))
                        last.then_inc(y_norm_mm, 1)
            pe.wait_ge(v_evac, NB)
            pe.wait_ge(qk_done, 4 * NM)
            pe.wait_ge(y_rms, 2)
            for t in range(NI + 4):
                if t < NI:
                    hh, i = t // NB, t % NB
                    w = P * (i + 1)
                    pe.wait_ge(qz_ready, 2 * hh + 2)
                    for cc in range(2):
                        if t >= 1:
                            pe.wait_ge(s_biased, 2 * (t - 1) + cc + 1)
                        for s in range(0, w, HALF):
                            last = mm_(ps[:, 2 * cc + s // HALF, 0:min(HALF, w - s)], qz[:, hh % 2, cc, i * P:(i + 1) * P],
                                       k[:, hh, s:min(w, s + HALF)], start=True, stop=True)
                        last.then_inc(s_done, 1)
                u = t - 3
                if 0 <= u < NI:
                    hh, i = u // NB, u % NB
                    pe.wait_ge(t_evac, tpos[("w", u)] + 1)
                    if u >= 2:
                        pe.wait_ge(o_evac, u - 1)
                    for j in range(i + 1):
                        last = mm_(ps[:, 6 + u % 2, 0:P], wT[:, u % 2, j * P:(j + 1) * P], v[:, j, hh * P:(hh + 1) * P],
                                   start=(j == 0), stop=(j == i))
                    last.then_inc(pv_done, 1)
                for kind, tt in tslots:
                    if not ((kind == "w" and tt == t - 2) or (kind == "y" and tt < NM - 1 and t - 2 == NB * (tt + 1) + 4)
                            or (kind == "y" and tt == NM - 1 and t == NI + 3)):
                        continue
                    ti = tpos[(kind, tt)]
                    if ti >= 1:
                        pe.wait_ge(t_evac, ti)
                    if kind == "w":
                        pe.wait_ge(w_ready, tt + 1)
                    else:
                        pe.wait_ge(o_normed, tt + 1)
                    cols = tt % NB + 1 if kind == "w" else NB
                    for j in range(cols):
                        src = pr[:, tt % 3, 1, j * P:(j + 1) * P] if kind == "w" else osb[:, tt % 2, j, :]
                        last = tr(ps[:, 4 + j // 4, j % 4 * P:(j % 4 + 1) * P], src, ident[:])
                    last.then_inc(t_done, 1)
            pe.wait_ge(t_evac, len(tslots))
            pe.wait_ge(lru_ready, NM)
            pe.wait_ge(wout_landed, 16 * 7)
            pe.wait_ge(s_biased, 2 * NI)
            pe.wait_ge(o_evac, NI)
            for b in range(NB + 2):
                if b < NB:
                    if b >= 2:
                        pe.wait_ge(h_ready, b - 1)
                    for s in range(2):
                        for kk in range(KD):
                            y = gg if kk < NM else yatt
                            last = mm_(ps[:, 2 * (b % 2) + s, :], y[:, kk % NM, b * P:(b + 1) * P],
                                       wout[:, kk, s * HALF:(s + 1) * HALF], start=(kk == 0), stop=(kk == KD - 1))
                    last.then_inc(op_done, 1)
                if b >= 2:
                    bb = b - 2
                    pe.wait_ge(xt2_evac, bb + 1)
                    if bb >= 2:
                        pe.wait_ge(logits_ready, bb - 1)
                    for kk in range(KD):
                        last = mm_(ps[:, 6 + bb % 2, 0:NR], hn2T[:, bb % 2, kk, :], wr[:, kk, :],
                                   start=(kk == 0), stop=(kk == KD - 1))
                    last.then_inc(r_done, 1)
                if 1 <= b <= NB:
                    bb = b - 1
                    pe.wait_ge(hn2_ready, bb + 1)
                    if bb >= 1:
                        pe.wait_ge(xt2_evac, bb)
                    for kk in range(KD):
                        last = tr(ps[:, 4 + kk // 4, kk % 4 * P:(kk % 4 + 1) * P], hn2[:, bb % 2, kk * P:(kk + 1) * P], ident[:])
                    last.then_inc(xt2_done, 1)
            pe.wait_ge(mask_ready, 1)
            pe.wait_ge(h_ready, NB)
            mm_(ps[:, 0, 0:NB * NE], upper[:], msum[:].rearrange("p b e -> p (b e)"), start=True, stop=False)
            mm_(ps[:, 0, 0:NB * NE], ones[:], mcum[:].rearrange("p b e -> p (b e)"), start=False, stop=True).then_inc(prefix_done, 1)
            mm_(ps[:, 1, 0:NE], ones[:], mtot[:], start=True, stop=True).then_inc(prefix_done, 1)
            for j in range(2 * NB):
                jj = j % 2
                pe.wait_ge(list_operands, j + 1)
                mm_(ps[:, 2, 0:64], lrow[:, jj, :], lval[:, jj, :, :].rearrange("p a n -> p (a n)"),
                    start=(j == 0), stop=(j == 2 * NB - 1)).then_inc(list_mm, 1)
            pe.wait_ge(lists_ready, 1)
            nt = pe.value_load(tiles_i[0:1, NE:NE + 1], min_val=NE, max_val=MAX_TILES)

            def rows_transposed():
                for kk in range(KD):
                    last = tr(ps[:, 2 + kk // 4, kk % 4 * P:(kk % 4 + 1) * P], xg[:, kk * P:(kk + 1) * P], ident[:])
                last.then_inc(mxt_done, 1)

            pe.wait_ge(gathered, 16)
            rows_transposed()
            with pe.Fori(0, nt) as g:
                landed = pe.value_load(texp_i[0:1, bass.ds(g, 1)], min_val=0, max_val=NE - 1) * 16 + 16
                pe.wait_ge(mxt_evac, g + 1)
                for bank, w, done, s0 in ((0, wg, gate_done, 0), (1, wu, up_done, 2)):
                    for kk in range(KD):
                        if kk % (KD // 2) == 0:
                            pe.wait_ge(we_landed[s0 + kk // (KD // 2)], landed)
                        last = mm_(ps[:, bank, :], xT[:, kk, :], w[:, kk, :], start=(kk == 0), stop=(kk == KD - 1))
                    last.then_inc(done, 1)
                pe.wait_ge(gathered, g * 16 + 32)
                rows_transposed()
                pe.wait_ge(hid_ready, g + 1)
                for f in range(KE):
                    last = tr(ps[:, 6, f * P:(f + 1) * P], hid[:, f * P:(f + 1) * P], ident[:])
                last.then_inc(ht_done, 1)
                pe.wait_ge(ht_evac, g + 1)
                for s in range(2):
                    for f in range(KE):
                        if s == 0 and f % (KE // 2) == 0:
                            pe.wait_ge(we_landed[4 + f // (KE // 2)], landed)
                        last = mm_(ps[:, 4 + s, :], hT[:, f, :], wd[:, f, s * HALF:(s + 1) * HALF],
                                   start=(f == 0), stop=(f == KE - 1))
                last.then_inc(y_done, 1)


_NAMES = ['x', 'norm1_g', 'w_in', 'conv_w', 'conv_b', 'w_gate_a', 'b_gate_a', 'w_gate_x', 'b_gate_x',
          'lru_lambda', 'lru_out_g', 'q_norm_g', 'k_norm_g', 'lambda_q1', 'lambda_k1', 'lambda_q2', 'lambda_k2',
          'sub_norm_g', 'w_out', 'norm2_g', 'w_router_group', 'b_router_group', 'w_router_expert',
          'b_router_expert', 'w_expert_gate', 'w_expert_up', 'w_expert_down']


def kernel(**inputs):
    import numpy as _np
    import concourse.bacc as _bacc
    from concourse import mybir as _mybir
    from concourse.bass_utils import run_bass_kernel_spmd as _run

    nc = _bacc.Bacc("TRN2", target_bir_lowering=False, num_devices=1)
    arrays, args = {}, []
    for name in _NAMES:
        a = _np.ascontiguousarray(inputs[name])
        arrays[f"in_{name}"] = a
        args.append(nc.dram_tensor(f"in_{name}", a.shape, _mybir.dt.from_np(a.dtype), kind="ExternalInput").ap())
    _, T, D = inputs['x'].shape
    out = nc.dram_tensor("out_rows", (T + 128, D), _mybir.dt.float32, kind="ExternalOutput").ap()
    hn2 = nc.dram_tensor("hn2_rows", (T + 128, D), _mybir.dt.float32, kind="Internal").ap()
    build_block(nc, *args, out, hn2)
    res = _run(nc, [arrays], core_ids=[0])
    return res.results[0]["out_rows"][:T].reshape(1, T, D)
```

```python
import math
from contextlib import ExitStack

import concourse.bass as bass
from concourse import mybir

F32 = mybir.dt.float32
F32R = mybir.dt.float32r
U32 = mybir.dt.uint32
I32 = mybir.dt.int32
ALU = mybir.AluOpType
ACT = mybir.ActivationFunctionType
AX = mybir.AxisListType

P = 128
EPS = 1e-6
NEG_BIG = -1e30
LAMBDA_INIT = 0.8 - 0.6 * math.exp(-0.3 * 0)
LRU_C = 8.0
CHUNK = 64


def build_block(nc, x, norm1_g, w_in, conv_w, conv_b, w_gate_a, b_gate_a, w_gate_x, b_gate_x,
                lru_lambda, lru_out_g, q_norm_g, k_norm_g, lambda_q1, lambda_k1, lambda_q2, lambda_k2,
                sub_norm_g, w_out, norm2_g, w_router_group, b_router_group, w_router_expert,
                b_router_expert, w_expert_gate, w_expert_up, w_expert_down, out, hn2_dram):
    T, D = x.shape[1], x.shape[2]
    NB = T // P
    KD = D // P
    NG, EPG = b_router_expert.shape[1], b_router_expert.shape[2]
    NE = NG * EPG
    DE = w_expert_gate.shape[3]
    KE = DE // P
    HALF = 512
    NM = 4
    HD = q_norm_g.shape[1]
    NR = NG + NG * EPG
    MAX_TILES = NE + (2 * T - NE) // P
    LIST = MAX_TILES + 1
    RING = 4
    assert D == 1024 and T == 1024 and NM * P == 512 and DE == HALF and LIST <= 32

    BASE = 16512
    used = {}

    def at(name, word, shape, dt=F32):
        n = 1
        for s in shape[1:]:
            n *= s
        used[name] = (word, word + n)
        assert BASE + 4 * (word + n) <= nc.sbuf_usable_end, name
        return nc.alloc_sbuf_tensor_at(name, shape, dt, offset=BASE + 4 * word)

    A0 = 0
    A1 = A0 + 2 * KD * T
    A2 = A1 + 4112 + 8192
    A3 = A2 + 5 * 4096
    A4 = A3 + 2048
    hnTh = at("hnTh", A0, [P, KD, T], F32R)
    hnTl = at("hnTl", A0 + 8192, [P, KD, T], F32R)
    XW = 4 + T
    xlp = at("xlp", A1, [P, 2, XW])
    a2 = at("a2", A1 + 2 * XW, [P, 2, T])
    v = at("v", A1, [P, NB, 512])
    q = at("q", A1 + 4112, [P, NM, T])
    k = at("k", A1 + 4112 + 4096, [P, NM, T])
    xs = at("xs", A1 + 4112, [P, 2, D])
    g1b = at("g1b", A1 + 4112 + 2048, [P, D])
    gg = at("gg", A2, [P, NM, T])
    wraw = at("wraw", A2 + 4096, [P, 2, KD, P])
    wih = at("wih", A2 + 6144, [P, RING, KD, P], F32R)
    wil = at("wil", A2 + 10240, [P, RING, KD, P], F32R)
    xc = at("xc", A2 + 14336, [P, 2, T])
    r = at("r", A2 + 16384, [P, T])
    ig = at("ig", A2 + 17408, [P, T])
    th = at("th", A2 + 18432, [P, 2, T])
    sq = at("sq", A3, [P, 2, HALF])
    rt = at("rt", A3 + 1024, [P, 2, HALF])
    yr = at("yr", A3, [P, T])
    junk = at("junk", A3, [P, D])
    qz = at("qz", A2 + 16384, [P, 2, 2, T])
    pr = at("pr", A0 + 4096, [P, 3, 2, T])
    wT = at("wT", A0 + 10240, [P, 2, T])
    nd = at("nd", A2 + 14336, [P, T])
    ndt = at("ndt", A2 + 15360, [P, T])
    osb = at("osb", A0 + 12288, [P, 2, NB, P])
    osq = at("osq", A0 + 14336, [P, NB, P])
    yatt = at("yatt", A0, [P, NM, T])
    wout = at("wout", A2 + 4096, [P, KD, D])
    xr = at("xr", A3, [P, 2, D])
    g2b = at("g2b", A2 + 12288, [P, D])
    wr = at("wr", A2 + 13312, [P, KD, NR])
    h = at("h", A0 + 4096, [P, 2, D])
    hn2 = at("hn2", A0 + 6144, [P, 2, D])
    hn2T = at("hn2T", A0 + 8192, [P, 2, KD, P])
    junk2 = at("junk2", A2 + 14336, [P, D])
    rc = [A0 + 12288]

    def route(name, shape, dt=F32):
        n = 1
        for s in shape[1:]:
            n *= s
        t = at(name, rc[0], shape, dt)
        rc[0] += (n + 7) // 8 * 8
        assert rc[0] <= A0 + 15360
        return t

    upper = route("upper", [P, P])
    iota_row = route("iota_row", [P, P])
    tok1 = route("tok1", [P, NB])
    pad1 = route("pad1", [P, 32])
    ohg, gexp = route("ohg", [P, NB, NG]), route("gexp", [P, NB, NG])
    sel, stmp = route("sel", [P, NB, EPG]), route("stmp", [P, NB, EPG])
    oh1, oh2 = route("oh1", [P, NB, EPG]), route("oh2", [P, NB, EPG])
    gtop, etop1, etop2, free = (route(f"top{j}", [P, NB]) for j in range(4))
    edif, esum, gsum = (route(f"e{j}", [P, NB]) for j in range(3))
    mm = route("mm", [P, 2, NB, NE])
    msum, mcum = route("msum", [P, NB, NE]), route("mcum", [P, NB, NE])
    mtot = route("mtot", [P, NE])
    gates = route("gates", [P, 2, NB])
    cnt, ntile, texcl = route("cnt", [P, NE]), route("ntile", [P, NE]), route("texcl", [P, NE])
    tincl = route("tincl", [P, NE + 2])
    slotm, stmp2 = route("slotm", [P, NB, NE]), route("stmp2", [P, NB, NE])
    slot, srow, scol = (route(f"slot{j}", [P, 2, NB]) for j in range(3))
    slot_i, srow_i, scol_i = (route(f"sloti{j}", [P, 2, NB], I32) for j in range(3))
    lrow = route("lrow", [P, 2, P])
    lval = route("lval", [P, 2, 2, 32])
    tcmp = route("tcmp", [P, 33, NE])
    texp = route("texp", [P, 33])
    tchg = route("tchg", [P, 33])
    lemp = route("lemp", [P, 32])
    NC = 4
    KC = KD // NC
    raw = at("raw", A1, [P, 3, NC, KC * DE])
    split_at = [A2 + 16384, A2 + 18432, A0 + 10240] + [A2 + 2048 * n for n in range(8)] + [A0 + 4096]
    whi = [at(f"whi{n}", split_at[n], [P, KC, DE], F32R) for n in range(3 * NC)]
    wlo = [at(f"wlo{n}", split_at[n] + 1024, [P, KC, DE], F32R) for n in range(3 * NC)]
    xg = at("xg", A0, [P, D])
    xTh = at("xTh", A0 + 1024, [P, KD, P], F32R)
    xTl = at("xTl", A0 + 2048, [P, KD, P], F32R)
    sil = at("sil", A0 + 3072, [P, DE])
    hid = at("hid", A0 + 3584, [P, DE])
    hTh = at("hTh", A0 + 6144, [P, KE, P], F32R)
    hTl = at("hTl", A0 + 6656, [P, KE, P], F32R)
    ysb = at("ysb", A0 + 15360, [P, D])
    c = [A4]

    def const(name, shape, dt=F32):
        n = 1
        for s in shape[1:]:
            n *= s
        t = at(name, c[0], shape, dt)
        c[0] += (n + 7) // 8 * 8
        return t

    ident = const("ident", [P, P])
    ones_blk = const("ones_blk", [P, P])
    ones = const("ones", [P, P])
    bd = at("bd", A1 + 4112 + 4096, [P, 2, NM, P])
    vrow = at("vrow", A1 + 4112 + 6144, [P, P])
    NV = 39
    vc = const("vc", [P, 40])
    CW, CB, BA, BX, LAM, LG, QG, KG, SG = 0, 16, 20, 24, 28, 32, 36, 37, 38
    br = const("br", [P, NR])
    eps = const("eps", [P, 1])
    ss = const("ss", [P, NB])
    rs = const("rs", [P, NB])
    sp = const("sp", [P, 8, NM])
    qgh = const("qgh", [P, NM])
    lamv = at("lamv", A1 + 4112 + 6272, [P, 4, HD])
    lams = const("lams", [P, 8])
    mx = const("mx", [P, NB * NM, 2])
    nb = const("nb", [P, NB * NM, 2])
    sm = const("sm", [P, NB * NM, 2])
    ri = const("ri", [P, NB * NM, 2])
    ra = const("ra", [P, NB * NM])
    oss = const("oss", [P, 2, NB])
    phalf = const("phalf", [P, NB])
    lg = const("lg", [P, NB, NR])
    ltok = const("ltok", [P, 32])
    lgate = const("lgate", [P, 32])
    tiles_i = const("tiles_i", [P, NE + 2], I32)
    texp_i = const("texp_i", [P, 33], I32)
    tlast_i = const("tlast_i", [P, 32], I32)
    tfirst_i = const("tfirst_i", [P, 32], I32)
    idx_g = const("idx_g", [P, 2], U32)
    idx_s = const("idx_s", [P, 2], U32)
    gcol = const("gcol", [P, 2])

    ps = nc.alloc_psum_tensor("ps", [P, 8, HALF], F32)
    xT_ps = ps[:, 2:4, :].rearrange("p a n -> p (a n)")
    y_ps = ps[:, 4:6, :].rearrange("p a n -> p (a n)")

    with ExitStack() as ctx:
        def sem(name):
            return ctx.enter_context(nc.semaphore(name))

        consts_built = sem("consts_built")
        vec_landed = sem("vec_landed")
        bd_landed = sem("bd_landed")
        bcast_landed = sem("bcast_landed")
        br_landed = sem("br_landed")
        g1_landed = sem("g1_landed")
        x_landed = [sem(f"x_landed{i}") for i in range(2)]
        w_landed = [sem(f"w_landed{i}") for i in range(2)]
        w_high = sem("w_high")
        w_low = sem("w_low")
        x_rms = sem("x_rms")
        hn_ready = sem("hn_ready")
        hn_transposed = sem("hn_transposed")
        hnT_act = sem("hnT_act")
        hnT_dve = sem("hnT_dve")
        act_seq = sem("act_seq")
        dve_seq = sem("dve_seq")
        pool_seq = sem("pool_seq")
        vec_transposed = sem("vec_transposed")
        vec_ready = sem("vec_ready")
        lam_y = sem("lam_y")
        sp_ready = sem("sp_ready")
        lam_dots = sem("lam_dots")
        lam_exp = sem("lam_exp")
        group_done = sem("group_done")
        lru_evac = sem("lru_evac")
        conv_done = sem("conv_done")
        gate_mm = sem("gate_mm")
        gate_sig = sem("gate_sig")
        lru_exp = sem("lru_exp")
        om_ready = sem("om_ready")
        om_sqrt = sem("om_sqrt")
        y_lru = sem("y_lru")
        y_sq = sem("y_sq")
        y_norm_mm = sem("y_norm_mm")
        nd_raw = sem("nd_raw")
        y_rms = sem("y_rms")
        lru_ready = sem("lru_ready")
        qk_sq = sem("qk_sq")
        qk_mm = sem("qk_mm")
        qk_rms = sem("qk_rms")
        qk_done = sem("qk_done")
        v_evac = sem("v_evac")
        qz_ready = sem("qz_ready")
        qz_zeroed = sem("qz_zeroed")
        s_done = sem("s_done")
        s_biased = sem("s_biased")
        s_nmax = sem("s_nmax")
        p_ready = sem("p_ready")
        w_ready = sem("w_ready")
        t_done = sem("t_done")
        t_evac = sem("t_evac")
        pv_done = sem("pv_done")
        o_evac = sem("o_evac")
        o_ms = sem("o_ms")
        o_pow = sem("o_pow")
        o_normed = sem("o_normed")
        wout_landed = sem("wout_landed")
        xr_landed = [sem(f"xr_landed{i}") for i in range(2)]
        op_done = sem("op_done")
        h_ready = sem("h_ready")
        h_rms = sem("h_rms")
        hn2_ready = sem("hn2_ready")
        h_stored = [sem(f"h_stored{i}") for i in range(2)]
        hn2_stored = [sem(f"hn2_stored{i}") for i in range(2)]
        pad_ready = sem("pad_ready")
        pad_stored = sem("pad_stored")
        xt2_done = sem("xt2_done")
        xt2_evac = sem("xt2_evac")
        r_done = sem("r_done")
        logits_ready = sem("logits_ready")
        route_const = sem("route_const")
        route_max = sem("route_max")
        route_exp = sem("route_exp")
        mask_ready = sem("mask_ready")
        prefix_done = sem("prefix_done")
        list_operands = sem("list_operands")
        list_mm = sem("list_mm")
        lists_ready = sem("lists_ready")
        we_landed = [[sem(f"we_landed{j}_{i}") for i in range(NC)] for j in range(3)]
        hi_ready = [sem(f"hi_ready{j}") for j in range(3)]
        lo_ready = [sem(f"lo_ready{j}") for j in range(3)]
        part_used = [sem(f"part_used{j}") for j in range(3)]
        hT_lo = sem("hT_lo")
        mxT_lo = sem("mxT_lo")
        gather_index = sem("gather_index")
        gathered = sem("gathered")
        scatter_index = sem("scatter_index")
        scattered = sem("scattered")
        sil_ready = sem("sil_ready")
        hid_ready = sem("hid_ready")
        mxt_done = sem("mxt_done")
        mxt_evac = sem("mxt_evac")
        ht_done = sem("ht_done")
        ht_evac = sem("ht_evac")
        y_done = sem("y_done")
        gcol_ready = sem("gcol_ready")
        y_ready = sem("y_ready")

        NI = NM * NB
        slope = [2.0 ** (-8.0 * (hh + 1) / NM) for hh in range(NM)]

        ORDER = [7, 0, 6, 1, 5, 2, 4, 3]

        def item(t):
            return t // NB, ORDER[t % NB]

        Y_AT = 6
        tslots = []
        for t in range(NI):
            tslots.append(("w", t))
            if t % NB == Y_AT and t >= NB:
                tslots.append(("y", t // NB - 1))
        tslots.append(("y", NM - 1))
        tpos = {s: n for n, s in enumerate(tslots)}

        def unit_columns(u):
            return (u % 2 * NM + u // 2) * P if u < 2 * NM else u * P

        W_EXPERTS = (w_expert_gate, w_expert_up, w_expert_down)

        def part_of(j, c, e):
            rows = (KD, KD, KE)[j] * P // NC
            return W_EXPERTS[j][0, e, c * rows:(c + 1) * rows, :]

        block = ctx.enter_context(nc.Block())

        @block.sync
        def _(sp_):
            def load_unit(u):
                if u >= 2:
                    sp_.wait_ge(w_low, u - 1)
                sp_.dma_start(wraw[:, u % 2, :, :],
                              w_in[0, :, unit_columns(u):unit_columns(u) + P]
                              .rearrange("(k p) n -> p k n", p=P)).then_inc(w_landed[u % 2], 16)

            for b in range(NB):
                if b >= 2:
                    sp_.wait_ge(hn_transposed, b - 1)
                sp_.dma_start(xs[:, b % 2, :], x[0, b * P:(b + 1) * P, :]).then_inc(x_landed[b % 2], 16)
                if b in (1, 2):
                    load_unit(b - 1)
            for u in range(2, 5 * NM):
                load_unit(u)
            sp_.wait_ge(group_done, 5 * NB)
            sp_.dma_start(wout[:, :, :], w_out[0].rearrange("(k p) n -> p k n", p=P)).then_inc(wout_landed, 16)
            sp_.dma_start(wr[:, :, 0:NG], w_router_group[0].rearrange("(k p) n -> p k n", p=P)).then_inc(wout_landed, 16)
            for gq in range(NG):
                sp_.dma_start(wr[:, :, NG + gq * EPG:NG + (gq + 1) * EPG],
                              w_router_expert[0, gq].rearrange("(k p) n -> p k n", p=P)).then_inc(wout_landed, 16)
            sp_.dma_start(g2b[:, :], norm2_g.to_broadcast([P, D])).then_inc(wout_landed, 16)
            sp_.wait_ge(lru_ready, NM)
            for b in range(2):
                sp_.dma_start(xr[:, b, :], x[0, b * P:(b + 1) * P, :]).then_inc(xr_landed[b], 16)
            sp_.wait_ge(pv_done, NI)
            for j in range(3):
                for c in range(NC):
                    sp_.dma_start(raw[:, j, c, :].rearrange("p (k n) -> p k n", n=(DE, DE, D)[j]),
                                  part_of(j, c, 0).rearrange("(k p) n -> p k n", p=P)).then_inc(we_landed[j][c], 16)
            sp_.wait_ge(pad_ready, 1)
            sp_.dma_start(hn2_dram[T:T + P, :], ysb[:, :]).then_inc(pad_stored, 16)
            for b in range(NB):
                sp_.wait_ge(h_ready, b + 1)
                sp_.dma_start(out[b * P:(b + 1) * P, :], h[:, b % 2, :]).then_inc(h_stored[b % 2], 16)
                if b + 2 < NB:
                    sp_.dma_start(xr[:, b % 2, :], x[0, (b + 2) * P:(b + 3) * P, :]).then_inc(xr_landed[b % 2], 16)
                sp_.wait_ge(hn2_ready, b + 1)
                sp_.dma_start(hn2_dram[b * P:(b + 1) * P, :], hn2[:, b % 2, :]).then_inc(hn2_stored[b % 2], 16)
            with sp_.Fori(1, NE) as e:
                for j in range(3):
                    for c in range(NC):
                        sp_.wait_ge(lo_ready[j], e * NC + (c + 1 - NC))
                        sp_.dma_start(raw[:, j, c, :].rearrange("p (k n) -> p k n", n=(DE, DE, D)[j]),
                                      part_of(j, c, bass.ds(e, 1)).rearrange("o (k p) n -> p (o k) n", p=P)
                                      ).then_inc(we_landed[j][c], 16)
            for j in range(3):
                for c in range(NC):
                    sp_.wait_ge(we_landed[j][c], 16 * NE)

        @block.gpsimd
        def _(pool):
            n = [0]

            def step(ins):
                n[0] += 1
                ins.then_inc(pool_seq, 1)
                pool.wait_ge(pool_seq, n[0])

            step(nc.gpsimd.memset(ident[:], 0.0))
            step(nc.gpsimd.memset(eps[:], EPS))
            step(nc.gpsimd.affine_select(out=ident[:], in_=ident[:], compare_op=ALU.not_equal, fill=1.0,
                                         base=0, pattern=[[-1, P]], channel_multiplier=1))
            step(nc.gpsimd.memset(ones[:], 1.0))
            step(nc.gpsimd.memset(ones_blk[:], 0.0))
            step(nc.gpsimd.memset(ones_blk[0:64, 0:64], 1.0))
            step(nc.gpsimd.memset(ones_blk[64:128, 64:128], 1.0))
            step(nc.gpsimd.memset(phalf[:], -0.5))
            nc.gpsimd.memset(bd[:], 0.0).then_inc(consts_built, 1)
            pool.wait_ge(y_norm_mm, 2 * NM)
            nc.gpsimd.iota(ndt[:], pattern=[[-1, T]], base=T - P, channel_multiplier=1,
                           allow_small_or_imprecise_dtypes=True).then_inc(nd_raw, 1)
            pool.wait_ge(nd_raw, 1)
            nc.gpsimd.memset(qz[:], 0.0).then_inc(qz_zeroed, 1)
            pool.wait_ge(qz_zeroed, 1)
            for hh in range(NM):
                pool.wait_ge(o_ms, hh + 1)
                nc.gpsimd.tensor_tensor(oss[:, hh % 2, :], oss[:, hh % 2, :], phalf[:], ALU.pow).then_inc(o_pow, 1)
                pool.wait_ge(o_pow, hh + 1)
            nc.gpsimd.memset(ysb[:], 0.0).then_inc(pad_ready, 1)
            pool.wait_ge(pad_ready, 1)
            pool.dma_start(out[T:T + P, :], ysb[:, :]).then_inc(scattered, 16)
            pool.wait_ge(t_done, len(tslots))
            step(nc.gpsimd.memset(upper[:], 1.0))
            step(nc.gpsimd.affine_select(out=upper[:], in_=upper[:], compare_op=ALU.is_gt, fill=0.0,
                                         base=0, pattern=[[1, P]], channel_multiplier=-1))
            step(nc.gpsimd.iota(iota_row[:], pattern=[[1, P]], base=0, channel_multiplier=0,
                                allow_small_or_imprecise_dtypes=True))
            step(nc.gpsimd.iota(tok1[:], pattern=[[P, NB]], base=1, channel_multiplier=1,
                                allow_small_or_imprecise_dtypes=True))
            nc.gpsimd.iota(pad1[:], pattern=[[0, 32]], base=T, channel_multiplier=1,
                           allow_small_or_imprecise_dtypes=True).then_inc(route_const, 1)
            for b in range(2):
                pool.wait_ge(hn2_stored[b], 16 * NB // 2)
                pool.wait_ge(h_stored[b], 16 * NB // 2)
            pool.wait_ge(pad_stored, 16)
            pool.wait_ge(scattered, 16)
            pool.wait_ge(lists_ready, 1)
            nt1 = pool.value_load(tiles_i[0:1, NE + 1:NE + 2], min_val=NE - 1, max_val=MAX_TILES - 1)

            def gather():
                nc.gpsimd.indirect_dma_start(
                    out=xg[:], out_offset=None, in_=hn2_dram,
                    in_offset=bass.IndirectOffsetOnAxis(ap=idx_g[:, 0:1], axis=0)).then_inc(gathered, 16)

            step(nc.gpsimd.tensor_copy(idx_g[:, 0:1], ltok[:, 0:1]))
            gather()

            def next_rows(g):
                pool.wait_ge(mxt_done, g)
                nc.gpsimd.tensor_copy(idx_g[:, 0:1], ltok[:, bass.ds(g, 1)]).then_inc(gather_index, 1)
                pool.wait_ge(lists_ready, 1)
                pool.wait_ge(gather_index, g)
                gather()

            def add_rows(g):
                pool.wait_ge(scattered, g * 16)
                nc.gpsimd.tensor_copy(idx_s[:, 0:1], ltok[:, bass.ds(g - 1, 1)]).then_inc(scatter_index, 1)
                pool.wait_ge(lists_ready, 1)
                pool.wait_ge(scatter_index, g)
                pool.wait_ge(y_ready, g)
                nc.gpsimd.indirect_dma_start(
                    out=out, out_offset=bass.IndirectOffsetOnAxis(ap=idx_s[:, 0:1], axis=0),
                    in_=ysb[:], in_offset=None, compute_op=ALU.add).then_inc(scattered, 16)

            pool.wait_ge(mxt_done, 1)
            nc.gpsimd.tensor_copy(idx_g[:, 0:1], ltok[:, 1:2]).then_inc(gather_index, 1)
            pool.wait_ge(gather_index, 1)
            gather()
            next_rows(2)
            with pool.Fori(1, nt1) as g:
                next_rows(g + 2)
                add_rows(g)
            add_rows(nt1)
            add_rows(nt1 + 1)
            pool.wait_ge(scattered, nt1 * 16 + 32)
            pool.wait_ge(gathered, nt1 * 16 + 32)

        @block.scalar
        def _(act):
            n = [0]

            def step(ins):
                n[0] += 1
                ins.then_inc(act_seq, 1)
                act.wait_ge(act_seq, n[0])

            A = nc.scalar.activation
            vrows = [(conv_w[0].rearrange("j (m c) -> (j m) c", c=P), CW, 4 * NM)]
            for ap, row in ((conv_b, CB), (b_gate_a, BA), (b_gate_x, BX), (lru_lambda, LAM), (lru_out_g, LG)):
                vrows.append((ap[0].rearrange("(m c) -> m c", c=P), row, NM))
            vrows.append((sub_norm_g, SG, 1))
            nvec = 0
            for src, row, cnt in vrows:
                act.dma_start(vrow[row:row + cnt, :], src).then_inc(vec_landed, 16)
                nvec += 16
            for src, row in ((q_norm_g, QG), (k_norm_g, KG)):
                for s in range(2):
                    act.dma_start(vrow[row:row + 1, s * HD:(s + 1) * HD], src).then_inc(vec_landed, 16)
                    nvec += 16
            for j, src in enumerate((lambda_q1, lambda_k1, lambda_q2, lambda_k2)):
                act.dma_start(lamv[:, j, :], src.to_broadcast([P, HD])).then_inc(bcast_landed, 16)
            act.dma_start(g1b[:, :], norm1_g.to_broadcast([P, D])).then_inc(g1_landed, 16)
            act.wait_ge(consts_built, 1)
            for gi, src in enumerate((w_gate_a, w_gate_x)):
                for s in range(2):
                    act.dma_start(bd[64 * s:64 * s + 64, gi, :, 64 * s:64 * s + 64],
                                  src[0].rearrange("(m two) c d -> two c m d", two=2)[s]).then_inc(bd_landed, 16)
            act.dma_start(br[:, 0:NG], b_router_group.to_broadcast([P, NG])).then_inc(br_landed, 16)
            act.dma_start(br[:, NG:NR], b_router_expert.rearrange("a g e -> a (g e)").to_broadcast([P, NE])).then_inc(br_landed, 16)

            def unit_high(u):
                act.wait_ge(w_landed[u % 2], 16 * (u // 2 + 1))
                if u >= RING:
                    act.wait_ge(group_done, 2 * (u - RING) + 2)
                A(wih[:, u % RING, :, :], wraw[:, u % 2, :, :], ACT.Copy).then_inc(w_high, 1)

            for b in range(NB + 1):
                if b < NB:
                    act.wait_ge(x_landed[b % 2], 16 * (b // 2 + 1))
                    step(A(junk[:], xs[:, b % 2, :], ACT.Square, accum_out=ss[:, b:b + 1]))
                    A(ss[:, b:b + 1], ss[:, b:b + 1], ACT.Sqrt, scale=1.0 / D, bias=eps[:, 0:1]).then_inc(x_rms, 1)
                if b >= 1:
                    bb = b - 1
                    act.wait_ge(hn_transposed, bb + 1)
                    A(hnTh[:, :, bb * P:(bb + 1) * P], ps[:, 2 * (bb % 2):2 * (bb % 2) + 2, :]
                      .rearrange("p a (k n) -> p (a k) n", n=P), ACT.Copy).then_inc(hnT_act, 1)
                if b >= NB - 2:
                    unit_high(b - NB + 2)
            act.wait_ge(vec_ready, 1)
            step(A(sp[:, 0, :], vc[:, LAM:LAM + NM], ACT.Abs))
            A(sp[:, 1, :], sp[:, 0, :], ACT.Exp, scale=-1.0).then_inc(lam_y, 1)
            act.wait_ge(lam_dots, 2)
            A(lams[:, 2:4], lams[:, 0:2], ACT.Exp).then_inc(lam_exp, 1)
            act.wait_ge(sp_ready, 1)
            for u in range(4 * NM + 1):
                if u >= 1:
                    unit_high(u + 2)
                if u == 4 * NM:
                    unit_high(u + 3)
                if u < 2 * NM:
                    m = u // 2
                    for s in range(2):
                        act.wait_ge(group_done, 2 * u + s + 1)
                        if u % 2 == 0:
                            if m >= 2:
                                act.wait_ge(conv_done, m - 1)
                            A(xlp[:, m % 2, 3 + s * HALF:3 + (s + 1) * HALF], ps[:, (2 * u + s) % 4, :], ACT.Copy).then_inc(lru_evac, 1)
                        else:
                            A(gg[:, m, s * HALF:(s + 1) * HALF], ps[:, (2 * u + s) % 4, :], ACT.Gelu_apprx_tanh).then_inc(lru_evac, 1)
                else:
                    for j in (2 * u - 4 * NM, 2 * u - 4 * NM + 1):
                        g = 4 * NM + j
                        if j < 4 * NM:
                            act.wait_ge(group_done, g + 1)
                            if j >= 2:
                                act.wait_ge(qk_mm, j - 1)
                            A(sq[:, j % 2, :], ps[:, g % 4, :], ACT.Square).then_inc(qk_sq, 1)
                        if 1 <= j <= 4 * NM:
                            jj = j - 1
                            act.wait_ge(qk_mm, jj + 1)
                            if jj >= 2:
                                act.wait_ge(qk_done, jj - 1)
                            A(rt[:, jj % 2, :], ps[:, 4 + jj % 2, :], ACT.Sqrt, scale=1.0 / HD, bias=eps[:, 0:1]).then_inc(qk_rms, 1)
                if u % 2 == 0 and 2 <= u <= 2 * NM:
                    m = u // 2 - 1
                    for j in range(4 * m, 4 * m + 4):
                        gi, s = j // 2 % 2, j % 2
                        act.wait_ge(gate_mm, j + 1)
                        if m >= 1:
                            act.wait_ge(y_lru, m)
                        A((r, ig)[gi][:, s * HALF:(s + 1) * HALF], ps[:, 6 + j % 2, :], ACT.Sigmoid,
                          bias=vc[:, (BA, BX)[gi] + m:(BA, BX)[gi] + m + 1]).then_inc(gate_sig, 1)
                    act.wait_ge(gate_sig, 4 * m + 4)
                    A(a2[:, m % 2, :], r[:], ACT.Exp, scale=sp[:, 5, m:m + 1]).then_inc(lru_exp, 1)
                    A(th[:, m % 2, :], r[:], ACT.Tanh, scale=sp[:, 6, m:m + 1]).then_inc(lru_exp, 1)
                    act.wait_ge(lru_exp, 3 * m + 2)
                    A(r[:], r[:], ACT.Exp, scale=sp[:, 4, m:m + 1]).then_inc(lru_exp, 1)
                    act.wait_ge(om_ready, m + 1)
                    A(th[:, m % 2, :], th[:, m % 2, :], ACT.Sqrt).then_inc(om_sqrt, 1)
            for m in range(NM):
                act.wait_ge(y_lru, m + 1)
                if m >= 2:
                    act.wait_ge(y_norm_mm, 2 * m - 2)
                A(th[:, m % 2, :], gg[:, m, :], ACT.Square).then_inc(y_sq, 1)
            for b in range(NB):
                act.wait_ge(group_done, 8 * NM + b + 1)
                if b == 0:
                    act.wait_ge(om_ready, NM)
                A(v[:, b, :], ps[:, b % 4, :], ACT.Copy).then_inc(v_evac, 1)
                if b == 2:
                    act.wait_ge(y_norm_mm, 2 * NM)
                    for s in range(2):
                        A(yr[:, s * HALF:(s + 1) * HALF], ps[:, 6 + s, :], ACT.Sqrt, scale=1.0 / (NM * P), bias=eps[:, 0:1]).then_inc(y_rms, 1)
                    act.wait_ge(qk_done, 4 * NM)
                    act.wait_ge(qz_zeroed, 1)
                    for hh in range(2):
                        for cc in range(2):
                            sl = slice(64 * cc, 64 * cc + 64)
                            A(qz[sl, hh, cc, :], q[sl, hh, :], ACT.Copy).then_inc(qz_ready, 1)
            for t in range(NI + 3):
                if t < NI:
                    hh, i = item(t)
                    w = P * (i + 1)
                    if t % NB == 1 and 1 <= hh < NM - 1:
                        act.wait_ge(s_done, 2 * NB * hh)
                        for cc in range(2):
                            sl = slice(64 * cc, 64 * cc + 64)
                            A(qz[sl, (hh + 1) % 2, cc, :], q[sl, hh + 1, :], ACT.Copy).then_inc(qz_ready, 1)
                    act.wait_ge(s_nmax, t + 1)
                    for cc in range(2):
                        A(pr[:, t % 3, cc, 0:w], pr[:, t % 3, cc, 0:w], ACT.Exp, scale=slope[hh],
                          bias=nb[:, t, cc:cc + 1], accum_out=sm[:, t, cc:cc + 1]).then_inc(p_ready, 1)
                for kind, tt in ((kd, tt) for kd, tt in tslots
                                 if (kd == "w" and tt == t - 2) or (kd == "y" and tt < NM - 1 and t - 2 == NB * (tt + 1) + Y_AT)
                                 or (kd == "y" and tt == NM - 1 and t == NI + 2)):
                    ti = tpos[(kind, tt)]
                    act.wait_ge(t_done, ti + 1)
                    src = ps[:, 4:6, :].rearrange("p a n -> p (a n)")
                    if kind == "w":
                        w = P * (item(tt)[1] + 1)
                        if tt >= 2:
                            act.wait_ge(pv_done, tt - 1)
                        A(wT[:, tt % 2, 0:w], src[:, 0:w], ACT.Copy).then_inc(t_evac, 1)
                    else:
                        A(yatt[:, tt, :], src, ACT.Copy, scale=lams[:, 6:7]).then_inc(t_evac, 1)
            for b in range(NB + 1):
                if b < NB:
                    act.wait_ge(h_ready, b + 1)
                    step(A(junk2[:], h[:, b % 2, :], ACT.Square, accum_out=ss[:, b:b + 1]))
                    A(ss[:, b:b + 1], ss[:, b:b + 1], ACT.Sqrt, scale=1.0 / D, bias=eps[:, 0:1]).then_inc(h_rms, 1)
                if b >= 1:
                    bb = b - 1
                    act.wait_ge(xt2_done, bb + 1)
                    if bb >= 2:
                        act.wait_ge(r_done, bb - 1)
                    A(hn2T[:, bb % 2, :, :], ps[:, 4:6, :].rearrange("p a (k n) -> p (a k) n", n=P), ACT.Copy).then_inc(xt2_evac, 1)
            act.wait_ge(route_max, 1)
            step(A(gexp[:], gexp[:], ACT.Exp))
            A(edif[:], edif[:], ACT.Exp).then_inc(route_exp, 1)
            def high(j, c, e, used):
                act.wait_ge(we_landed[j][c], e * 16 + 16)
                if used is not None:
                    act.wait_ge(part_used[j], used)
                A(whi[NC * j + c][:].rearrange("p k n -> p (k n)"), raw[:, j, c, :], ACT.Copy).then_inc(hi_ready[j], 1)

            act.wait_ge(op_done, NB)
            act.wait_ge(r_done, NB)
            for b in range(2):
                act.wait_ge(h_stored[b], 16 * NB // 2)
                act.wait_ge(hn2_stored[b], 16 * NB // 2)
            for j in range(3):
                for c in range(NC):
                    high(j, c, 0, None)
            act.wait_ge(lists_ready, 1)
            nt = act.value_load(tiles_i[0:1, NE:NE + 1], min_val=NE, max_val=MAX_TILES)

            def x_evac(count):
                act.wait_ge(mxt_done, count)
                A(xTh[:, :, :].rearrange("p k n -> p (k n)"), xT_ps, ACT.Copy).then_inc(mxt_evac, 1)

            def silu(g):
                act.wait_ge(part_used[0], g * NC + NC)
                A(sil[:], ps[:, 0, :], ACT.Silu).then_inc(sil_ready, 1)

            def h_evac(g):
                act.wait_ge(ht_done, g)
                A(hTh[:, :, :].rearrange("p k n -> p (k n)"), ps[:, 6, :], ACT.Copy).then_inc(ht_evac, 1)

            x_evac(1)
            silu(0)
            x_evac(2)
            with act.Fori(1, nt) as g:
                e = act.value_load(texp_i[0:1, bass.ds(g, 1)], min_val=0, max_val=NE - 1)
                last = act.value_load(tlast_i[0:1, bass.ds(g, 1)], min_val=0, max_val=1)
                first = act.value_load(tfirst_i[0:1, bass.ds(g, 1)], min_val=0, max_val=1)
                with act.If(last != 0):
                    for c in range(NC - 1):
                        high(0, c, e + 1, g * NC + (c + 1))
                    silu(g)
                    h_evac(g)
                    high(0, NC - 1, e + 1, g * NC + NC)
                    for c in range(NC - 1):
                        high(1, c, e + 1, g * NC + (c + 1))
                    x_evac(g + 2)
                    high(1, NC - 1, e + 1, g * NC + NC)
                with act.Else():
                    silu(g)
                    h_evac(g)
                    x_evac(g + 2)
                with act.If(first != 0):
                    for c in range(NC):
                        high(2, c, e, g * NC + (c + 1 - NC))
            h_evac(nt)

        @block.vector
        def _(dve):
            n = [0]
            V = nc.vector

            def step(ins):
                n[0] += 1
                ins.then_inc(dve_seq, 1)
                dve.wait_ge(dve_seq, n[0])

            def unit_low(u):
                dve.wait_ge(w_high, u + 1)
                V.tensor_tensor(wil[:, u % RING, :, :], wraw[:, u % 2, :, :], wih[:, u % RING, :, :].bitcast(F32),
                                ALU.subtract).then_inc(w_low, 1)

            step(V.memset(xlp[:, :, 0:3], 0.0))
            dve.wait_ge(g1_landed, 16)
            for b in range(NB + 1):
                if b < NB:
                    dve.wait_ge(x_rms, b + 1)
                    step(V.reciprocal(rs[:, b:b + 1], ss[:, b:b + 1]))
                    V.scalar_tensor_tensor(out=xs[:, b % 2, :], in0=xs[:, b % 2, :], scalar=rs[:, b:b + 1],
                                           in1=g1b[:], op0=ALU.mult, op1=ALU.mult).then_inc(hn_ready, 1)
                if b >= 1:
                    bb = b - 1
                    dve.wait_ge(hnT_act, bb + 1)
                    V.tensor_tensor(hnTl[:, :, bb * P:(bb + 1) * P], ps[:, 2 * (bb % 2):2 * (bb % 2) + 2, :]
                                    .rearrange("p a (k n) -> p (a k) n", n=P),
                                    hnTh[:, :, bb * P:(bb + 1) * P].bitcast(F32), ALU.subtract).then_inc(hnT_dve, 1)
                if b >= NB - 2:
                    unit_low(b - NB + 2)
            dve.wait_ge(vec_transposed, 1)
            step(V.tensor_copy(vc[:, 0:NV], ps[:, 7, 0:NV]))
            for hh in range(NM):
                step(V.tensor_scalar(qgh[:, hh:hh + 1], vc[:, QG:QG + 1], HD ** -0.5 / slope[hh], None, ALU.mult))
            V.tensor_scalar(lams[:, 6:7], vc[:, SG:SG + 1], 1.0 - LAMBDA_INIT, None, ALU.mult).then_inc(vec_ready, 1)
            dve.wait_ge(vec_ready, 1)
            dve.wait_ge(bcast_landed, 64)
            for j in range(2):
                V.tensor_tensor_reduce(out=lamv[:, 2 * j, :], in0=lamv[:, 2 * j, :], in1=lamv[:, 2 * j + 1, :], scale=1.0,
                                       scalar=0.0, op0=ALU.mult, op1=ALU.add, accum_out=lams[:, j:j + 1]).then_inc(lam_dots, 1)
            dve.wait_ge(lam_y, 1)
            y_, z_, z2, acc = sp[:, 1, :], sp[:, 2, :], sp[:, 3, :], sp[:, 7, :]
            step(V.tensor_scalar(z2, y_, 2.0, None, ALU.add))
            step(V.reciprocal(z2, z2))
            step(V.tensor_tensor(z_, y_, z2, ALU.mult))
            step(V.tensor_tensor(z2, z_, z_, ALU.mult))
            step(V.tensor_scalar(acc, z2, 1.0 / 17, 1.0 / 15, ALU.mult, ALU.add))
            for d in (13, 11, 9, 7, 5, 3, 1):
                step(V.tensor_tensor(acc, acc, z2, ALU.mult))
                step(V.tensor_scalar(acc, acc, 1.0 / d, None, ALU.add))
            step(V.tensor_tensor(acc, acc, z_, ALU.mult))
            step(V.tensor_scalar(z_, vc[:, LAM:LAM + NM], -1.0, 0.0, ALU.mult, ALU.max))
            step(V.scalar_tensor_tensor(out=acc, in0=acc, scalar=2.0, in1=z_, op0=ALU.mult, op1=ALU.add))
            step(V.tensor_scalar(sp[:, 4, :], acc, -LRU_C, None, ALU.mult))
            step(V.tensor_scalar(sp[:, 5, :], acc, -2.0 * LRU_C, None, ALU.mult))
            step(V.tensor_scalar(sp[:, 6, :], acc, LRU_C, None, ALU.mult))
            dve.wait_ge(lam_exp, 1)
            step(V.tensor_tensor(lams[:, 4:5], lams[:, 3:4], lams[:, 2:3], ALU.subtract))
            V.tensor_scalar(lams[:, 5:6], lams[:, 4:5], -LAMBDA_INIT, None, ALU.add).then_inc(sp_ready, 1)
            neg_lam = lams[:, 5:6]

            def conv(m):
                dve.wait_ge(lru_evac, 4 * m + 2)
                if m >= 2:
                    dve.wait_ge(gate_mm, 4 * m - 4)
                    dve.wait_ge(y_lru, m - 1)
                xp = xlp[:, m % 2, :]
                step(V.tensor_scalar(xc[:, m % 2, :], xp[:, 0:T], vc[:, CW + m:CW + m + 1],
                                     vc[:, CB + m:CB + m + 1], ALU.mult, ALU.add))
                for j in (1, 2, 3):
                    ins = V.scalar_tensor_tensor(out=xc[:, m % 2, :], in0=xp[:, j:j + T],
                                                 scalar=vc[:, CW + NM * j + m:CW + NM * j + m + 1],
                                                 in1=xc[:, m % 2, :], op0=ALU.mult, op1=ALU.add)
                    if j < 3:
                        step(ins)
                ins.then_inc(conv_done, 1)
                dve.wait_ge(conv_done, m + 1)

            for u in range(4 * NM + 1):
                if u >= 1:
                    unit_low(u + 2)
                if u == 4 * NM:
                    unit_low(u + 3)
                if u < 2 * NM and u % 2 == 0:
                    conv(u // 2)
                if u % 2 == 0 and 2 <= u <= 2 * NM:
                    m = u // 2 - 1
                    dve.wait_ge(gate_sig, 4 * m + 4)
                    step(V.tensor_tensor(ig[:], ig[:], xc[:, m % 2, :], ALU.mult))
                    dve.wait_ge(lru_exp, 3 * m + 2)
                    V.scalar_tensor_tensor(out=th[:, m % 2, :], in0=a2[:, m % 2, :], scalar=1.0, in1=th[:, m % 2, :],
                                           op0=ALU.add, op1=ALU.mult).then_inc(om_ready, 1)
                    dve.wait_ge(om_sqrt, m + 1)
                    step(V.tensor_tensor(ig[:], ig[:], th[:, m % 2, :], ALU.mult))
                    dve.wait_ge(lru_exp, 3 * m + 3)
                    step(V.tensor_tensor_scan(xc[:, m % 2, :], r[:], ig[:], 0.0, ALU.mult, ALU.add))
                    dve.wait_ge(lru_evac, 4 * m + 4)
                    V.tensor_tensor(gg[:, m, :], gg[:, m, :], xc[:, m % 2, :], ALU.mult).then_inc(y_lru, 1)
                if u >= 2 * NM:
                    for j in (2 * u - 4 * NM, 2 * u - 4 * NM + 1):
                        j -= 1
                        if j < 0 or j >= 4 * NM:
                            continue
                        m, s, isk = j // 2 % NM, j % 2, j >= 2 * NM
                        dve.wait_ge(qk_rms, j + 1)
                        step(V.reciprocal(rt[:, j % 2, :], rt[:, j % 2, :]))
                        gain = vc[:, KG:KG + 1] if isk else qgh[:, m:m + 1]
                        V.scalar_tensor_tensor(out=(k if isk else q)[:, m, s * HALF:(s + 1) * HALF], in0=ps[:, (4 * NM + j) % 4, :],
                                               scalar=gain, in1=rt[:, j % 2, :], op0=ALU.mult, op1=ALU.mult).then_inc(qk_done, 1)

            def lru_norm():
                dve.wait_ge(y_rms, 2)
                step(V.reciprocal(yr[:], yr[:]))
                dve.wait_ge(y_sq, NM)
                for m in range(NM):
                    V.scalar_tensor_tensor(out=gg[:, m, :], in0=gg[:, m, :], scalar=vc[:, LG + m:LG + m + 1],
                                           in1=yr[:], op0=ALU.mult, op1=ALU.mult).then_inc(lru_ready, 1)

            dve.wait_ge(nd_raw, 1)
            step(V.scalar_tensor_tensor(out=nd[:], in0=ndt[:], scalar=-1.0, in1=ndt[:], op0=ALU.mult, op1=ALU.min))
            step(V.memset(nd[0:CHUNK, T - CHUNK:T], NEG_BIG))
            for t in range(NI + 6):
                if t == NI + 2:
                    lru_norm()
                if t < NI:
                    hh, i = item(t)
                    w = P * (i + 1)
                    for cc in range(2):
                        dve.wait_ge(s_done, 2 * t + cc + 1)
                        if t >= 3:
                            dve.wait_ge(t_done, tpos[("w", t - 3)] + 1)
                        src = ps[:, 2 * cc:2 * cc + 2, :].rearrange("p a n -> p (a n)")
                        V.tensor_tensor_reduce(out=pr[:, t % 3, cc, 0:w], in0=src[:, 0:w], in1=nd[:, T - w:T], scale=1.0,
                                               scalar=-3e38, op0=ALU.add, op1=ALU.max,
                                               accum_out=mx[:, t, cc:cc + 1]).then_inc(s_biased, 1)
                    dve.wait_ge(s_biased, 2 * t + 2)
                    V.tensor_scalar(nb[:, t, :], mx[:, t, :], -slope[hh], None, ALU.mult).then_inc(s_nmax, 1)
                u = t - 4
                if 0 <= u < NI:
                    dve.wait_ge(pv_done, u + 1)
                    hh, i = item(u)
                    if hh >= 2 and u % NB == 0:
                        dve.wait_ge(t_done, tpos[("y", hh - 2)] + 1)
                    V.tensor_scalar(osb[:, hh % 2, i, :], ps[:, 6 + u % 2, 0:P], ri[:, u, 0:1], None, ALU.mult).then_inc(o_evac, 1)
                    if u % NB == NB - 1:
                        dve.wait_ge(o_evac, u + 1)
                        step(V.tensor_tensor(osq[:], osb[:, hh % 2, :, :], osb[:, hh % 2, :, :], ALU.mult))
                        step(V.tensor_reduce(out=oss[:, hh % 2, :], in_=osq[:], axis=AX.X, op=ALU.add))
                        V.tensor_scalar(oss[:, hh % 2, :], oss[:, hh % 2, :], 1.0 / P, EPS, ALU.mult, ALU.add).then_inc(o_ms, 1)
                u = t - 1
                if 0 <= u < NI:
                    w = P * (item(u)[1] + 1)
                    dve.wait_ge(p_ready, 2 * u + 2)
                    step(V.reciprocal(ri[:, u, :], sm[:, u, :]))
                    step(V.tensor_scalar(ra[:, u:u + 1], ri[:, u, 1:2], neg_lam, sm[:, u, 0:1], ALU.mult, ALU.mult))
                    V.scalar_tensor_tensor(out=pr[:, u % 3, 1, 0:w], in0=pr[:, u % 3, 1, 0:w], scalar=ra[:, u:u + 1],
                                           in1=pr[:, u % 3, 0, 0:w], op0=ALU.mult, op1=ALU.add).then_inc(w_ready, 1)
                u = t - 5
                if 0 <= u < NI and u % NB == NB - 1:
                    hh = u // NB
                    dve.wait_ge(o_pow, hh + 1)
                    V.tensor_tensor(osb[:, hh % 2, :, :], osb[:, hh % 2, :, :],
                                    oss[:, hh % 2, :].unsqueeze(2).to_broadcast([P, NB, P]), ALU.mult).then_inc(o_normed, 1)
            for b in range(NB + 2):
                if b < NB:
                    dve.wait_ge(op_done, b + 1)
                    dve.wait_ge(xr_landed[b % 2], 16 * (b // 2 + 1))
                    if b >= 2:
                        dve.wait_ge(h_stored[b % 2], 16 * (b // 2))
                        dve.wait_ge(hn2_stored[b % 2], 16 * (b // 2))
                        dve.wait_ge(xt2_done, b - 1)
                    src = ps[:, 2 * (b % 2):2 * (b % 2) + 2, :].rearrange("p a n -> p (a n)")
                    V.tensor_tensor(h[:, b % 2, :], src, xr[:, b % 2, :], ALU.add).then_inc(h_ready, 1)
                    dve.wait_ge(h_rms, b + 1)
                    if b == 0:
                        dve.wait_ge(wout_landed, 16 * 7)
                        dve.wait_ge(br_landed, 32)
                    step(V.reciprocal(rs[:, b:b + 1], ss[:, b:b + 1]))
                    V.scalar_tensor_tensor(out=hn2[:, b % 2, :], in0=h[:, b % 2, :], scalar=rs[:, b:b + 1],
                                           in1=g2b[:], op0=ALU.mult, op1=ALU.mult).then_inc(hn2_ready, 1)
                if b >= 2:
                    bb = b - 2
                    dve.wait_ge(r_done, bb + 1)
                    V.tensor_tensor(lg[:, bb, :], ps[:, 6 + bb % 2, 0:NR], br[:], ALU.add).then_inc(logits_ready, 1)
            dve.wait_ge(logits_ready, NB)
            dve.wait_ge(route_const, 1)

            def first_max(onehot, values, top, free, cnt):
                step(V.tensor_reduce(out=top, in_=values, axis=AX.X, op=ALU.max))
                step(V.tensor_tensor(onehot, values, top.unsqueeze(2).to_broadcast([P, NB, cnt]), ALU.is_equal))
                step(V.tensor_scalar(free, onehot[:, :, 0], -1.0, 1.0, ALU.mult, ALU.add))
                for j in range(1, cnt):
                    step(V.tensor_tensor(onehot[:, :, j], onehot[:, :, j], free, ALU.mult))
                    if j < cnt - 1:
                        step(V.tensor_tensor(free, free, onehot[:, :, j], ALU.subtract))

            lgg = lg[:, :, 0:NG]
            first_max(ohg[:], lgg, gtop[:], free[:], NG)
            step(V.tensor_tensor(gexp[:], lgg, gtop[:].unsqueeze(2).to_broadcast([P, NB, NG]), ALU.subtract))
            for gq in range(NG):
                le = lg[:, :, NG + gq * EPG:NG + (gq + 1) * EPG]
                oh = ohg[:, :, gq].unsqueeze(2).to_broadcast([P, NB, EPG])
                if gq == 0:
                    step(V.tensor_tensor(sel[:], le, oh, ALU.mult))
                else:
                    step(V.tensor_tensor(stmp[:], le, oh, ALU.mult))
                    step(V.tensor_tensor(sel[:], sel[:], stmp[:], ALU.add))
            first_max(oh1[:], sel[:], etop1[:], free[:], EPG)
            step(V.tensor_scalar(stmp[:], oh1[:], -3e38, None, ALU.mult))
            step(V.tensor_tensor(stmp[:], stmp[:], sel[:], ALU.add))
            first_max(oh2[:], stmp[:], etop2[:], free[:], EPG)
            V.tensor_tensor(edif[:], etop2[:], etop1[:], ALU.subtract).then_inc(route_max, 1)
            for j, oh in enumerate((oh1, oh2)):
                for gq in range(NG):
                    step(V.tensor_tensor(mm[:, j, :, gq * EPG:(gq + 1) * EPG], oh[:],
                                         ohg[:, :, gq].unsqueeze(2).to_broadcast([P, NB, EPG]), ALU.mult))
            step(V.tensor_tensor(msum[:], mm[:, 0, :, :], mm[:, 1, :, :], ALU.add))
            step(V.memset(mcum[:, 0, :], 0.0))
            for b in range(1, NB):
                step(V.tensor_tensor(mcum[:, b, :], mcum[:, b - 1, :], msum[:, b - 1, :], ALU.add))
            V.tensor_tensor(mtot[:], mcum[:, NB - 1, :], msum[:, NB - 1, :], ALU.add).then_inc(mask_ready, 1)
            dve.wait_ge(route_exp, 1)
            step(V.tensor_reduce(out=gsum[:], in_=gexp[:], axis=AX.X, op=ALU.add))
            step(V.tensor_scalar(esum[:], edif[:], 1.0, None, ALU.add))
            step(V.tensor_tensor(gsum[:], gsum[:], esum[:], ALU.mult))
            step(V.reciprocal(gates[:, 0, :], gsum[:]))
            step(V.tensor_tensor(gates[:, 1, :], gates[:, 0, :], edif[:], ALU.mult))
            dve.wait_ge(prefix_done, 2)
            step(V.tensor_copy(cnt[:], ps[:, 1, 0:NE]))
            step(V.memset(ntile[:], 1.0))
            for j in range(1, NB):
                step(V.scalar_tensor_tensor(out=ntile[:], in0=cnt[:], scalar=float(P * j), in1=ntile[:],
                                            op0=ALU.is_gt, op1=ALU.add))
            step(V.tensor_tensor_scan(tincl[:, 0:NE], ones[:, 0:NE], ntile[:], 0.0, ALU.mult, ALU.add))
            step(V.tensor_copy(tincl[:, NE:NE + 1], tincl[:, NE - 1:NE]))
            step(V.tensor_scalar(tincl[:, NE + 1:NE + 2], tincl[:, NE - 1:NE], -1.0, None, ALU.add))
            step(V.tensor_copy(tiles_i[:], tincl[:]))
            step(V.tensor_tensor(texcl[:], tincl[:, 0:NE], ntile[:], ALU.subtract))
            step(V.scalar_tensor_tensor(out=slotm[:], in0=texcl[:].unsqueeze(1).to_broadcast([P, NB, NE]), scalar=float(P),
                                        in1=ps[:, 0, 0:NB * NE].rearrange("p (b e) -> p b e", e=NE), op0=ALU.mult, op1=ALU.add))
            for j in range(2):
                step(V.tensor_tensor(stmp2[:], slotm[:], mm[:, j, :, :], ALU.mult))
                step(V.tensor_reduce(out=slot[:, j, :], in_=stmp2[:], axis=AX.X, op=ALU.add))
            step(V.tensor_copy(slot_i[:], slot[:]))
            step(V.tensor_scalar(srow_i[:], slot_i[:], P - 1, None, ALU.bitwise_and))
            step(V.tensor_scalar(scol_i[:], slot_i[:], 7, None, ALU.logical_shift_right))
            step(V.tensor_copy(srow[:], srow_i[:]))
            step(V.tensor_copy(scol[:], scol_i[:]))
            for j in range(2 * NB):
                jj, b = j % 2, j // 2
                if j >= 2:
                    dve.wait_ge(list_mm, j - 1)
                step(V.tensor_scalar(lrow[:, jj, :], iota_row[:], srow[:, jj, b:b + 1], None, ALU.is_equal))
                step(V.tensor_scalar(lval[:, jj, 0, :], iota_row[:, 0:32], scol[:, jj, b:b + 1], tok1[:, b:b + 1],
                                     ALU.is_equal, ALU.mult))
                V.tensor_scalar(lval[:, jj, 1, :], iota_row[:, 0:32], scol[:, jj, b:b + 1], gates[:, jj, b:b + 1],
                                ALU.is_equal, ALU.mult).then_inc(list_operands, 1)
            step(V.tensor_tensor(tcmp[:], iota_row[:, 0:33].unsqueeze(2).to_broadcast([P, 33, NE]),
                                 tincl[:, 0:NE].unsqueeze(1).to_broadcast([P, 33, NE]), ALU.is_ge))
            step(V.tensor_reduce(out=texp[:], in_=tcmp[:], axis=AX.X, op=ALU.add))
            step(V.tensor_copy(texp_i[:], texp[:]))
            step(V.tensor_tensor(tchg[:, 0:32], texp[:, 1:33], texp[:, 0:32], ALU.is_gt))
            step(V.tensor_copy(tfirst_i[:, 1:32], tchg[:, 0:31]))
            step(V.memset(tchg[:, 32:33], 0.0))
            step(V.tensor_copy(tfirst_i[:, 0:1], tchg[:, 32:33]))
            step(V.scalar_tensor_tensor(out=tchg[:, 0:32], in0=texp[:, 0:32], scalar=float(NE - 1), in1=tchg[:, 0:32],
                                        op0=ALU.is_lt, op1=ALU.mult))
            step(V.tensor_copy(tlast_i[:], tchg[:, 0:32]))
            dve.wait_ge(list_mm, 2 * NB)
            step(V.tensor_copy(ltok[:], ps[:, 2, 0:32]))
            step(V.tensor_copy(lgate[:], ps[:, 2, 32:64]))
            step(V.tensor_scalar(lemp[:], ltok[:], 0.0, 1.0, ALU.is_equal, ALU.mult))
            step(V.scalar_tensor_tensor(out=ltok[:], in0=ltok[:], scalar=-1.0, in1=lemp[:], op0=ALU.add, op1=ALU.add))
            step(V.tensor_tensor(lemp[:], lemp[:], pad1[:], ALU.mult))
            V.tensor_tensor(ltok[:], ltok[:], lemp[:], ALU.add).then_inc(lists_ready, 1)
            dve.wait_ge(lists_ready, 1)
            def low(j, c, count):
                dve.wait_ge(hi_ready[j], count)
                V.tensor_tensor(wlo[NC * j + c][:].rearrange("p k n -> p (k n)"), raw[:, j, c, :],
                                whi[NC * j + c][:].rearrange("p k n -> p (k n)").bitcast(F32),
                                ALU.subtract).then_inc(lo_ready[j], 1)

            def x_low(count):
                dve.wait_ge(mxt_evac, count)
                V.tensor_tensor(xTl[:, :, :].rearrange("p k n -> p (k n)"), xT_ps,
                                xTh[:, :, :].rearrange("p k n -> p (k n)").bitcast(F32), ALU.subtract).then_inc(mxT_lo, 1)

            def h_low(g):
                dve.wait_ge(ht_evac, g)
                V.tensor_tensor(hTl[:, :, :].rearrange("p k n -> p (k n)"), ps[:, 6, :],
                                hTh[:, :, :].rearrange("p k n -> p (k n)").bitcast(F32), ALU.subtract).then_inc(hT_lo, 1)

            def hidden(g):
                dve.wait_ge(sil_ready, g + 1)
                dve.wait_ge(part_used[1], g * NC + NC)
                V.tensor_tensor(hid[:], ps[:, 1, :], sil[:], ALU.mult).then_inc(hid_ready, 1)

            def gated(g):
                V.tensor_copy(gcol[:, 0:1], lgate[:, bass.ds(g - 1, 1)]).then_inc(gcol_ready, 1)
                dve.wait_ge(gcol_ready, g)
                dve.wait_ge(part_used[2], g * NC)
                dve.wait_ge(scattered, g * 16)
                V.tensor_scalar(ysb[:], y_ps, gcol[:, 0:1], None, ALU.mult).then_inc(y_ready, 1)

            x_low(1)
            for j in range(3):
                for c in range(NC):
                    low(j, c, c + 1)
                if j == 0:
                    dve.wait_ge(pad_stored, 16)
            hidden(0)
            x_low(2)
            nt = dve.value_load(tiles_i[0:1, NE:NE + 1], min_val=NE, max_val=MAX_TILES)
            with dve.Fori(1, nt) as g:
                e = dve.value_load(texp_i[0:1, bass.ds(g, 1)], min_val=0, max_val=NE - 1)
                last = dve.value_load(tlast_i[0:1, bass.ds(g, 1)], min_val=0, max_val=1)
                first = dve.value_load(tfirst_i[0:1, bass.ds(g, 1)], min_val=0, max_val=1)
                with dve.If(last != 0):
                    for c in range(NC - 1):
                        low(0, c, e * NC + (c + 1 + NC))
                    h_low(g)
                    low(0, NC - 1, e * NC + 2 * NC)
                    for c in range(NC - 1):
                        low(1, c, e * NC + (c + 1 + NC))
                    hidden(g)
                    x_low(g + 2)
                    low(1, NC - 1, e * NC + 2 * NC)
                with dve.Else():
                    h_low(g)
                    hidden(g)
                    x_low(g + 2)
                with dve.If(first != 0):
                    for c in range(NC):
                        low(2, c, e * NC + (c + 1))
                gated(g)
                dve.wait_ge(y_ready, g)
            h_low(nt)
            gated(nt)

        @block.tensor
        def _(pe):
            mm_, tr = nc.tensor.matmul, nc.tensor.transpose

            pe.wait_ge(consts_built, 1)
            pe.wait_ge(vec_landed, 16 * 11)
            tr(ps[:, 7, 0:NV], vrow[0:NV, :], ident[0:NV, 0:NV]).then_inc(vec_transposed, 1)
            for b in range(NB):
                pe.wait_ge(hn_ready, b + 1)
                if b >= 2:
                    pe.wait_ge(hnT_act, b - 1)
                    pe.wait_ge(hnT_dve, b - 1)
                for kk in range(KD):
                    last = tr(ps[:, 2 * (b % 2) + kk // 4, kk % 4 * P:(kk % 4 + 1) * P],
                              xs[:, b % 2, kk * P:(kk + 1) * P], ident[:])
                last.then_inc(hn_transposed, 1)
            pe.wait_ge(hnT_act, NB)
            pe.wait_ge(hnT_dve, NB)

            def bank_free(g):
                if g < 4 * NM:
                    pe.wait_ge(lru_evac, g + 1)
                elif g < 8 * NM:
                    pe.wait_ge(qk_done, g - 4 * NM + 1)
                else:
                    pe.wait_ge(v_evac, g - 8 * NM + 1)

            def qk_norm(j):
                pe.wait_ge(qk_sq, j + 1)
                if j >= 2:
                    pe.wait_ge(qk_rms, j - 1)
                mm_(ps[:, 4 + j % 2, :], ones_blk[:], sq[:, j % 2, :], start=True, stop=True).then_inc(qk_mm, 1)

            def gates(m):
                pe.wait_ge(bd_landed, 64)
                pe.wait_ge(conv_done, m + 1)
                for j in range(4 * m, 4 * m + 4):
                    gi, s = j // 2 % 2, j % 2
                    if j >= 2:
                        pe.wait_ge(gate_sig, j - 1)
                    mm_(ps[:, 6 + j % 2, :], bd[:, gi, m, :], xc[:, m % 2, s * HALF:(s + 1) * HALF],
                        start=True, stop=True).then_inc(gate_mm, 1)

            for u in range(4 * NM):
                pe.wait_ge(w_low, u + 1)
                for s in range(2):
                    g = 2 * u + s
                    if g >= 4:
                        bank_free(g - 4)
                    hs = slice(s * HALF, (s + 1) * HALF)
                    for kk in range(KD):
                        for w, hx in ((wih, hnTh), (wih, hnTl), (wil, hnTh)):
                            last = mm_(ps[:, g % 4, :], w[:, u % RING, kk, :], hx[:, kk, hs],
                                       start=(kk == 0 and w is wih and hx is hnTh), stop=(kk == KD - 1 and w is wil))
                    last.then_inc(group_done, 1)
                    if g >= 4 * NM + 1:
                        qk_norm(g - 4 * NM - 1)
                if u % 2 == 0 and 2 <= u <= 2 * NM:
                    gates(u // 2 - 1)
            pe.wait_ge(w_low, 5 * NM)
            for b in range(NB):
                g = 8 * NM + b
                bank_free(g - 4)
                for kk in range(KD):
                    for hx, w in ((hnTh, wih), (hnTh, wil), (hnTl, wih)):
                        last = mm_(ps[:, g % 4, :].rearrange("p (u n) -> p u n", n=P), hx[:, kk, b * P:(b + 1) * P],
                                   w[:, 0:NM, kk, :], start=(kk == 0 and hx is hnTh and w is wih),
                                   stop=(kk == KD - 1 and hx is hnTl))
                last.then_inc(group_done, 1)
                if b == 0:
                    qk_norm(4 * NM - 1)
                    pe.wait_ge(gate_sig, 4 * NM)
                    for m in range(NM):
                        pe.wait_ge(y_sq, m + 1)
                        for s in range(2):
                            mm_(ps[:, 6 + s, :], ones[:], th[:, m % 2, s * HALF:(s + 1) * HALF],
                                start=(m == 0), stop=(m == NM - 1)).then_inc(y_norm_mm, 1)
            pe.wait_ge(v_evac, NB)
            pe.wait_ge(qk_done, 4 * NM)
            pe.wait_ge(y_rms, 2)
            for t in range(NI + 4):
                if t < NI:
                    hh, i = item(t)
                    w = P * (i + 1)
                    pe.wait_ge(qz_ready, 2 * hh + 2)
                    for cc in range(2):
                        if t >= 1:
                            pe.wait_ge(s_biased, 2 * (t - 1) + cc + 1)
                        for s in range(0, w, HALF):
                            last = mm_(ps[:, 2 * cc + s // HALF, 0:min(HALF, w - s)], qz[:, hh % 2, cc, i * P:(i + 1) * P],
                                       k[:, hh, s:min(w, s + HALF)], start=True, stop=True)
                        last.then_inc(s_done, 1)
                u = t - 3
                if 0 <= u < NI:
                    hh, i = item(u)
                    pe.wait_ge(t_evac, tpos[("w", u)] + 1)
                    if u >= 2:
                        pe.wait_ge(o_evac, u - 1)
                    for j in range(i + 1):
                        last = mm_(ps[:, 6 + u % 2, 0:P], wT[:, u % 2, j * P:(j + 1) * P], v[:, j, hh * P:(hh + 1) * P],
                                   start=(j == 0), stop=(j == i))
                    last.then_inc(pv_done, 1)
                for kind, tt in tslots:
                    if not ((kind == "w" and tt == t - 2) or (kind == "y" and tt < NM - 1 and t - 2 == NB * (tt + 1) + Y_AT)
                            or (kind == "y" and tt == NM - 1 and t == NI + 3)):
                        continue
                    ti = tpos[(kind, tt)]
                    if ti >= 1:
                        pe.wait_ge(t_evac, ti)
                    if kind == "w":
                        pe.wait_ge(w_ready, tt + 1)
                    else:
                        pe.wait_ge(o_normed, tt + 1)
                    cols = item(tt)[1] + 1 if kind == "w" else NB
                    for j in range(cols):
                        src = pr[:, tt % 3, 1, j * P:(j + 1) * P] if kind == "w" else osb[:, tt % 2, j, :]
                        last = tr(ps[:, 4 + j // 4, j % 4 * P:(j % 4 + 1) * P], src, ident[:])
                    last.then_inc(t_done, 1)
            pe.wait_ge(t_evac, len(tslots))
            pe.wait_ge(lru_ready, NM)
            pe.wait_ge(wout_landed, 16 * 7)
            pe.wait_ge(s_biased, 2 * NI)
            pe.wait_ge(o_evac, NI)
            for b in range(NB + 2):
                if b < NB:
                    if b >= 2:
                        pe.wait_ge(h_ready, b - 1)
                    for s in range(2):
                        for kk in range(KD):
                            y = gg if kk < NM else yatt
                            last = mm_(ps[:, 2 * (b % 2) + s, :], y[:, kk % NM, b * P:(b + 1) * P],
                                       wout[:, kk, s * HALF:(s + 1) * HALF], start=(kk == 0), stop=(kk == KD - 1))
                    last.then_inc(op_done, 1)
                if b >= 2:
                    bb = b - 2
                    pe.wait_ge(xt2_evac, bb + 1)
                    if bb >= 2:
                        pe.wait_ge(logits_ready, bb - 1)
                    for kk in range(KD):
                        last = mm_(ps[:, 6 + bb % 2, 0:NR], hn2T[:, bb % 2, kk, :], wr[:, kk, :],
                                   start=(kk == 0), stop=(kk == KD - 1))
                    last.then_inc(r_done, 1)
                if 1 <= b <= NB:
                    bb = b - 1
                    pe.wait_ge(hn2_ready, bb + 1)
                    if bb >= 1:
                        pe.wait_ge(xt2_evac, bb)
                    for kk in range(KD):
                        last = tr(ps[:, 4 + kk // 4, kk % 4 * P:(kk % 4 + 1) * P], hn2[:, bb % 2, kk * P:(kk + 1) * P], ident[:])
                    last.then_inc(xt2_done, 1)
            pe.wait_ge(mask_ready, 1)
            pe.wait_ge(h_ready, NB)
            mm_(ps[:, 0, 0:NB * NE], upper[:], msum[:].rearrange("p b e -> p (b e)"), start=True, stop=False)
            mm_(ps[:, 0, 0:NB * NE], ones[:], mcum[:].rearrange("p b e -> p (b e)"), start=False, stop=True).then_inc(prefix_done, 1)
            mm_(ps[:, 1, 0:NE], ones[:], mtot[:], start=True, stop=True).then_inc(prefix_done, 1)
            for j in range(2 * NB):
                jj = j % 2
                pe.wait_ge(list_operands, j + 1)
                mm_(ps[:, 2, 0:64], lrow[:, jj, :], lval[:, jj, :, :].rearrange("p a n -> p (a n)"),
                    start=(j == 0), stop=(j == 2 * NB - 1)).then_inc(list_mm, 1)
            pe.wait_ge(lists_ready, 1)
            nt = pe.value_load(tiles_i[0:1, NE:NE + 1], min_val=NE, max_val=MAX_TILES)

            def rows_transposed():
                for kk in range(KD):
                    last = tr(ps[:, 2 + kk // 4, kk % 4 * P:(kk % 4 + 1) * P], xg[:, kk * P:(kk + 1) * P], ident[:])
                last.then_inc(mxt_done, 1)

            pe.wait_ge(gathered, 16)
            rows_transposed()
            def product(j, banks, lhs, count):
                per = (KD, KD, KE)[j] // NC
                for c in range(NC):
                    pe.wait_ge(lo_ready[j], count + c)
                    for kk in range(per):
                        n = c * per + kk
                        for a, w in ((0, whi), (0, wlo), (1, whi)):
                            for s, bank in enumerate(banks):
                                part = w[NC * j + c]
                                rhs = part[:, kk, :] if j < 2 else part[:, s, :]
                                last = mm_(ps[:, bank, :], lhs[a][:, n, :], rhs,
                                           start=(n == 0 and a == 0 and w is whi),
                                           stop=(n == (KD, KD, KE)[j] - 1 and a == 1))
                    last.then_inc(part_used[j], 1)

            def hidden_transposed():
                for f in range(KE):
                    last = tr(ps[:, 6, f * P:(f + 1) * P], hid[:, f * P:(f + 1) * P], ident[:])
                last.then_inc(ht_done, 1)

            pe.wait_ge(mxT_lo, 1)
            product(0, (0,), (xTh, xTl), 1)
            product(1, (1,), (xTh, xTl), 1)
            pe.wait_ge(gathered, 32)
            rows_transposed()
            with pe.Fori(1, nt) as g:
                e = pe.value_load(texp_i[0:1, bass.ds(g, 1)], min_val=0, max_val=NE - 1)
                e_before = pe.value_load(texp_i[0:1, bass.ds(g - 1, 1)], min_val=0, max_val=NE - 1)
                pe.wait_ge(mxT_lo, g + 1)
                pe.wait_ge(hid_ready, g)
                product(0, (0,), (xTh, xTl), e * NC + 1)
                hidden_transposed()
                product(1, (1,), (xTh, xTl), e * NC + 1)
                pe.wait_ge(gathered, g * 16 + 32)
                rows_transposed()
                pe.wait_ge(hT_lo, g)
                product(2, (4, 5), (hTh, hTl), e_before * NC + 1)
            pe.wait_ge(hid_ready, nt)
            hidden_transposed()
            pe.wait_ge(hT_lo, nt)
            product(2, (4, 5), (hTh, hTl), NE * NC - NC + 1)


_NAMES = ['x', 'norm1_g', 'w_in', 'conv_w', 'conv_b', 'w_gate_a', 'b_gate_a', 'w_gate_x', 'b_gate_x',
          'lru_lambda', 'lru_out_g', 'q_norm_g', 'k_norm_g', 'lambda_q1', 'lambda_k1', 'lambda_q2', 'lambda_k2',
          'sub_norm_g', 'w_out', 'norm2_g', 'w_router_group', 'b_router_group', 'w_router_expert',
          'b_router_expert', 'w_expert_gate', 'w_expert_up', 'w_expert_down']


def kernel(**inputs):
    import numpy as _np
    import concourse.bacc as _bacc
    from concourse import mybir as _mybir
    from concourse.bass_utils import run_bass_kernel_spmd as _run

    nc = _bacc.Bacc("TRN2", target_bir_lowering=False, num_devices=1)
    arrays, args = {}, []
    for name in _NAMES:
        a = _np.ascontiguousarray(inputs[name])
        arrays[f"in_{name}"] = a
        args.append(nc.dram_tensor(f"in_{name}", a.shape, _mybir.dt.from_np(a.dtype), kind="ExternalInput").ap())
    _, T, D = inputs['x'].shape
    out = nc.dram_tensor("out_rows", (T + 128, D), _mybir.dt.float32, kind="ExternalOutput").ap()
    hn2 = nc.dram_tensor("hn2_rows", (T + 128, D), _mybir.dt.float32, kind="Internal").ap()
    build_block(nc, *args, out, hn2)
    res = _run(nc, [arrays], core_ids=[0])
    return res.results[0]["out_rows"][:T].reshape(1, T, D)
```

```python
import math
from contextlib import ExitStack

import concourse.bass as bass
from concourse import mybir

F32 = mybir.dt.float32
F32R = mybir.dt.float32r
U32 = mybir.dt.uint32
I32 = mybir.dt.int32
ALU = mybir.AluOpType
ACT = mybir.ActivationFunctionType
AX = mybir.AxisListType

P = 128
EPS = 1e-6
NEG_BIG = -1e30
LAMBDA_INIT = 0.8 - 0.6 * math.exp(-0.3 * 0)
LRU_C = 8.0
CHUNK = 64


def build_block(nc, x, norm1_g, w_in, conv_w, conv_b, w_gate_a, b_gate_a, w_gate_x, b_gate_x,
                lru_lambda, lru_out_g, q_norm_g, k_norm_g, lambda_q1, lambda_k1, lambda_q2, lambda_k2,
                sub_norm_g, w_out, norm2_g, w_router_group, b_router_group, w_router_expert,
                b_router_expert, w_expert_gate, w_expert_up, w_expert_down, out, hn2_dram):
    T, D = x.shape[1], x.shape[2]
    NB = T // P
    KD = D // P
    NG, EPG = b_router_expert.shape[1], b_router_expert.shape[2]
    NE = NG * EPG
    DE = w_expert_gate.shape[3]
    KE = DE // P
    HALF = 512
    NM = 4
    HD = q_norm_g.shape[1]
    NR = NG + NG * EPG
    MAX_TILES = NE + (2 * T - NE) // P
    LIST = MAX_TILES + 1
    RING = 4
    assert D == 1024 and T == 1024 and NM * P == 512 and DE == HALF and LIST <= 32

    BASE = 16512

    def at(name, word, shape, dt=F32):
        n = 1
        for s in shape[1:]:
            n *= s
        assert BASE + 4 * (word + n) <= nc.sbuf_usable_end, name
        return nc.alloc_sbuf_tensor_at(name, shape, dt, offset=BASE + 4 * word)

    A0 = 0
    A1 = A0 + 2 * KD * T
    A2 = A1 + 4112 + 8192
    A3 = A2 + 5 * 4096
    A4 = A3 + 2048
    hnTh = at("hnTh", A0, [P, KD, T], F32R)
    hnTl = at("hnTl", A0 + 8192, [P, KD, T], F32R)
    XW = 4 + T
    xlp = at("xlp", A1, [P, 2, XW])
    a2 = at("a2", A1 + 2 * XW, [P, 2, T])
    v = at("v", A1, [P, NB, 512])
    q = at("q", A1 + 4112, [P, NM, T])
    k = at("k", A1 + 4112 + 4096, [P, NM, T])
    xs_a = at("xs_a", A1, [P, NB // 2, D])
    xs_b = at("xs_b", A2, [P, NB // 2, D])
    g1b = at("g1b", A1 + 4112 + 2048, [P, D])
    gg = at("gg", A2, [P, NM, T])
    wraw = at("wraw", A2 + 4096, [P, 2, KD, P])
    wih = at("wih", A2 + 6144, [P, RING, KD, P], F32R)
    wil = at("wil", A2 + 10240, [P, RING, KD, P], F32R)
    xc = at("xc", A2 + 14336, [P, 2, T])
    r = at("r", A2 + 16384, [P, T])
    ig = at("ig", A2 + 17408, [P, T])
    th = at("th", A2 + 18432, [P, 2, T])
    sq = at("sq", A3, [P, 2, HALF])
    rt = at("rt", A3 + 1024, [P, 2, HALF])
    yr = at("yr", A3, [P, T])
    junk = at("junk", A3, [P, D])
    qz = at("qz", A2 + 16384, [P, 2, 2, T])
    pr = at("pr", A0 + 4096, [P, 3, 2, T])
    wT = at("wT", A0 + 10240, [P, 2, T])
    nd = at("nd", A2 + 14336, [P, T])
    ndt = at("ndt", A2 + 15360, [P, T])
    osb = at("osb", A0 + 12288, [P, 2, NB, P])
    osq = at("osq", A0 + 14336, [P, NB, P])
    yatt = at("yatt", A0, [P, NM, T])
    wout = at("wout", A2 + 4096, [P, KD, D])
    woh = [at(f"woh{kk}", A1 + 4112 + D * kk, [P, D], F32R) for kk in range(KD)]
    wol = [at(f"wol{kk}", A2 + 4096 + D * kk, [P, D], F32R) for kk in range(KD)]
    yh = [at(f"yh{gr}", A2 + 16384 + 2048 * gr, [P, 2, NM, P], F32R) for gr in range(2)]
    yl = [at(f"yl{gr}", A2 + 17408 + 2048 * gr, [P, 2, NM, P], F32R) for gr in range(2)]
    xr = at("xr", A3, [P, 2, D])
    g2b = at("g2b", A2 + 12288, [P, D])
    wr = at("wr", A2 + 13312, [P, KD, NR])
    h = at("h", A0 + 4096, [P, 2, D])
    hn2 = at("hn2", A0 + 6144, [P, 2, D])
    hn2T = at("hn2T", A0 + 8192, [P, 2, KD, P])
    junk2 = at("junk2", A2 + 14336, [P, D])
    rc = [A0 + 12288]

    def route(name, shape, dt=F32):
        n = 1
        for s in shape[1:]:
            n *= s
        t = at(name, rc[0], shape, dt)
        rc[0] += (n + 7) // 8 * 8
        assert rc[0] <= A0 + 15360
        return t

    below = route("below", [P, P])
    iota_row = route("iota_row", [P, P])
    tok1 = route("tok1", [P, NB])
    pad1 = route("pad1", [P, 32])
    rank = route("rank", [P, EPG])
    restart = route("restart", [P, NE, NB])
    full = route("full", [P, NB])
    ohg, gexp = route("ohg", [P, NB, NG]), route("gexp", [P, NB, NG])
    selp = route("selp", [P, NB, NG, EPG])
    sel, stmp = route("sel", [P, NB, EPG]), route("stmp", [P, NB, EPG])
    oh1, oh2 = route("oh1", [P, NB, EPG]), route("oh2", [P, NB, EPG])
    key = route("key", [P, NB, EPG])
    gtop, etop1, etop2, ktop = (route(f"top{j}", [P, NB]) for j in range(4))
    edif, esum, gsum = (route(f"e{j}", [P, NB]) for j in range(3))
    mm = route("mm", [P, 2, NE, NB])
    msum, mincl = route("msum", [P, NE, NB]), route("mincl", [P, NE, NB])
    gates = route("gates", [P, 2, NB])
    tfull = route("tfull", [P, NE, NB])
    ntile, texcl, tincl = route("ntile", [P, NE]), route("texcl", [P, NE]), route("tincl", [P, NE])
    slotm, stmp2 = route("slotm", [P, NE, NB]), route("stmp2", [P, 2, NE, NB])
    slot, srow, scol = (route(f"slot{j}", [P, 2, NB]) for j in range(3))
    slot_i, srow_i, scol_i = (route(f"sloti{j}", [P, 2, NB], I32) for j in range(3))
    tcmp = route("tcmp", [P, 33, NE])
    texp = route("texp", [P, 33])
    tchg = route("tchg", [P, 33])
    lemp = route("lemp", [P, 32])
    lrow = at("lrow", A3, [P, 2, NB, P], F32R)
    lfrm = at("lfrm", A0 + 2048, [P, 2, NB, 32], F32R)
    lval = at("lval", A0 + 2560, [P, 2, NB, 32])
    leq = at("leq", A0 + 3072, [P, 2, NB, 32])
    NC = 4
    KC = KD // NC
    raw = at("raw", A1, [P, 3, NC, KC * DE])
    split_at = [A2 + 16384, A2 + 18432, A0 + 10240] + [A2 + 2048 * n for n in range(8)] + [A0 + 4096]
    whi = [at(f"whi{n}", split_at[n], [P, KC, DE], F32R) for n in range(3 * NC)]
    wlo = [at(f"wlo{n}", split_at[n] + 1024, [P, KC, DE], F32R) for n in range(3 * NC)]
    xg = at("xg", A0, [P, D])
    xTh = at("xTh", A0 + 1024, [P, KD, P], F32R)
    xTl = at("xTl", A0 + 2048, [P, KD, P], F32R)
    sil = at("sil", A0 + 3072, [P, DE])
    hid = at("hid", A0 + 3584, [P, DE])
    hTh = at("hTh", A0 + 6144, [P, KE, P], F32R)
    hTl = at("hTl", A0 + 6656, [P, KE, P], F32R)
    ysb = at("ysb", A0 + 15360, [P, D])
    c = [A4]

    def xs(b):
        return (xs_a, xs_b)[b // (NB // 2)][:, b % (NB // 2), :]

    def const(name, shape, dt=F32):
        n = 1
        for s in shape[1:]:
            n *= s
        t = at(name, c[0], shape, dt)
        c[0] += (n + 7) // 8 * 8
        return t

    ident = const("ident", [P, P])
    ones_blk = const("ones_blk", [P, P])
    ones = const("ones", [P, P])
    bd = at("bd", A1 + 4112 + 4096, [P, 2, NM, P])
    vrow = at("vrow", A1 + 4112 + 6144, [P, P])
    NV = 39
    vc = const("vc", [P, 40])
    CW, CB, BA, BX, LAM, LG, QG, KG, SG = 0, 16, 20, 24, 28, 32, 36, 37, 38
    br = const("br", [P, NR])
    eps = const("eps", [P, 1])
    ss = const("ss", [P, NB])
    rs = const("rs", [P, NB])
    sp = const("sp", [P, 8, NM])
    qgh = const("qgh", [P, NM])
    lamv = at("lamv", A1 + 4112 + 6272, [P, 4, HD])
    lams = const("lams", [P, 8])
    mx = const("mx", [P, NB * NM, 2])
    nb = const("nb", [P, NB * NM, 2])
    sm = const("sm", [P, NB * NM, 2])
    ri = const("ri", [P, NB * NM, 2])
    ra = const("ra", [P, NB * NM])
    oss = const("oss", [P, 2, NB])
    phalf = const("phalf", [P, NB])
    lg = const("lg", [P, NB, NR])
    ltok = const("ltok", [P, 32])
    lgate = const("lgate", [P, 32])
    tiles_i = const("tiles_i", [P, 2], I32)
    texp_i = const("texp_i", [P, 33], I32)
    tlast_i = const("tlast_i", [P, 32], I32)
    tfirst_i = const("tfirst_i", [P, 32], I32)
    idx_g = const("idx_g", [P, 2], U32)
    idx_s = const("idx_s", [P, 2], U32)
    gcol = const("gcol", [P, 2])

    ps = nc.alloc_psum_tensor("ps", [P, 8, HALF], F32)
    xT_ps = ps[:, 2:4, :].rearrange("p a n -> p (a n)")
    y_ps = ps[:, 4:6, :].rearrange("p a n -> p (a n)")

    with ExitStack() as ctx:
        def sem(name):
            return ctx.enter_context(nc.semaphore(name))

        consts_built = sem("consts_built")
        eps_ready = sem("eps_ready")
        vec_landed = sem("vec_landed")
        bd_landed = sem("bd_landed")
        bcast_landed = sem("bcast_landed")
        br_landed = sem("br_landed")
        g1_landed = sem("g1_landed")
        x_landed = [sem(f"x_landed{i}") for i in range(NB)]
        w_landed = [sem(f"w_landed{i}") for i in range(2)]
        w_high = sem("w_high")
        w_low = sem("w_low")
        x_rms = sem("x_rms")
        hn_ready = sem("hn_ready")
        hn_transposed = sem("hn_transposed")
        hnT_act = sem("hnT_act")
        hnT_dve = sem("hnT_dve")
        act_seq = sem("act_seq")
        dve_seq = sem("dve_seq")
        pool_seq = sem("pool_seq")
        vec_transposed = sem("vec_transposed")
        vec_ready = sem("vec_ready")
        lam_y = sem("lam_y")
        sp_ready = sem("sp_ready")
        lam_dots = sem("lam_dots")
        lam_exp = sem("lam_exp")
        group_done = sem("group_done")
        lru_evac = sem("lru_evac")
        conv_done = sem("conv_done")
        gate_mm = sem("gate_mm")
        gate_sig = sem("gate_sig")
        lru_exp = sem("lru_exp")
        om_ready = sem("om_ready")
        om_sqrt = sem("om_sqrt")
        y_lru = sem("y_lru")
        y_sq = sem("y_sq")
        y_norm_mm = sem("y_norm_mm")
        nd_raw = sem("nd_raw")
        y_rms = sem("y_rms")
        lru_ready = sem("lru_ready")
        qk_sq = sem("qk_sq")
        qk_mm = sem("qk_mm")
        qk_rms = sem("qk_rms")
        qk_done = sem("qk_done")
        v_evac = sem("v_evac")
        qz_ready = sem("qz_ready")
        qz_zeroed = sem("qz_zeroed")
        s_done = sem("s_done")
        s_biased = sem("s_biased")
        s_nmax = sem("s_nmax")
        p_ready = sem("p_ready")
        w_ready = sem("w_ready")
        t_done = sem("t_done")
        t_evac = sem("t_evac")
        pv_done = sem("pv_done")
        o_evac = sem("o_evac")
        o_ms = sem("o_ms")
        o_pow = sem("o_pow")
        o_normed = sem("o_normed")
        wout_landed = sem("wout_landed")
        xr_landed = [sem(f"xr_landed{i}") for i in range(2)]
        wout_hi = sem("wout_hi")
        wout_lo = sem("wout_lo")
        y_hi = [sem(f"y_hi{gr}") for gr in range(2)]
        y_lo = [sem(f"y_lo{gr}") for gr in range(2)]
        op_done = sem("op_done")
        h_ready = sem("h_ready")
        h_rms = sem("h_rms")
        hn2_ready = sem("hn2_ready")
        h_stored = [sem(f"h_stored{i}") for i in range(2)]
        hn2_stored = [sem(f"hn2_stored{i}") for i in range(2)]
        pad_ready = sem("pad_ready")
        pad_stored = sem("pad_stored")
        xt2_done = sem("xt2_done")
        xt2_evac = sem("xt2_evac")
        r_done = sem("r_done")
        logits_ready = sem("logits_ready")
        route_const = sem("route_const")
        route_max = sem("route_max")
        route_exp = sem("route_exp")
        mask_ready = sem("mask_ready")
        prefix_done = sem("prefix_done")
        list_operands = sem("list_operands")
        list_mm = sem("list_mm")
        lists_ready = sem("lists_ready")
        we_landed = [[sem(f"we_landed{j}_{i}") for i in range(NC)] for j in range(3)]
        hi_ready = [sem(f"hi_ready{j}") for j in range(3)]
        lo_ready = [sem(f"lo_ready{j}") for j in range(3)]
        part_used = [sem(f"part_used{j}") for j in range(3)]
        hT_lo = sem("hT_lo")
        mxT_lo = sem("mxT_lo")
        gather_index = sem("gather_index")
        gathered = sem("gathered")
        scatter_index = sem("scatter_index")
        scattered = sem("scattered")
        sil_ready = sem("sil_ready")
        hid_ready = sem("hid_ready")
        mxt_done = sem("mxt_done")
        mxt_evac = sem("mxt_evac")
        ht_done = sem("ht_done")
        ht_evac = sem("ht_evac")
        gcol_ready = sem("gcol_ready")
        y_ready = sem("y_ready")

        NI = NM * NB
        slope = [2.0 ** (-8.0 * (hh + 1) / NM) for hh in range(NM)]

        ORDER = [0, 7, 1, 6, 2, 5, 3, 4]

        def item(t):
            return t // NB, ORDER[t % NB]

        Y_AT = 6
        tslots = []
        for t in range(NI):
            tslots.append(("w", t))
            if t % NB == Y_AT and t >= NB:
                tslots.append(("y", t // NB - 1))
        tslots.append(("y", NM - 1))
        tpos = {s: n for n, s in enumerate(tslots)}
        Y_STEPS = [NB * (hh + 1) + Y_AT + 3 for hh in range(NM - 1)]
        WOUT_AT = [2 * NB + 2 + n for n in range(4)] + [2 * NB + 6, 2 * NB + 7, 3 * NB + 2, NI + 1]
        Y_SPLIT_AT = [3 * NB + 4, 3 * NB + 6]

        def unit_columns(u):
            return (u % 2 * NM + u // 2) * P if u < 2 * NM else u * P

        def x_bank(b):
            return 2 * b if b < 4 else 4 + 2 * (b % 2)

        def through(g):
            return {1: 3, 2: 2}.get(g, g + 1)

        UNIT_AT = (NB // 2, NB - 2, NB + 1)

        W_EXPERTS = (w_expert_gate, w_expert_up, w_expert_down)

        def part_of(j, c, e):
            rows = (KD, KD, KE)[j] * P // NC
            return W_EXPERTS[j][0, e, c * rows:(c + 1) * rows, :]

        block = ctx.enter_context(nc.Block())

        @block.sync
        def _(sp_):
            def load_unit(u):
                if u >= 2:
                    sp_.wait_ge(w_low, u - 1)
                sp_.dma_start(wraw[:, u % 2, :, :],
                              w_in[0, :, unit_columns(u):unit_columns(u) + P]
                              .rearrange("(k p) n -> p k n", p=P)).then_inc(w_landed[u % 2], 16)

            for b in range(NB):
                sp_.dma_start(xs(b), x[0, b * P:(b + 1) * P, :]).then_inc(x_landed[b], 16)
                if b == 0:
                    sp_.dma_start(g1b[:, :], norm1_g.to_broadcast([P, D])).then_inc(g1_landed, 16)
                if b in (2, 4):
                    load_unit(b // 2 - 1)
            sp_.dma_start(vrow[CW:CW + 4 * NM, :], conv_w[0].rearrange("j (m c) -> (j m) c", c=P)).then_inc(vec_landed, 16)
            for ap, row in ((conv_b, CB), (b_gate_a, BA), (b_gate_x, BX), (lru_lambda, LAM), (lru_out_g, LG)):
                sp_.dma_start(vrow[row:row + NM, :], ap[0].rearrange("(m c) -> m c", c=P)).then_inc(vec_landed, 16)
            sp_.dma_start(vrow[SG:SG + 1, :], sub_norm_g).then_inc(vec_landed, 16)
            for ap, row in ((q_norm_g, QG), (k_norm_g, KG)):
                for s in range(2):
                    sp_.dma_start(vrow[row:row + 1, s * HD:(s + 1) * HD], ap).then_inc(vec_landed, 16)
            for j, ap in enumerate((lambda_q1, lambda_k1, lambda_q2, lambda_k2)):
                sp_.dma_start(lamv[:, j, :], ap.to_broadcast([P, HD])).then_inc(bcast_landed, 16)
            sp_.wait_ge(consts_built, 1)
            for gi, ap in enumerate((w_gate_a, w_gate_x)):
                for s in range(2):
                    sp_.dma_start(bd[64 * s:64 * s + 64, gi, :, 64 * s:64 * s + 64],
                                  ap[0].rearrange("(m two) c d -> two c m d", two=2)[s]).then_inc(bd_landed, 16)
            sp_.dma_start(br[:, 0:NG], b_router_group.to_broadcast([P, NG])).then_inc(br_landed, 16)
            sp_.dma_start(br[:, NG:NR], b_router_expert.rearrange("a g e -> a (g e)").to_broadcast([P, NE])).then_inc(br_landed, 16)
            for u in range(2, 5 * NM):
                load_unit(u)
            sp_.wait_ge(group_done, 5 * NB)
            sp_.dma_start(wout[:, :, :], w_out[0].rearrange("(k p) n -> p k n", p=P)).then_inc(wout_landed, 16)
            sp_.dma_start(wr[:, :, 0:NG], w_router_group[0].rearrange("(k p) n -> p k n", p=P)).then_inc(wout_landed, 16)
            for gq in range(NG):
                sp_.dma_start(wr[:, :, NG + gq * EPG:NG + (gq + 1) * EPG],
                              w_router_expert[0, gq].rearrange("(k p) n -> p k n", p=P)).then_inc(wout_landed, 16)
            sp_.dma_start(g2b[:, :], norm2_g.to_broadcast([P, D])).then_inc(wout_landed, 16)
            sp_.wait_ge(lru_ready, NM)
            for b in range(2):
                sp_.dma_start(xr[:, b, :], x[0, b * P:(b + 1) * P, :]).then_inc(xr_landed[b], 16)
            sp_.wait_ge(pv_done, NI)
            def load_first(j):
                for c in range(NC):
                    sp_.dma_start(raw[:, j, c, :].rearrange("p (k n) -> p k n", n=(DE, DE, D)[j]),
                                  part_of(j, c, 0).rearrange("(k p) n -> p k n", p=P)).then_inc(we_landed[j][c], 16)

            load_first(0)
            sp_.wait_ge(pad_ready, 1)
            sp_.dma_start(hn2_dram[T:T + P, :], ysb[:, :]).then_inc(pad_stored, 16)
            for b in range(NB):
                sp_.wait_ge(h_ready, b + 1)
                sp_.dma_start(out[b * P:(b + 1) * P, :], h[:, b % 2, :]).then_inc(h_stored[b % 2], 16)
                if b + 2 < NB:
                    sp_.dma_start(xr[:, b % 2, :], x[0, (b + 2) * P:(b + 3) * P, :]).then_inc(xr_landed[b % 2], 16)
                sp_.wait_ge(hn2_ready, b + 1)
                sp_.dma_start(hn2_dram[b * P:(b + 1) * P, :], hn2[:, b % 2, :]).then_inc(hn2_stored[b % 2], 16)
            load_first(1)
            load_first(2)
            def load_matrix(j, e):
                for c in range(NC):
                    sp_.wait_ge(lo_ready[j], e * NC + (c + 1 - NC))
                    src = part_of(j, c, bass.ds(e, 1)).rearrange("o (k p) n -> p (o k) n", p=P) if not isinstance(e, int) \
                        else part_of(j, c, e).rearrange("(k p) n -> p k n", p=P)
                    sp_.dma_start(raw[:, j, c, :].rearrange("p (k n) -> p k n", n=(DE, DE, D)[j]),
                                  src).then_inc(we_landed[j][c], 16)

            load_matrix(0, 1)
            load_matrix(1, 1)
            with sp_.Fori(1, NE - 1) as e:
                load_matrix(0, e + 1)
                load_matrix(1, e + 1)
                load_matrix(2, e)
            load_matrix(2, NE - 1)
            for j in range(3):
                for c in range(NC):
                    sp_.wait_ge(we_landed[j][c], 16 * NE)

        @block.gpsimd
        def _(pool):
            n = [0]

            def step(ins):
                n[0] += 1
                ins.then_inc(pool_seq, 1)
                pool.wait_ge(pool_seq, n[0])

            nc.gpsimd.memset(eps[:], EPS).then_inc(eps_ready, 1)
            pool.wait_ge(eps_ready, 1)
            step(nc.gpsimd.memset(ident[:], 0.0))
            step(nc.gpsimd.affine_select(out=ident[:], in_=ident[:], compare_op=ALU.not_equal, fill=1.0,
                                         base=0, pattern=[[-1, P]], channel_multiplier=1))
            step(nc.gpsimd.memset(ones[:], 1.0))
            step(nc.gpsimd.memset(ones_blk[:], 0.0))
            step(nc.gpsimd.memset(ones_blk[0:64, 0:64], 1.0))
            step(nc.gpsimd.memset(ones_blk[64:128, 64:128], 1.0))
            step(nc.gpsimd.memset(phalf[:], -0.5))
            nc.gpsimd.memset(bd[:], 0.0).then_inc(consts_built, 1)
            pool.wait_ge(y_norm_mm, 2 * NM)
            nc.gpsimd.iota(ndt[:], pattern=[[-1, T]], base=T - P, channel_multiplier=1,
                           allow_small_or_imprecise_dtypes=True).then_inc(nd_raw, 1)
            pool.wait_ge(nd_raw, 1)
            nc.gpsimd.memset(qz[:], 0.0).then_inc(qz_zeroed, 1)
            pool.wait_ge(qz_zeroed, 1)

            def wout_low(kk):
                pool.wait_ge(wout_hi, kk + 1)
                nc.gpsimd.tensor_tensor(wol[kk][:], wout[:, kk, :], woh[kk][:].bitcast(F32), ALU.subtract).then_inc(wout_lo, 1)
                pool.wait_ge(wout_lo, kk + 1)

            for hh in range(NM):
                for kk in ((), (0, 1), (2, 3, 4, 5, 6), (7,))[hh]:
                    wout_low(kk)
                pool.wait_ge(o_ms, hh + 1)
                nc.gpsimd.tensor_tensor(oss[:, hh % 2, :], oss[:, hh % 2, :], phalf[:], ALU.pow).then_inc(o_pow, 1)
                pool.wait_ge(o_pow, hh + 1)
            nc.gpsimd.memset(ysb[:], 0.0).then_inc(pad_ready, 1)
            pool.wait_ge(pad_ready, 1)
            pool.dma_start(out[T:T + P, :], ysb[:, :]).then_inc(scattered, 16)
            pool.wait_ge(t_done, len(tslots))
            step(nc.gpsimd.memset(below[:], 0.0))
            step(nc.gpsimd.affine_select(out=below[:], in_=below[:], compare_op=ALU.is_gt, fill=-1.0,
                                         base=0, pattern=[[1, P]], channel_multiplier=-1))
            step(nc.gpsimd.iota(iota_row[:], pattern=[[1, P]], base=0, channel_multiplier=0,
                                allow_small_or_imprecise_dtypes=True))
            step(nc.gpsimd.iota(tok1[:], pattern=[[P, NB]], base=1, channel_multiplier=1,
                                allow_small_or_imprecise_dtypes=True))
            step(nc.gpsimd.iota(rank[:], pattern=[[-1, EPG]], base=EPG, channel_multiplier=0,
                                allow_small_or_imprecise_dtypes=True))
            step(nc.gpsimd.iota(full[:], pattern=[[P, NB]], base=0, channel_multiplier=0,
                                allow_small_or_imprecise_dtypes=True))
            step(nc.gpsimd.memset(full[:, 0:1], -1.0))
            step(nc.gpsimd.memset(restart[:], 1.0))
            step(nc.gpsimd.memset(restart[:, :, 0:1], 0.0))
            nc.gpsimd.iota(pad1[:], pattern=[[0, 32]], base=T + 1, channel_multiplier=1,
                           allow_small_or_imprecise_dtypes=True).then_inc(route_const, 1)
            for b in range(2):
                pool.wait_ge(hn2_stored[b], 16 * NB // 2)
                pool.wait_ge(h_stored[b], 16 * NB // 2)
            pool.wait_ge(pad_stored, 16)
            pool.wait_ge(scattered, 16)

            def gather():
                nc.gpsimd.indirect_dma_start(
                    out=xg[:], out_offset=None, in_=hn2_dram,
                    in_offset=bass.IndirectOffsetOnAxis(ap=idx_g[:, 0:1], axis=0)).then_inc(gathered, 16)

            pool.wait_ge(lists_ready, 1)
            step(nc.gpsimd.tensor_copy(idx_g[:, 0:1], ltok[:, 0:1]))
            gather()
            pool.wait_ge(lists_ready, 2)
            nt1 = pool.value_load(tiles_i[0:1, 1:2], min_val=NE - 1, max_val=MAX_TILES - 1)

            def next_rows(g):
                pool.wait_ge(mxt_done, g)
                nc.gpsimd.tensor_copy(idx_g[:, 0:1], ltok[:, bass.ds(g, 1)]).then_inc(gather_index, 1)
                pool.wait_ge(lists_ready, 1)
                pool.wait_ge(gather_index, g)
                gather()

            def add_rows(g):
                pool.wait_ge(scattered, g * 16)
                nc.gpsimd.tensor_copy(idx_s[:, 0:1], ltok[:, bass.ds(g - 1, 1)]).then_inc(scatter_index, 1)
                pool.wait_ge(lists_ready, 1)
                pool.wait_ge(scatter_index, g)
                pool.wait_ge(y_ready, g)
                nc.gpsimd.indirect_dma_start(
                    out=out, out_offset=bass.IndirectOffsetOnAxis(ap=idx_s[:, 0:1], axis=0),
                    in_=ysb[:], in_offset=None, compute_op=ALU.add).then_inc(scattered, 16)

            pool.wait_ge(mxt_done, 1)
            nc.gpsimd.tensor_copy(idx_g[:, 0:1], ltok[:, 1:2]).then_inc(gather_index, 1)
            pool.wait_ge(gather_index, 1)
            gather()
            next_rows(2)
            with pool.Fori(1, nt1) as g:
                next_rows(g + 2)
                add_rows(g)
            add_rows(nt1)
            add_rows(nt1 + 1)
            pool.wait_ge(scattered, nt1 * 16 + 32)
            pool.wait_ge(gathered, nt1 * 16 + 32)

        @block.scalar
        def _(act):
            n = [0]

            def step(ins):
                n[0] += 1
                ins.then_inc(act_seq, 1)
                act.wait_ge(act_seq, n[0])

            A = nc.scalar.activation

            act.wait_ge(eps_ready, 1)
            step(A(ss[:, 0:1], eps[:], ACT.Sqrt))
            def unit_high(u):
                act.wait_ge(w_landed[u % 2], 16 * (u // 2 + 1))
                if u >= RING:
                    act.wait_ge(group_done, through(2 * (u - RING) + 1))
                A(wih[:, u % RING, :, :], wraw[:, u % 2, :, :], ACT.Copy).then_inc(w_high, 1)

            for b in range(NB + 2):
                if b < NB:
                    act.wait_ge(x_landed[b], 16)
                    step(A(junk[:], xs(b), ACT.Square, accum_out=ss[:, b:b + 1]))
                    A(ss[:, b:b + 1], ss[:, b:b + 1], ACT.Sqrt, scale=1.0 / D, bias=eps[:, 0:1]).then_inc(x_rms, 1)
                if b >= 2:
                    bb = b - 2
                    act.wait_ge(hn_transposed, bb + 1)
                    A(hnTh[:, :, bb * P:(bb + 1) * P], ps[:, x_bank(bb):x_bank(bb) + 2, :]
                      .rearrange("p a (k n) -> p (a k) n", n=P), ACT.Copy).then_inc(hnT_act, 1)
                if b in UNIT_AT:
                    unit_high(UNIT_AT.index(b))
            act.wait_ge(vec_ready, 1)
            step(A(sp[:, 0, :], vc[:, LAM:LAM + NM], ACT.Abs))
            A(sp[:, 1, :], sp[:, 0, :], ACT.Exp, scale=-1.0).then_inc(lam_y, 1)
            act.wait_ge(lam_dots, 2)
            A(lams[:, 2:4], lams[:, 0:2], ACT.Exp).then_inc(lam_exp, 1)
            act.wait_ge(sp_ready, 1)
            for u in range(4 * NM + 1):
                if u >= 1:
                    unit_high(u + 2)
                if u == 4 * NM:
                    unit_high(u + 3)
                if u < 2 * NM:
                    m = u // 2
                    for s in range(2):
                        act.wait_ge(group_done, through(2 * u + s))
                        if u % 2 == 0:
                            if m >= 2:
                                act.wait_ge(conv_done, m - 1)
                            A(xlp[:, m % 2, 3 + s * HALF:3 + (s + 1) * HALF], ps[:, (2 * u + s) % 4, :], ACT.Copy).then_inc(lru_evac, 1)
                        else:
                            A(gg[:, m, s * HALF:(s + 1) * HALF], ps[:, (2 * u + s) % 4, :], ACT.Gelu_apprx_tanh).then_inc(lru_evac, 1)
                else:
                    if u == 2 * NM + 2 or u == 2 * NM + 6:
                        act.wait_ge(y_lru, NM)
                        for m in (0, 1) if u == 2 * NM + 2 else (2, 3):
                            if m >= 2:
                                act.wait_ge(y_norm_mm, 2 * m - 2)
                            A(th[:, m % 2, :], gg[:, m, :], ACT.Square).then_inc(y_sq, 1)
                    for j in (2 * u - 4 * NM, 2 * u - 4 * NM + 1):
                        g = 4 * NM + j
                        if j < 4 * NM:
                            act.wait_ge(group_done, g + 1)
                            if j >= 2:
                                act.wait_ge(qk_mm, j - 1)
                            A(sq[:, j % 2, :], ps[:, g % 4, :], ACT.Square).then_inc(qk_sq, 1)
                        if 1 <= j <= 4 * NM:
                            jj = j - 1
                            act.wait_ge(qk_mm, jj + 1)
                            if jj >= 2:
                                act.wait_ge(qk_done, jj - 1)
                            A(rt[:, jj % 2, :], ps[:, 4 + jj % 2, :], ACT.Sqrt, scale=1.0 / HD, bias=eps[:, 0:1]).then_inc(qk_rms, 1)
                if u % 2 == 0 and 2 <= u <= 2 * NM:
                    m = u // 2 - 1
                    for j in range(4 * m, 4 * m + 4):
                        gi, s = j // 2 % 2, j % 2
                        act.wait_ge(gate_mm, j + 1)
                        if m >= 1:
                            act.wait_ge(y_lru, m)
                        A((r, ig)[gi][:, s * HALF:(s + 1) * HALF], ps[:, 6 + j % 2, :], ACT.Sigmoid,
                          bias=vc[:, (BA, BX)[gi] + m:(BA, BX)[gi] + m + 1]).then_inc(gate_sig, 1)
                    act.wait_ge(gate_sig, 4 * m + 4)
                    A(a2[:, m % 2, :], r[:], ACT.Exp, scale=sp[:, 5, m:m + 1]).then_inc(lru_exp, 1)
                    A(th[:, m % 2, :], r[:], ACT.Tanh, scale=sp[:, 6, m:m + 1]).then_inc(lru_exp, 1)
                    act.wait_ge(lru_exp, 3 * m + 2)
                    A(r[:], r[:], ACT.Exp, scale=sp[:, 4, m:m + 1]).then_inc(lru_exp, 1)
                    act.wait_ge(om_ready, m + 1)
                    A(th[:, m % 2, :], th[:, m % 2, :], ACT.Sqrt).then_inc(om_sqrt, 1)
            act.wait_ge(y_norm_mm, 2 * NM)
            for s in range(2):
                A(yr[:, s * HALF:(s + 1) * HALF], ps[:, 6 + s, :], ACT.Sqrt, scale=1.0 / (NM * P), bias=eps[:, 0:1]).then_inc(y_rms, 1)
            for b in range(NB):
                act.wait_ge(group_done, 8 * NM + b + 1)
                if b == 0:
                    act.wait_ge(om_ready, NM)
                A(v[:, b, :], ps[:, b % 4, :], ACT.Copy).then_inc(v_evac, 1)
                if b == 2:
                    act.wait_ge(qk_done, 4 * NM)
                    act.wait_ge(qz_zeroed, 1)
                    for hh in range(2):
                        for cc in range(2):
                            sl = slice(64 * cc, 64 * cc + 64)
                            A(qz[sl, hh, cc, :], q[sl, hh, :], ACT.Copy).then_inc(qz_ready, 1)
            def wout_high(kk):
                A(woh[kk][:], wout[:, kk, :], ACT.Copy).then_inc(wout_hi, 1)

            def y_high(gr, b):
                if b >= 2:
                    act.wait_ge(op_done, b - 1)
                A(yh[gr][:, b % 2, :, :], (gg, yatt)[gr][:, :, b * P:(b + 1) * P], ACT.Copy).then_inc(y_hi[gr], 1)

            def t_out(kind, tt):
                act.wait_ge(t_done, tpos[(kind, tt)] + 1)
                src = ps[:, 4:6, :].rearrange("p a n -> p (a n)")
                if kind == "w":
                    w = P * (item(tt)[1] + 1)
                    if tt >= 2:
                        act.wait_ge(pv_done, tt - 1)
                    A(wT[:, tt % 2, 0:w], src[:, 0:w], ACT.Copy).then_inc(t_evac, 1)
                else:
                    A(yatt[:, tt, :], src, ACT.Copy, scale=lams[:, 6:7]).then_inc(t_evac, 1)

            for t in range(NI + 3):
                if t in Y_STEPS:
                    t_out("y", Y_STEPS.index(t))
                if t in WOUT_AT:
                    kk = WOUT_AT.index(t)
                    act.wait_ge(qz_ready, 2 * NM)
                    act.wait_ge(wout_landed, 16 * 7)
                    if kk >= NM:
                        act.wait_ge(s_done, 2 * NB * (kk - NM + 1))
                    wout_high(kk)
                if t in Y_SPLIT_AT:
                    act.wait_ge(lru_ready, NM)
                    act.wait_ge(s_done, 2 * NB * (NM - 1))
                    y_high(0, Y_SPLIT_AT.index(t))
                if t < NI:
                    hh, i = item(t)
                    w = P * (i + 1)
                    if t % NB == 1 and 1 <= hh < NM - 1:
                        act.wait_ge(s_done, 2 * NB * hh)
                        for cc in range(2):
                            sl = slice(64 * cc, 64 * cc + 64)
                            A(qz[sl, (hh + 1) % 2, cc, :], q[sl, hh + 1, :], ACT.Copy).then_inc(qz_ready, 1)
                    act.wait_ge(s_nmax, t + 1)
                    for cc in range(2):
                        A(pr[:, t % 3, cc, 0:w], pr[:, t % 3, cc, 0:w], ACT.Exp, scale=slope[hh],
                          bias=nb[:, t, cc:cc + 1], accum_out=sm[:, t, cc:cc + 1]).then_inc(p_ready, 1)
                if 0 <= t - 2 < NI:
                    t_out("w", t - 2)
                if t == NI + 2:
                    t_out("y", NM - 1)
            def mean_square(b):
                act.wait_ge(h_ready, b + 1)
                step(A(junk2[:], h[:, b % 2, :], ACT.Square, accum_out=ss[:, b:b + 1]))
                A(ss[:, b:b + 1], ss[:, b:b + 1], ACT.Sqrt, scale=1.0 / D, bias=eps[:, 0:1]).then_inc(h_rms, 1)

            def transposed_evac(b):
                act.wait_ge(xt2_done, b + 1)
                if b >= 2:
                    act.wait_ge(r_done, b - 1)
                A(hn2T[:, b % 2, :, :], ps[:, 4:6, :].rearrange("p a (k n) -> p (a k) n", n=P), ACT.Copy).then_inc(xt2_evac, 1)

            def y_highs(b):
                y_high(0, b)
                y_high(1, b)

            act.wait_ge(s_done, 2 * NI)
            act.wait_ge(t_evac, len(tslots))
            y_high(1, 0)
            y_high(1, 1)
            mean_square(0)
            y_highs(2)
            mean_square(1)
            y_highs(3)
            transposed_evac(0)
            for b in range(2, NB):
                transposed_evac(b - 1)
                mean_square(b)
                if b + 2 < NB:
                    y_highs(b + 2)
            transposed_evac(NB - 1)
            def high(j, c, e, used):
                act.wait_ge(we_landed[j][c], e * 16 + 16)
                if used is not None:
                    act.wait_ge(part_used[j], used)
                A(whi[NC * j + c][:].rearrange("p k n -> p (k n)"), raw[:, j, c, :], ACT.Copy).then_inc(hi_ready[j], 1)

            act.wait_ge(op_done, NB)
            act.wait_ge(r_done, NB)
            for b in range(2):
                act.wait_ge(h_stored[b], 16 * NB // 2)
                act.wait_ge(hn2_stored[b], 16 * NB // 2)
            for j in range(3):
                for c in range(NC):
                    if (j, c) == (1, 0):
                        act.wait_ge(route_max, 1)
                        step(A(gexp[:], gexp[:], ACT.Exp))
                        A(edif[:], edif[:], ACT.Exp).then_inc(route_exp, 1)
                    high(j, c, 0, None)
            act.wait_ge(lists_ready, 2)
            nt = act.value_load(tiles_i[0:1, 0:1], min_val=NE, max_val=MAX_TILES)

            def x_evac(count):
                act.wait_ge(mxt_done, count)
                A(xTh[:, :, :].rearrange("p k n -> p (k n)"), xT_ps, ACT.Copy).then_inc(mxt_evac, 1)

            def silu(g):
                act.wait_ge(part_used[0], g * NC + NC)
                A(sil[:], ps[:, 0, :], ACT.Silu).then_inc(sil_ready, 1)

            def h_evac(g):
                act.wait_ge(ht_done, g)
                A(hTh[:, :, :].rearrange("p k n -> p (k n)"), ps[:, 6, :], ACT.Copy).then_inc(ht_evac, 1)

            x_evac(1)
            silu(0)
            x_evac(2)
            with act.Fori(1, nt) as g:
                e = act.value_load(texp_i[0:1, bass.ds(g, 1)], min_val=0, max_val=NE - 1)
                last = act.value_load(tlast_i[0:1, bass.ds(g, 1)], min_val=0, max_val=1)
                first = act.value_load(tfirst_i[0:1, bass.ds(g, 1)], min_val=0, max_val=1)
                with act.If(last != 0):
                    for c in range(NC - 1):
                        high(0, c, e + 1, g * NC + (c + 1))
                    silu(g)
                    h_evac(g)
                    high(0, NC - 1, e + 1, g * NC + NC)
                    for c in range(NC - 1):
                        high(1, c, e + 1, g * NC + (c + 1))
                    x_evac(g + 2)
                    high(1, NC - 1, e + 1, g * NC + NC)
                with act.Else():
                    silu(g)
                    h_evac(g)
                    x_evac(g + 2)
                with act.If(first != 0):
                    for c in range(NC):
                        high(2, c, e, g * NC + (c + 1 - NC))
            h_evac(nt)

        @block.vector
        def _(dve):
            n = [0]
            V = nc.vector

            def step(ins):
                n[0] += 1
                ins.then_inc(dve_seq, 1)
                dve.wait_ge(dve_seq, n[0])

            def unit_low(u):
                dve.wait_ge(w_high, u + 1)
                V.tensor_tensor(wil[:, u % RING, :, :], wraw[:, u % 2, :, :], wih[:, u % RING, :, :].bitcast(F32),
                                ALU.subtract).then_inc(w_low, 1)

            dve.wait_ge(g1_landed, 16)
            for b in range(NB + 2):
                if b < NB:
                    dve.wait_ge(x_rms, b + 1)
                    step(V.reciprocal(rs[:, b:b + 1], ss[:, b:b + 1]))
                    V.scalar_tensor_tensor(out=xs(b), in0=xs(b), scalar=rs[:, b:b + 1],
                                           in1=g1b[:], op0=ALU.mult, op1=ALU.mult).then_inc(hn_ready, 1)
                if b >= 2:
                    bb = b - 2
                    dve.wait_ge(hnT_act, bb + 1)
                    V.tensor_tensor(hnTl[:, :, bb * P:(bb + 1) * P], ps[:, x_bank(bb):x_bank(bb) + 2, :]
                                    .rearrange("p a (k n) -> p (a k) n", n=P),
                                    hnTh[:, :, bb * P:(bb + 1) * P].bitcast(F32), ALU.subtract).then_inc(hnT_dve, 1)
                if b in (UNIT_AT[0] + 1, UNIT_AT[1] + 1, UNIT_AT[2]):
                    unit_low((UNIT_AT[0] + 1, UNIT_AT[1] + 1, UNIT_AT[2]).index(b))
            dve.wait_ge(hn_transposed, NB)
            step(V.memset(xlp[:, :, 0:3], 0.0))
            dve.wait_ge(vec_transposed, 1)
            step(V.tensor_copy(vc[:, 0:NV], ps[:, 7, 0:NV]))
            for hh in range(NM):
                step(V.tensor_scalar(qgh[:, hh:hh + 1], vc[:, QG:QG + 1], HD ** -0.5 / slope[hh], None, ALU.mult))
            V.tensor_scalar(lams[:, 6:7], vc[:, SG:SG + 1], 1.0 - LAMBDA_INIT, None, ALU.mult).then_inc(vec_ready, 1)
            dve.wait_ge(vec_ready, 1)
            dve.wait_ge(bcast_landed, 64)
            for j in range(2):
                V.tensor_tensor_reduce(out=lamv[:, 2 * j, :], in0=lamv[:, 2 * j, :], in1=lamv[:, 2 * j + 1, :], scale=1.0,
                                       scalar=0.0, op0=ALU.mult, op1=ALU.add, accum_out=lams[:, j:j + 1]).then_inc(lam_dots, 1)
            dve.wait_ge(lam_y, 1)
            y_, z_, z2, acc = sp[:, 1, :], sp[:, 2, :], sp[:, 3, :], sp[:, 7, :]
            step(V.tensor_scalar(z2, y_, 2.0, None, ALU.add))
            step(V.reciprocal(z2, z2))
            step(V.tensor_tensor(z_, y_, z2, ALU.mult))
            step(V.tensor_tensor(z2, z_, z_, ALU.mult))
            step(V.tensor_scalar(acc, z2, 1.0 / 17, 1.0 / 15, ALU.mult, ALU.add))
            for d in (13, 11, 9, 7, 5, 3, 1):
                step(V.tensor_tensor(acc, acc, z2, ALU.mult))
                step(V.tensor_scalar(acc, acc, 1.0 / d, None, ALU.add))
            step(V.tensor_tensor(acc, acc, z_, ALU.mult))
            step(V.tensor_scalar(z_, vc[:, LAM:LAM + NM], -1.0, 0.0, ALU.mult, ALU.max))
            step(V.scalar_tensor_tensor(out=acc, in0=acc, scalar=2.0, in1=z_, op0=ALU.mult, op1=ALU.add))
            step(V.tensor_scalar(sp[:, 4, :], acc, -LRU_C, None, ALU.mult))
            step(V.tensor_scalar(sp[:, 5, :], acc, -2.0 * LRU_C, None, ALU.mult))
            step(V.tensor_scalar(sp[:, 6, :], acc, LRU_C, None, ALU.mult))
            dve.wait_ge(lam_exp, 1)
            step(V.tensor_tensor(lams[:, 4:5], lams[:, 3:4], lams[:, 2:3], ALU.subtract))
            V.tensor_scalar(lams[:, 5:6], lams[:, 4:5], -LAMBDA_INIT, None, ALU.add).then_inc(sp_ready, 1)
            neg_lam = lams[:, 5:6]

            def conv(m):
                dve.wait_ge(lru_evac, 4 * m + 2)
                if m >= 2:
                    dve.wait_ge(gate_mm, 4 * m - 4)
                    dve.wait_ge(y_lru, m - 1)
                xp = xlp[:, m % 2, :]
                step(V.tensor_scalar(xc[:, m % 2, :], xp[:, 0:T], vc[:, CW + m:CW + m + 1],
                                     vc[:, CB + m:CB + m + 1], ALU.mult, ALU.add))
                for j in (1, 2, 3):
                    ins = V.scalar_tensor_tensor(out=xc[:, m % 2, :], in0=xp[:, j:j + T],
                                                 scalar=vc[:, CW + NM * j + m:CW + NM * j + m + 1],
                                                 in1=xc[:, m % 2, :], op0=ALU.mult, op1=ALU.add)
                    if j < 3:
                        step(ins)
                ins.then_inc(conv_done, 1)
                dve.wait_ge(conv_done, m + 1)

            for u in range(4 * NM + 1):
                if u >= 1:
                    unit_low(u + 2)
                if u == 4 * NM:
                    unit_low(u + 3)
                if u < 2 * NM and u % 2 == 0:
                    conv(u // 2)
                if u >= 2 * NM:
                    for j in (2 * u - 4 * NM, 2 * u - 4 * NM + 1):
                        j -= 1
                        if j < 0 or j >= 4 * NM:
                            continue
                        m, s, isk = j // 2 % NM, j % 2, j >= 2 * NM
                        dve.wait_ge(qk_rms, j + 1)
                        step(V.reciprocal(rt[:, j % 2, :], rt[:, j % 2, :]))
                        gain = vc[:, KG:KG + 1] if isk else qgh[:, m:m + 1]
                        V.scalar_tensor_tensor(out=(k if isk else q)[:, m, s * HALF:(s + 1) * HALF], in0=ps[:, (4 * NM + j) % 4, :],
                                               scalar=gain, in1=rt[:, j % 2, :], op0=ALU.mult, op1=ALU.mult).then_inc(qk_done, 1)
                if u % 2 == 0 and 2 <= u <= 2 * NM:
                    m = u // 2 - 1
                    dve.wait_ge(gate_sig, 4 * m + 4)
                    step(V.tensor_tensor(ig[:], ig[:], xc[:, m % 2, :], ALU.mult))
                    dve.wait_ge(lru_exp, 3 * m + 2)
                    V.scalar_tensor_tensor(out=th[:, m % 2, :], in0=a2[:, m % 2, :], scalar=1.0, in1=th[:, m % 2, :],
                                           op0=ALU.add, op1=ALU.mult).then_inc(om_ready, 1)
                    dve.wait_ge(om_sqrt, m + 1)
                    step(V.tensor_tensor(ig[:], ig[:], th[:, m % 2, :], ALU.mult))
                    dve.wait_ge(lru_exp, 3 * m + 3)
                    step(V.tensor_tensor_scan(xc[:, m % 2, :], r[:], ig[:], 0.0, ALU.mult, ALU.add))
                    dve.wait_ge(lru_evac, 4 * m + 4)
                    V.tensor_tensor(gg[:, m, :], gg[:, m, :], xc[:, m % 2, :], ALU.mult).then_inc(y_lru, 1)

            def lru_norm():
                dve.wait_ge(y_rms, 2)
                step(V.reciprocal(yr[:], yr[:]))
                dve.wait_ge(y_sq, NM)
                for m in range(NM):
                    V.scalar_tensor_tensor(out=gg[:, m, :], in0=gg[:, m, :], scalar=vc[:, LG + m:LG + m + 1],
                                           in1=yr[:], op0=ALU.mult, op1=ALU.mult).then_inc(lru_ready, 1)

            lru_norm()
            dve.wait_ge(nd_raw, 1)
            step(V.scalar_tensor_tensor(out=nd[:], in0=ndt[:], scalar=-1.0, in1=ndt[:], op0=ALU.mult, op1=ALU.min))
            step(V.memset(nd[0:CHUNK, T - CHUNK:T], NEG_BIG))
            def y_low(gr, b):
                dve.wait_ge(y_hi[gr], b + 1)
                V.tensor_tensor(yl[gr][:, b % 2, :, :], (gg, yatt)[gr][:, :, b * P:(b + 1) * P],
                                yh[gr][:, b % 2, :, :].bitcast(F32), ALU.subtract).then_inc(y_lo[gr], 1)

            for t in range(NI + 7):
                if t - 1 in Y_SPLIT_AT:
                    y_low(0, Y_SPLIT_AT.index(t - 1))
                if t < NI:
                    hh, i = item(t)
                    w = P * (i + 1)
                    for cc in range(2):
                        dve.wait_ge(s_done, 2 * t + cc + 1)
                        if t >= 3:
                            dve.wait_ge(t_done, tpos[("w", t - 3)] + 1)
                        src = ps[:, 2 * cc:2 * cc + 2, :].rearrange("p a n -> p (a n)")
                        V.tensor_tensor_reduce(out=pr[:, t % 3, cc, 0:w], in0=src[:, 0:w], in1=nd[:, T - w:T], scale=1.0,
                                               scalar=-3e38, op0=ALU.add, op1=ALU.max,
                                               accum_out=mx[:, t, cc:cc + 1]).then_inc(s_biased, 1)
                    dve.wait_ge(s_biased, 2 * t + 2)
                    V.tensor_scalar(nb[:, t, :], mx[:, t, :], -slope[hh], None, ALU.mult).then_inc(s_nmax, 1)
                u = t - 5
                if 0 <= u < NI:
                    dve.wait_ge(pv_done, u + 1)
                    hh, i = item(u)
                    if hh >= 2 and u % NB == 0:
                        dve.wait_ge(t_done, tpos[("y", hh - 2)] + 1)
                    V.tensor_scalar(osb[:, hh % 2, i, :], ps[:, 6 + u % 2, 0:P], ri[:, u, 0:1], None, ALU.mult).then_inc(o_evac, 1)
                    if u % NB == NB - 1:
                        dve.wait_ge(o_evac, u + 1)
                        step(V.tensor_tensor(osq[:], osb[:, hh % 2, :, :], osb[:, hh % 2, :, :], ALU.mult))
                        step(V.tensor_reduce(out=oss[:, hh % 2, :], in_=osq[:], axis=AX.X, op=ALU.add))
                        V.tensor_scalar(oss[:, hh % 2, :], oss[:, hh % 2, :], 1.0 / P, EPS, ALU.mult, ALU.add).then_inc(o_ms, 1)
                u = t - 1
                if 0 <= u < NI:
                    w = P * (item(u)[1] + 1)
                    dve.wait_ge(p_ready, 2 * u + 2)
                    step(V.reciprocal(ri[:, u, :], sm[:, u, :]))
                    step(V.tensor_scalar(ra[:, u:u + 1], ri[:, u, 1:2], neg_lam, sm[:, u, 0:1], ALU.mult, ALU.mult))
                    V.scalar_tensor_tensor(out=pr[:, u % 3, 1, 0:w], in0=pr[:, u % 3, 1, 0:w], scalar=ra[:, u:u + 1],
                                           in1=pr[:, u % 3, 0, 0:w], op0=ALU.mult, op1=ALU.add).then_inc(w_ready, 1)
                u = t - 6
                if 0 <= u < NI and u % NB == NB - 1:
                    hh = u // NB
                    dve.wait_ge(o_pow, hh + 1)
                    V.tensor_tensor(osb[:, hh % 2, :, :], osb[:, hh % 2, :, :],
                                    oss[:, hh % 2, :].unsqueeze(2).to_broadcast([P, NB, P]), ALU.mult).then_inc(o_normed, 1)
            y_low(1, 0)
            y_low(1, 1)
            for b in range(NB + 2):
                if b < NB:
                    dve.wait_ge(op_done, b + 1)
                    dve.wait_ge(xr_landed[b % 2], 16 * (b // 2 + 1))
                    if b >= 2:
                        dve.wait_ge(h_stored[b % 2], 16 * (b // 2))
                        dve.wait_ge(hn2_stored[b % 2], 16 * (b // 2))
                        dve.wait_ge(xt2_done, b - 1)
                    src = ps[:, 2 * (b % 2):2 * (b % 2) + 2, :].rearrange("p a n -> p (a n)")
                    V.tensor_tensor(h[:, b % 2, :], src, xr[:, b % 2, :], ALU.add).then_inc(h_ready, 1)
                    if b + 2 < NB:
                        y_low(0, b + 2)
                        y_low(1, b + 2)
                    dve.wait_ge(h_rms, b + 1)
                    if b == 0:
                        dve.wait_ge(wout_landed, 16 * 7)
                        dve.wait_ge(br_landed, 32)
                    step(V.reciprocal(rs[:, b:b + 1], ss[:, b:b + 1]))
                    V.scalar_tensor_tensor(out=hn2[:, b % 2, :], in0=h[:, b % 2, :], scalar=rs[:, b:b + 1],
                                           in1=g2b[:], op0=ALU.mult, op1=ALU.mult).then_inc(hn2_ready, 1)
                if b >= 2:
                    bb = b - 2
                    dve.wait_ge(r_done, bb + 1)
                    V.tensor_tensor(lg[:, bb, :], ps[:, 6 + bb % 2, 0:NR], br[:], ALU.add).then_inc(logits_ready, 1)
            dve.wait_ge(logits_ready, NB)
            dve.wait_ge(route_const, 1)

            assert NG == EPG

            def first_max(onehot, values, top):
                step(V.tensor_reduce(out=top, in_=values, axis=AX.X, op=ALU.max))
                step(V.tensor_tensor(onehot, values, top.unsqueeze(2).to_broadcast([P, NB, EPG]), ALU.is_equal))
                step(V.tensor_tensor(key[:], onehot, rank[:].unsqueeze(1).to_broadcast([P, NB, EPG]), ALU.mult))
                step(V.tensor_reduce(out=ktop[:], in_=key[:], axis=AX.X, op=ALU.max))
                step(V.tensor_tensor(onehot, key[:], ktop[:].unsqueeze(2).to_broadcast([P, NB, EPG]), ALU.is_equal))

            lgg = lg[:, :, 0:NG]
            per_group = [P, NB, NG, EPG]
            group_of = ohg[:].unsqueeze(3).to_broadcast(per_group)
            first_max(ohg[:], lgg, gtop[:])
            step(V.tensor_tensor(selp[:], lg[:, :, NG:NR].rearrange("p b (g e) -> p b g e", e=EPG), group_of, ALU.mult))
            step(V.tensor_reduce(out=sel[:], in_=selp[:].rearrange("p b g e -> p b e g"), axis=AX.X, op=ALU.add))
            first_max(oh1[:], sel[:], etop1[:])
            step(V.scalar_tensor_tensor(out=stmp[:], in0=oh1[:], scalar=-3e38, in1=sel[:], op0=ALU.mult, op1=ALU.add))
            first_max(oh2[:], stmp[:], etop2[:])
            for j, oh in enumerate((oh1, oh2)):
                step(V.tensor_tensor(mm[:, j, :, :].rearrange("p (g e) b -> p b g e", e=EPG),
                                     oh[:].unsqueeze(2).to_broadcast(per_group), group_of, ALU.mult))
            step(V.tensor_tensor(msum[:], mm[:, 0, :, :], mm[:, 1, :, :], ALU.add))
            V.tensor_tensor_scan(mincl[:].rearrange("p e b -> p (e b)"), restart[:].rearrange("p e b -> p (e b)"),
                                 msum[:].rearrange("p e b -> p (e b)"), 0.0, ALU.mult, ALU.add).then_inc(mask_ready, 1)
            step(V.tensor_tensor(gexp[:], lgg, gtop[:].unsqueeze(2).to_broadcast([P, NB, NG]), ALU.subtract))
            V.tensor_tensor(edif[:], etop2[:], etop1[:], ALU.subtract).then_inc(route_max, 1)
            dve.wait_ge(prefix_done, 2)
            step(V.tensor_tensor(tfull[:], ps[:, 1, 0:NE].unsqueeze(2).to_broadcast([P, NE, NB]),
                                 full[:].unsqueeze(1).to_broadcast([P, NE, NB]), ALU.is_gt))
            step(V.tensor_reduce(out=ntile[:], in_=tfull[:], axis=AX.X, op=ALU.add))
            step(V.tensor_tensor_scan(tincl[:], ones[:, 0:NE], ntile[:], 0.0, ALU.mult, ALU.add))
            step(V.tensor_tensor(texcl[:], tincl[:], ntile[:], ALU.subtract))
            step(V.scalar_tensor_tensor(out=slotm[:], in0=texcl[:].unsqueeze(2).to_broadcast([P, NE, NB]), scalar=float(P),
                                        in1=ps[:, 0, 0:NB * NE].rearrange("p (e b) -> p e b", b=NB), op0=ALU.mult, op1=ALU.add))
            step(V.tensor_tensor(stmp2[:], slotm[:].unsqueeze(1).to_broadcast([P, 2, NE, NB]), mm[:], ALU.mult))
            step(V.tensor_reduce(out=slot[:], in_=stmp2[:].rearrange("p j e b -> p j b e"), axis=AX.X, op=ALU.add))
            step(V.tensor_copy(slot_i[:], slot[:]))
            step(V.tensor_scalar(srow_i[:], slot_i[:], P - 1, None, ALU.bitwise_and))
            step(V.tensor_scalar(scol_i[:], slot_i[:], 7, None, ALU.logical_shift_right))
            step(V.tensor_copy(srow[:], srow_i[:]))
            step(V.tensor_copy(scol[:], scol_i[:]))
            each = [P, NB, 32]
            for j in range(2):
                step(V.tensor_tensor(leq[:, j, :, :], iota_row[:, 0:32].unsqueeze(1).to_broadcast(each),
                                     scol[:, j, :].unsqueeze(2).to_broadcast(each), ALU.is_equal))
                step(V.tensor_tensor(lfrm[:, j, :, :], leq[:, j, :, :], tok1[:].unsqueeze(2).to_broadcast(each), ALU.mult))
                V.tensor_tensor(lrow[:, j, :, :], iota_row[:].unsqueeze(1).to_broadcast([P, NB, P]),
                                srow[:, j, :].unsqueeze(2).to_broadcast([P, NB, P]), ALU.is_equal).then_inc(list_operands, 1)
            dve.wait_ge(route_exp, 1)
            step(V.tensor_reduce(out=gsum[:], in_=gexp[:], axis=AX.X, op=ALU.add))
            step(V.tensor_scalar(esum[:], edif[:], 1.0, None, ALU.add))
            step(V.tensor_tensor(gsum[:], gsum[:], esum[:], ALU.mult))
            step(V.reciprocal(gates[:, 0, :], gsum[:]))
            step(V.tensor_tensor(gates[:, 1, :], gates[:, 0, :], edif[:], ALU.mult))
            for j in range(2):
                V.tensor_tensor(lval[:, j, :, :], leq[:, j, :, :], gates[:, j, :].unsqueeze(2).to_broadcast(each),
                                ALU.mult).then_inc(list_operands, 1)
            dve.wait_ge(list_mm, 1)
            step(V.scalar_tensor_tensor(out=lemp[:], in0=ps[:, 2, 0:32], scalar=0.0, in1=pad1[:], op0=ALU.is_equal, op1=ALU.mult))
            V.scalar_tensor_tensor(out=ltok[:], in0=ps[:, 2, 0:32], scalar=-1.0, in1=lemp[:], op0=ALU.add,
                                   op1=ALU.add).then_inc(lists_ready, 1)
            step(V.tensor_tensor(tcmp[:], iota_row[:, 0:33].unsqueeze(2).to_broadcast([P, 33, NE]),
                                 tincl[:].unsqueeze(1).to_broadcast([P, 33, NE]), ALU.is_ge))
            step(V.tensor_reduce(out=texp[:], in_=tcmp[:], axis=AX.X, op=ALU.add))
            step(V.tensor_copy(texp_i[:], texp[:]))
            step(V.tensor_tensor(tchg[:, 0:32], texp[:, 1:33], texp[:, 0:32], ALU.is_gt))
            step(V.tensor_copy(tfirst_i[:, 1:32], tchg[:, 0:31]))
            step(V.memset(tchg[:, 32:33], 0.0))
            step(V.tensor_copy(tfirst_i[:, 0:1], tchg[:, 32:33]))
            step(V.scalar_tensor_tensor(out=tchg[:, 0:32], in0=texp[:, 0:32], scalar=float(NE - 1), in1=tchg[:, 0:32],
                                        op0=ALU.is_lt, op1=ALU.mult))
            step(V.tensor_copy(tlast_i[:], tchg[:, 0:32]))
            step(V.tensor_copy(tiles_i[:, 0:1], tincl[:, NE - 1:NE]))
            dve.wait_ge(list_mm, 2)
            step(V.tensor_copy(lgate[:], ps[:, 3, 0:32]))
            V.tensor_scalar(tiles_i[:, 1:2], tincl[:, NE - 1:NE], -1.0, None, ALU.add).then_inc(lists_ready, 1)
            dve.wait_ge(lists_ready, 2)
            def low(j, c, count):
                dve.wait_ge(hi_ready[j], count)
                V.tensor_tensor(wlo[NC * j + c][:].rearrange("p k n -> p (k n)"), raw[:, j, c, :],
                                whi[NC * j + c][:].rearrange("p k n -> p (k n)").bitcast(F32),
                                ALU.subtract).then_inc(lo_ready[j], 1)

            def x_low(count):
                dve.wait_ge(mxt_evac, count)
                V.tensor_tensor(xTl[:, :, :].rearrange("p k n -> p (k n)"), xT_ps,
                                xTh[:, :, :].rearrange("p k n -> p (k n)").bitcast(F32), ALU.subtract).then_inc(mxT_lo, 1)

            def h_low(g):
                dve.wait_ge(ht_evac, g)
                V.tensor_tensor(hTl[:, :, :].rearrange("p k n -> p (k n)"), ps[:, 6, :],
                                hTh[:, :, :].rearrange("p k n -> p (k n)").bitcast(F32), ALU.subtract).then_inc(hT_lo, 1)

            def hidden(g):
                dve.wait_ge(sil_ready, g + 1)
                dve.wait_ge(part_used[1], g * NC + NC)
                V.tensor_tensor(hid[:], ps[:, 1, :], sil[:], ALU.mult).then_inc(hid_ready, 1)

            def gated(g):
                V.tensor_copy(gcol[:, 0:1], lgate[:, bass.ds(g - 1, 1)]).then_inc(gcol_ready, 1)
                dve.wait_ge(gcol_ready, g)
                dve.wait_ge(part_used[2], g * NC)
                dve.wait_ge(scattered, g * 16)
                V.tensor_scalar(ysb[:], y_ps, gcol[:, 0:1], None, ALU.mult).then_inc(y_ready, 1)

            for j in range(3):
                for c in range(NC):
                    low(j, c, c + 1)
                    if (j, c) == (0, 2):
                        x_low(1)
                if j == 0:
                    dve.wait_ge(pad_stored, 16)
            hidden(0)
            x_low(2)
            nt = dve.value_load(tiles_i[0:1, 0:1], min_val=NE, max_val=MAX_TILES)
            with dve.Fori(1, nt) as g:
                e = dve.value_load(texp_i[0:1, bass.ds(g, 1)], min_val=0, max_val=NE - 1)
                last = dve.value_load(tlast_i[0:1, bass.ds(g, 1)], min_val=0, max_val=1)
                first = dve.value_load(tfirst_i[0:1, bass.ds(g, 1)], min_val=0, max_val=1)
                with dve.If(last != 0):
                    for c in range(NC - 1):
                        low(0, c, e * NC + (c + 1 + NC))
                    h_low(g)
                    low(0, NC - 1, e * NC + 2 * NC)
                    low(1, 0, e * NC + (1 + NC))
                    hidden(g)
                    x_low(g + 2)
                    for c in range(1, NC):
                        low(1, c, e * NC + (c + 1 + NC))
                with dve.Else():
                    h_low(g)
                    hidden(g)
                    x_low(g + 2)
                with dve.If(first != 0):
                    for c in range(NC):
                        low(2, c, e * NC + (c + 1))
                gated(g)
                dve.wait_ge(y_ready, g)
            h_low(nt)
            gated(nt)

        @block.tensor
        def _(pe):
            mm_, tr = nc.tensor.matmul, nc.tensor.transpose

            pe.wait_ge(consts_built, 1)
            def x_transposed(b):
                pe.wait_ge(hn_ready, b + 1)
                if b >= 4:
                    pe.wait_ge(hnT_act, b - 1)
                    pe.wait_ge(hnT_dve, b - 1)
                for kk in range(KD):
                    last = tr(ps[:, x_bank(b) + kk // 4, kk % 4 * P:(kk % 4 + 1) * P],
                              xs(b)[:, kk * P:(kk + 1) * P], ident[:])
                last.then_inc(hn_transposed, 1)

            def projection(u, s, kks=range(KD)):
                for kk in kks:
                    for w, hx in ((wih, hnTh), (wih, hnTl), (wil, hnTh)):
                        last = mm_(ps[:, (2 * u + s) % 4, :], w[:, u % RING, kk, :], hx[:, kk, s * HALF:(s + 1) * HALF],
                                   start=(kk == 0 and w is wih and hx is hnTh), stop=(kk == KD - 1 and w is wil))
                return last

            for b in range(NB - 2):
                x_transposed(b)
            pe.wait_ge(hnT_act, NB // 2)
            pe.wait_ge(hnT_dve, NB // 2)
            pe.wait_ge(w_low, 1)
            projection(0, 0, range(KD // 2))
            x_transposed(NB - 2)
            projection(0, 0, range(KD // 2, KD)).then_inc(group_done, 1)
            x_transposed(NB - 1)
            pe.wait_ge(w_low, 2)
            projection(1, 0).then_inc(group_done, 1)
            pe.wait_ge(hnT_act, NB)
            pe.wait_ge(hnT_dve, NB)
            pe.wait_ge(vec_landed, 16 * 11)
            tr(ps[:, 7, 0:NV], vrow[0:NV, :], ident[0:NV, 0:NV]).then_inc(vec_transposed, 1)
            projection(0, 1).then_inc(group_done, 1)
            projection(1, 1).then_inc(group_done, 1)

            def bank_free(g):
                if g < 4 * NM:
                    pe.wait_ge(lru_evac, g + 1)
                elif g < 8 * NM:
                    pe.wait_ge(qk_done, g - 4 * NM + 1)
                else:
                    pe.wait_ge(v_evac, g - 8 * NM + 1)

            def qk_norm(j):
                pe.wait_ge(qk_sq, j + 1)
                if j >= 2:
                    pe.wait_ge(qk_rms, j - 1)
                mm_(ps[:, 4 + j % 2, :], ones_blk[:], sq[:, j % 2, :], start=True, stop=True).then_inc(qk_mm, 1)

            def gates(m):
                pe.wait_ge(bd_landed, 64)
                pe.wait_ge(conv_done, m + 1)
                for j in range(4 * m, 4 * m + 4):
                    gi, s = j // 2 % 2, j % 2
                    if j >= 2:
                        pe.wait_ge(gate_sig, j - 1)
                    mm_(ps[:, 6 + j % 2, :], bd[:, gi, m, :], xc[:, m % 2, s * HALF:(s + 1) * HALF],
                        start=True, stop=True).then_inc(gate_mm, 1)

            def y_norm(m):
                pe.wait_ge(gate_sig, 4 * NM)
                pe.wait_ge(y_sq, m + 1)
                for s in range(2):
                    mm_(ps[:, 6 + s, :], ones[:], th[:, m % 2, s * HALF:(s + 1) * HALF],
                        start=(m == 0), stop=(m == NM - 1)).then_inc(y_norm_mm, 1)

            for u in range(2, 4 * NM):
                pe.wait_ge(w_low, u + 1)
                for s in range(2):
                    g = 2 * u + s
                    bank_free(g - 4)
                    projection(u, s).then_inc(group_done, 1)
                    if g >= 4 * NM + 1:
                        qk_norm(g - 4 * NM - 1)
                if u % 2 == 0 and 2 <= u <= 2 * NM:
                    gates(u // 2 - 1)
                if u == 2 * NM + 5:
                    y_norm(0)
                    y_norm(1)
            qk_norm(4 * NM - 1)
            y_norm(2)
            y_norm(3)
            pe.wait_ge(w_low, 5 * NM)
            for b in range(NB):
                g = 8 * NM + b
                bank_free(g - 4)
                for kk in range(KD):
                    for hx, w in ((hnTh, wih), (hnTh, wil), (hnTl, wih)):
                        last = mm_(ps[:, g % 4, :].rearrange("p (u n) -> p u n", n=P), hx[:, kk, b * P:(b + 1) * P],
                                   w[:, 0:NM, kk, :], start=(kk == 0 and hx is hnTh and w is wih),
                                   stop=(kk == KD - 1 and hx is hnTl))
                last.then_inc(group_done, 1)
            pe.wait_ge(v_evac, NB)
            pe.wait_ge(qk_done, 4 * NM)
            pe.wait_ge(y_rms, 2)
            def projected(b, group, halves=(0, 1)):
                pe.wait_ge(y_lo[group], b + 1)
                for s in halves:
                    for kk in range(group * NM, group * NM + NM):
                        for y, w in ((yh, woh), (yh, wol), (yl, woh)):
                            last = mm_(ps[:, 2 * (b % 2) + s, :], y[group][:, b % 2, kk % NM, :],
                                       w[kk][:, s * HALF:(s + 1) * HALF],
                                       start=(kk == 0 and y is yh and w is woh), stop=(kk == KD - 1 and y is yl))
                return last

            def transposed(kind, tt):
                ti = tpos[(kind, tt)]
                if ti >= 1:
                    pe.wait_ge(t_evac, ti)
                if kind == "w":
                    pe.wait_ge(w_ready, tt + 1)
                else:
                    pe.wait_ge(o_normed, tt + 1)
                cols = item(tt)[1] + 1 if kind == "w" else NB
                for j in range(cols):
                    src = pr[:, tt % 3, 1, j * P:(j + 1) * P] if kind == "w" else osb[:, tt % 2, j, :]
                    last = tr(ps[:, 4 + j // 4, j % 4 * P:(j % 4 + 1) * P], src, ident[:])
                last.then_inc(t_done, 1)

            for t in range(NI + 4):
                if t < NI:
                    hh, i = item(t)
                    w = P * (i + 1)
                    pe.wait_ge(qz_ready, 2 * hh + 2)
                    for cc in range(2):
                        if t >= 1:
                            pe.wait_ge(s_biased, 2 * (t - 1) + cc + 1)
                        for s in range(0, w, HALF):
                            last = mm_(ps[:, 2 * cc + s // HALF, 0:min(HALF, w - s)], qz[:, hh % 2, cc, i * P:(i + 1) * P],
                                       k[:, hh, s:min(w, s + HALF)], start=True, stop=True)
                        last.then_inc(s_done, 1)
                if t in Y_STEPS:
                    transposed("y", Y_STEPS.index(t))
                u = t - 4
                if 0 <= u < NI:
                    hh, i = item(u)
                    pe.wait_ge(t_evac, tpos[("w", u)] + 1)
                    if u >= 2:
                        pe.wait_ge(o_evac, u - 1)
                    for j in range(i + 1):
                        last = mm_(ps[:, 6 + u % 2, 0:P], wT[:, u % 2, j * P:(j + 1) * P], v[:, j, hh * P:(hh + 1) * P],
                                   start=(j == 0), stop=(j == i))
                    last.then_inc(pv_done, 1)
                if t == NI + 3:
                    pe.wait_ge(lru_ready, NM)
                    pe.wait_ge(wout_lo, NM)
                    pe.wait_ge(s_biased, 2 * NI)
                    projected(0, 0)
                if 0 <= t - 2 < NI:
                    transposed("w", t - 2)
                if t == NI + 3:
                    transposed("y", NM - 1)
            projected(1, 0)
            pe.wait_ge(t_evac, len(tslots))
            pe.wait_ge(o_evac, NI)

            pe.wait_ge(wout_landed, 16 * 7)

            def logits(b):
                pe.wait_ge(xt2_evac, b + 1)
                if b >= 2:
                    pe.wait_ge(logits_ready, b - 1)
                for kk in range(KD):
                    last = mm_(ps[:, 6 + b % 2, 0:NR], hn2T[:, b % 2, kk, :], wr[:, kk, :],
                               start=(kk == 0), stop=(kk == KD - 1))
                last.then_inc(r_done, 1)

            def second_norm_transposed(b):
                pe.wait_ge(hn2_ready, b + 1)
                if b >= 1:
                    pe.wait_ge(xt2_evac, b)
                for kk in range(KD):
                    last = tr(ps[:, 4 + kk // 4, kk % 4 * P:(kk % 4 + 1) * P], hn2[:, b % 2, kk * P:(kk + 1) * P], ident[:])
                last.then_inc(xt2_done, 1)

            pe.wait_ge(wout_lo, KD)
            projected(0, 1).then_inc(op_done, 1)
            projected(1, 1).then_inc(op_done, 1)
            for b in range(2, NB):
                pe.wait_ge(h_ready, b - 1)
                projected(b, 0)
                if b == 2:
                    second_norm_transposed(0)
                projected(b, 1, (0,))
                if b == 2:
                    logits(0)
                second_norm_transposed(b - 1)
                projected(b, 1, (1,)).then_inc(op_done, 1)
                logits(b - 1)
            second_norm_transposed(NB - 1)
            logits(NB - 1)
            pe.wait_ge(mask_ready, 1)
            pe.wait_ge(h_ready, NB)
            mm_(ps[:, 0, 0:NB * NE], below[:], msum[:].rearrange("p e b -> p (e b)"), start=True, stop=False)
            mm_(ps[:, 0, 0:NB * NE], ones[:], mincl[:].rearrange("p e b -> p (e b)"), start=False, stop=True).then_inc(prefix_done, 1)
            mm_(ps[:, 1, 0:NE], ones[:], mincl[:, :, NB - 1], start=True, stop=True).then_inc(prefix_done, 1)
            for n, (value, bank) in enumerate(((lfrm, 2), (lval, 3))):
                for j in range(2):
                    pe.wait_ge(list_operands, 2 * n + j + 1)
                    for b in range(NB):
                        row = lrow[:, j, b, :] if value is lfrm else lrow[:, j, b, :].bitcast(F32)
                        last = mm_(ps[:, bank, 0:32], row, value[:, j, b, :],
                                   start=(j == 0 and b == 0), stop=(j == 1 and b == NB - 1))
                last.then_inc(list_mm, 1)
            pe.wait_ge(lists_ready, 2)
            nt = pe.value_load(tiles_i[0:1, 0:1], min_val=NE, max_val=MAX_TILES)

            def rows_transposed():
                for kk in range(KD):
                    last = tr(ps[:, 2 + kk // 4, kk % 4 * P:(kk % 4 + 1) * P], xg[:, kk * P:(kk + 1) * P], ident[:])
                last.then_inc(mxt_done, 1)

            pe.wait_ge(gathered, 16)
            rows_transposed()
            def product(j, banks, lhs, count):
                per = (KD, KD, KE)[j] // NC
                for c in range(NC):
                    pe.wait_ge(lo_ready[j], count + c)
                    for kk in range(per):
                        n = c * per + kk
                        for a, w in ((0, whi), (0, wlo), (1, whi)):
                            for s, bank in enumerate(banks):
                                part = w[NC * j + c]
                                rhs = part[:, kk, :] if j < 2 else part[:, s, :]
                                last = mm_(ps[:, bank, :], lhs[a][:, n, :], rhs,
                                           start=(n == 0 and a == 0 and w is whi),
                                           stop=(n == (KD, KD, KE)[j] - 1 and a == 1))
                    last.then_inc(part_used[j], 1)

            def hidden_transposed():
                for f in range(KE):
                    last = tr(ps[:, 6, f * P:(f + 1) * P], hid[:, f * P:(f + 1) * P], ident[:])
                last.then_inc(ht_done, 1)

            pe.wait_ge(mxT_lo, 1)
            product(0, (0,), (xTh, xTl), 1)
            product(1, (1,), (xTh, xTl), 1)
            pe.wait_ge(gathered, 32)
            rows_transposed()
            with pe.Fori(1, nt) as g:
                e = pe.value_load(texp_i[0:1, bass.ds(g, 1)], min_val=0, max_val=NE - 1)
                e_before = pe.value_load(texp_i[0:1, bass.ds(g - 1, 1)], min_val=0, max_val=NE - 1)
                pe.wait_ge(mxT_lo, g + 1)
                pe.wait_ge(hid_ready, g)
                product(0, (0,), (xTh, xTl), e * NC + 1)
                hidden_transposed()
                product(1, (1,), (xTh, xTl), e * NC + 1)
                pe.wait_ge(gathered, g * 16 + 32)
                rows_transposed()
                pe.wait_ge(hT_lo, g)
                product(2, (4, 5), (hTh, hTl), e_before * NC + 1)
            pe.wait_ge(hid_ready, nt)
            hidden_transposed()
            pe.wait_ge(hT_lo, nt)
            product(2, (4, 5), (hTh, hTl), NE * NC - NC + 1)


_NAMES = ['x', 'norm1_g', 'w_in', 'conv_w', 'conv_b', 'w_gate_a', 'b_gate_a', 'w_gate_x', 'b_gate_x',
          'lru_lambda', 'lru_out_g', 'q_norm_g', 'k_norm_g', 'lambda_q1', 'lambda_k1', 'lambda_q2', 'lambda_k2',
          'sub_norm_g', 'w_out', 'norm2_g', 'w_router_group', 'b_router_group', 'w_router_expert',
          'b_router_expert', 'w_expert_gate', 'w_expert_up', 'w_expert_down']


def kernel(**inputs):
    import numpy as _np
    import concourse.bacc as _bacc
    from concourse import mybir as _mybir
    from concourse.bass_utils import run_bass_kernel_spmd as _run

    nc = _bacc.Bacc("TRN2", target_bir_lowering=False, num_devices=1)
    arrays, args = {}, []
    for name in _NAMES:
        a = _np.ascontiguousarray(inputs[name])
        arrays[f"in_{name}"] = a
        args.append(nc.dram_tensor(f"in_{name}", a.shape, _mybir.dt.from_np(a.dtype), kind="ExternalInput").ap())
    _, T, D = inputs['x'].shape
    out = nc.dram_tensor("out_rows", (T + 128, D), _mybir.dt.float32, kind="ExternalOutput").ap()
    hn2 = nc.dram_tensor("hn2_rows", (T + 128, D), _mybir.dt.float32, kind="Internal").ap()
    build_block(nc, *args, out, hn2)
    res = _run(nc, [arrays], core_ids=[0])
    return res.results[0]["out_rows"][:T].reshape(1, T, D)
```
